# Optimizing a Trainium2 kernel written in Bass

```python
import math
import jax, jax.numpy as jnp
from jax import lax
import numpy as np

D_MODEL = 1024
BATCH = 1
SEQ = 256
DEPTH = 1

CHUNK = 64
D_RNN = 1280
H_RNN = 16
RNN_BLOCK = D_RNN // H_RNN
CONV_A = 4
LRU_C = 8.0
H_ATT = 16
HEAD_DIM = 64
D_ATT = H_ATT * HEAD_DIM
Q_BLOCK = 128
D_FF = 3 * D_MODEL
CONV_F = 3
N_BRANCH = 2
D_IN = 2 * D_RNN + 3 * D_ATT + H_ATT + N_BRANCH * D_MODEL
RMS_EPS = 1e-6


def rms_norm(x, gain):
    xf = x.astype(jnp.float32)
    y = xf * lax.rsqrt(jnp.mean(xf * xf, axis=-1, keepdims=True) + RMS_EPS)
    return (y * gain.astype(jnp.float32)).astype(x.dtype)

def causal_dwconv(x, w, b):
    k_w, c = w.shape
    y = lax.conv_general_dilated(
        x, w[:, None, :].astype(x.dtype), window_strides=(1,), padding=[(k_w - 1, 0)],
        dimension_numbers=("NWC", "WIO", "NWC"), feature_group_count=c)
    return y + b.astype(x.dtype)

def rg_lru(xc, w_a, b_a, w_x, b_x, lam):
    bsz, s, _ = xc.shape
    xb = xc.reshape(bsz, s, H_RNN, RNN_BLOCK)
    r = jax.nn.sigmoid(jnp.einsum("bshi,hij->bshj", xb, w_a).reshape(bsz, s, D_RNN) + b_a)
    i = jax.nn.sigmoid(jnp.einsum("bshi,hij->bshj", xb, w_x).reshape(bsz, s, D_RNN) + b_x)
    log_a = -LRU_C * r.astype(jnp.float32) * jax.nn.softplus(-lam.astype(jnp.float32))
    a = jnp.exp(log_a)
    b_term = jnp.sqrt(-jnp.expm1(2.0 * log_a)) * (i * xc).astype(jnp.float32)

    def combine(left, right):
        a1, h1 = left
        a2, h2 = right
        return a1 * a2, a2 * h1 + h2

    _, h = lax.associative_scan(combine, (a, b_term), axis=1)
    return h.astype(xc.dtype)

def forgetting_attention(q, k, v, f_logit):
    bsz, s, _ = q.shape
    q = q.reshape(bsz, s, H_ATT, HEAD_DIM).transpose(0, 2, 1, 3)
    k = k.reshape(bsz, s, H_ATT, HEAD_DIM).transpose(0, 2, 1, 3)
    v = v.reshape(bsz, s, H_ATT, HEAD_DIM).transpose(0, 2, 1, 3)
    cum = jnp.cumsum(jax.nn.log_sigmoid(f_logit.astype(jnp.float32)), axis=1).transpose(0, 2, 1)
    scale = 1.0 / math.sqrt(HEAD_DIM)
    outs = []
    for blk in range(s // Q_BLOCK):
        qs, qe = blk * Q_BLOCK, (blk + 1) * Q_BLOCK
        sc = jnp.einsum("bhqd,bhkd->bhqk", q[:, :, qs:qe], k[:, :, :qe]).astype(jnp.float32) * scale
        sc = sc + cum[:, :, qs:qe, None] - cum[:, :, None, :qe]
        allowed = jnp.arange(qe)[None, :] <= jnp.arange(qs, qe)[:, None]
        sc = jnp.where(allowed, sc, -jnp.inf)
        p = jax.nn.softmax(sc, axis=-1).astype(v.dtype)
        outs.append(jnp.einsum("bhqk,bhkd->bhqd", p, v[:, :, :qe]))
    o = jnp.concatenate(outs, axis=2)
    return o.transpose(0, 2, 1, 3).reshape(bsz, s, D_ATT)

def first_inputs(seed: int = 0) -> dict:
    key = jax.random.key(seed)
    ks = jax.random.split(key, 24)
    f32 = jnp.float32
    nrm = lambda k, shape, fan_in: jax.random.normal(k, shape, f32) * (fan_in ** -0.5)
    gain = lambda k: 1.0 + 0.05 * jax.random.normal(k, (DEPTH, D_MODEL), f32)
    small = lambda k, shape: 0.01 * jax.random.normal(k, shape, f32)
    u = jax.random.uniform(ks[9], (DEPTH, D_RNN), f32, 0.9, 0.999)
    a0 = u ** (1.0 / LRU_C)
    lru_lambda = jnp.log(a0) - jnp.log1p(-a0)
    return {
        "x": jax.random.normal(ks[0], (BATCH, SEQ, D_MODEL), f32),
        "mix_norm_pre": gain(ks[1]),
        "mix_norm_post": gain(ks[2]),
        "w_in": nrm(ks[3], (DEPTH, D_MODEL, D_IN), D_MODEL),
        "conv_a_w": nrm(ks[4], (DEPTH, CONV_A, D_RNN), CONV_A),
        "conv_a_b": small(ks[5], (DEPTH, D_RNN)),
        "w_rg_a": nrm(ks[6], (DEPTH, H_RNN, RNN_BLOCK, RNN_BLOCK), RNN_BLOCK),
        "b_rg_a": small(ks[7], (DEPTH, D_RNN)),
        "w_rg_x": nrm(ks[8], (DEPTH, H_RNN, RNN_BLOCK, RNN_BLOCK), RNN_BLOCK),
        "b_rg_x": small(ks[10], (DEPTH, D_RNN)),
        "lru_lambda": lru_lambda,
        "b_forget": jax.random.uniform(ks[11], (DEPTH, H_ATT), f32, 1.0, 4.0),
        "b_merge": small(ks[12], (DEPTH, N_BRANCH, D_MODEL)),
        "w_proj_a": nrm(ks[13], (DEPTH, D_RNN, D_MODEL), D_RNN),
        "w_proj_b": nrm(ks[14], (DEPTH, D_ATT, D_MODEL), D_ATT),
        "w_out": nrm(ks[15], (DEPTH, D_MODEL, D_MODEL), D_MODEL),
        "ffn_norm_pre": gain(ks[16]),
        "ffn_norm_post": gain(ks[17]),
        "w_up": nrm(ks[18], (DEPTH, D_MODEL, 2 * D_FF), D_MODEL),
        "conv_f_w": nrm(ks[19], (DEPTH, CONV_F, 2 * D_FF), CONV_F),
        "conv_f_b": small(ks[20], (DEPTH, 2 * D_FF)),
        "w_down": nrm(ks[21], (DEPTH, D_FF, D_MODEL), D_FF),
    }

def first_block(x, mix_norm_pre, mix_norm_post, w_in, conv_a_w, conv_a_b, w_rg_a, b_rg_a,
              w_rg_x, b_rg_x, lru_lambda, b_forget, b_merge, w_proj_a, w_proj_b, w_out,
              ffn_norm_pre, ffn_norm_post, w_up, conv_f_w, conv_f_b, w_down):
    offs = np.cumsum([D_RNN, D_RNN, D_ATT, D_ATT, D_ATT, H_ATT, D_MODEL]).tolist()
    for layer in range(DEPTH):
        h = rms_norm(x, mix_norm_pre[layer])
        proj = jnp.einsum("bsd,de->bse", h, w_in[layer])
        xa, ga, q, k, v, f_logit, g_a, g_b = jnp.split(proj, offs, axis=-1)
        xc = causal_dwconv(xa, conv_a_w[layer], conv_a_b[layer])
        hr = rg_lru(xc, w_rg_a[layer], b_rg_a[layer], w_rg_x[layer], b_rg_x[layer], lru_lambda[layer])
        y_a = jax.nn.gelu(ga) * hr
        y_b = forgetting_attention(q, k, v, f_logit + b_forget[layer])
        merged = (jax.nn.sigmoid(g_a + b_merge[layer, 0]) * jnp.einsum("bse,ed->bsd", y_a, w_proj_a[layer])
                  + jax.nn.sigmoid(g_b + b_merge[layer, 1]) * jnp.einsum("bse,ed->bsd", y_b, w_proj_b[layer]))
        mix_out = jnp.einsum("bsd,de->bse", merged, w_out[layer])
        x = x + rms_norm(mix_out, mix_norm_post[layer])
        h = rms_norm(x, ffn_norm_pre[layer])
        up = jnp.einsum("bsd,df->bsf", h, w_up[layer])
        up = causal_dwconv(up, conv_f_w[layer], conv_f_b[layer])
        gate, val = jnp.split(up, 2, axis=-1)
        ffn_out = jnp.einsum("bsf,fd->bsd", jax.nn.gelu(gate) * val, w_down[layer])
        x = x + rms_norm(ffn_out, ffn_norm_post[layer])
    return x


DEPTH_2 = 2

N_MIXERS = 2
N_A_LAYERS = (DEPTH_2 + 1) // 2
N_B_LAYERS = DEPTH_2 // 2

HGRN_EXPAND = 128
HGRN_HEADS = D_MODEL // HGRN_EXPAND
HGRN_FDIM = HGRN_HEADS * HGRN_EXPAND
HGRN_IDIM = D_MODEL // HGRN_HEADS
HGRN_CHUNK = 64

ATTN_HEADS = 8
ATTN_HEAD_DIM = D_MODEL // ATTN_HEADS
MOBA_BLOCK = 256
MOBA_TOPK = 3
MOBA_QCHUNK = 32

REL_BUCKETS = 32
REL_MAX_DISTANCE = 1024

D_FF_2 = -(-(8 * D_MODEL) // (3 * 256)) * 256


def rms_norm_2(x, g):
    xf = x.astype(jnp.float32)
    y = xf * lax.rsqrt(jnp.mean(xf * xf, axis=-1, keepdims=True) + RMS_EPS)
    return (y * g.astype(jnp.float32)).astype(x.dtype)

def t5_bucket(dist):
    n = jnp.maximum(dist, 0)
    max_exact = REL_BUCKETS // 2
    nf = jnp.maximum(n, max_exact).astype(jnp.float32)
    large = max_exact + (jnp.log(nf / max_exact) / math.log(REL_MAX_DISTANCE / max_exact)
                         * (REL_BUCKETS - max_exact)).astype(jnp.int32)
    large = jnp.minimum(large, REL_BUCKETS - 1)
    return jnp.where(n < max_exact, n, large)

def hgrn2_mixer(h, w_in, w_out, lb, out_norm):
    b_, s_, _ = h.shape
    f32 = jnp.float32
    proj = h @ w_in
    q, fz, inp, og = jnp.split(proj, [HGRN_FDIM, 2 * HGRN_FDIM, 2 * HGRN_FDIM + D_MODEL], axis=-1)
    q = jax.nn.silu(q.astype(f32))
    lbf = lb.astype(f32)
    f = lbf + (1.0 - lbf) * jax.nn.sigmoid(fz.astype(f32))
    k = 1.0 - f
    logf = jnp.log(f)
    nc = s_ // HGRN_CHUNK

    def to_chunks(t, d):
        return t.reshape(b_, nc, HGRN_CHUNK, HGRN_HEADS, d).transpose(1, 0, 3, 2, 4)

    qc = to_chunks(q, HGRN_EXPAND)
    kc = to_chunks(k, HGRN_EXPAND)
    gc = to_chunks(logf, HGRN_EXPAND)
    ic = to_chunks(inp.astype(f32), HGRN_IDIM)
    causal = jnp.tril(jnp.ones((HGRN_CHUNK, HGRN_CHUNK), dtype=bool))

    def step(state, xs):
        qb, kb, gb, ib = xs
        cum = jnp.cumsum(gb, axis=2)
        diff = cum[:, :, :, None, :] - cum[:, :, None, :, :]
        decay = jnp.exp(jnp.where(causal[:, :, None], diff, -jnp.inf))
        scores = jnp.einsum('bhtn,bhsn,bhtsn->bhts', qb, kb, decay)
        o = (jnp.einsum('bhts,bhsd->bhtd', scores, ib)
             + jnp.einsum('bhtn,bhnd->bhtd', qb * jnp.exp(cum), state))
        last = cum[:, :, -1:, :]
        state = (state * jnp.exp(last[:, :, 0, :, None])
                 + jnp.einsum('bhsn,bhsd->bhnd', kb * jnp.exp(last - cum), ib))
        return state, o

    s0 = jnp.zeros((b_, HGRN_HEADS, HGRN_EXPAND, HGRN_IDIM), f32)
    _, o = lax.scan(step, s0, (qc, kc, gc, ic))
    o = o.transpose(1, 0, 3, 2, 4).reshape(b_, s_, D_MODEL)
    o = rms_norm_2(o, out_norm) * jax.nn.sigmoid(og.astype(f32))
    return (o.astype(h.dtype) @ w_out).astype(h.dtype)

def moba_mixer(h, w_in, w_out, rel_table):
    b_, s_, _ = h.shape
    f32 = jnp.float32
    nh, dh = ATTN_HEADS, ATTN_HEAD_DIM
    q, k, v = jnp.split(h @ w_in, 3, axis=-1)
    heads = lambda t: t.reshape(b_, s_, nh, dh).transpose(0, 2, 1, 3)
    q, k, v = heads(q), heads(k), heads(v)
    nb = -(-s_ // MOBA_BLOCK)
    pad = nb * MOBA_BLOCK - s_
    kp = jnp.pad(k, ((0, 0), (0, 0), (0, pad), (0, 0)))
    vp = jnp.pad(v, ((0, 0), (0, 0), (0, pad), (0, 0)))
    kb = kp.reshape(b_, nh, nb, MOBA_BLOCK, dh)
    vb = vp.reshape(b_, nh, nb, MOBA_BLOCK, dh)
    kmean = jnp.mean(kb.astype(f32), axis=3)
    scale = dh ** -0.5
    nqc = s_ // MOBA_QCHUNK
    qch = q.reshape(b_, nh, nqc, MOBA_QCHUNK, dh).transpose(2, 0, 1, 3, 4)
    bi = jnp.arange(b_)[:, None, None, None]
    hi = jnp.arange(nh)[None, :, None, None]
    table_t = rel_table.T
    topk = min(MOBA_TOPK, nb)
    kk = topk * MOBA_BLOCK

    def chunk(args):
        c, qb = args
        q0 = c * MOBA_QCHUNK
        qpos = q0 + jnp.arange(MOBA_QCHUNK)
        j = q0 // MOBA_BLOCK
        gate = jnp.einsum('bhqd,bhnd->bhqn', qb.astype(f32), kmean)
        gate = jnp.where(jnp.arange(nb) < j, gate, -jnp.inf)
        _, sel = lax.top_k(gate, topk)
        sel_ok = jnp.arange(topk) < j
        ks = kb[bi, hi, sel]
        vs = vb[bi, hi, sel]
        s_sel = jnp.einsum('bhqd,bhqkpd->bhqkp', qb, ks).astype(f32) * scale
        kpos_sel = sel[..., None] * MOBA_BLOCK + jnp.arange(MOBA_BLOCK)
        bias_sel = table_t[hi[..., None], t5_bucket(qpos[:, None, None] - kpos_sel)]
        s_sel = jnp.where(sel_ok[:, None], s_sel + bias_sel.astype(f32), -jnp.inf)
        kown = lax.dynamic_slice_in_dim(kp, j * MOBA_BLOCK, MOBA_BLOCK, axis=2)
        vown = lax.dynamic_slice_in_dim(vp, j * MOBA_BLOCK, MOBA_BLOCK, axis=2)
        dist_own = qpos[:, None] - (j * MOBA_BLOCK + jnp.arange(MOBA_BLOCK))[None, :]
        bias_own = rel_table[t5_bucket(dist_own)].transpose(2, 0, 1).astype(f32)
        s_own = jnp.einsum('bhqd,bhpd->bhqp', qb, kown).astype(f32) * scale + bias_own
        s_own = jnp.where(dist_own >= 0, s_own, -jnp.inf)
        logits = jnp.concatenate([s_sel.reshape(b_, nh, MOBA_QCHUNK, kk), s_own], axis=-1)
        p = jax.nn.softmax(logits, axis=-1).astype(vb.dtype)
        p_sel = p[..., :kk].reshape(b_, nh, MOBA_QCHUNK, topk, MOBA_BLOCK)
        p_own = p[..., kk:]
        return (jnp.einsum('bhqkp,bhqkpd->bhqd', p_sel, vs)
                + jnp.einsum('bhqp,bhpd->bhqd', p_own, vown))

    o = lax.map(chunk, (jnp.arange(nqc), qch))
    o = o.transpose(1, 0, 3, 2, 4).reshape(b_, s_, D_MODEL)
    return (o @ w_out).astype(h.dtype)

def swiglu(h, w13, w2):
    g, u = jnp.split(h @ w13, 2, axis=-1)
    return ((jax.nn.silu(g) * u) @ w2).astype(h.dtype)

def second_inputs(seed: int = 0) -> dict:
    key = jax.random.key(seed)
    ks = jax.random.split(key, 14)
    nrm = lambda k, shape, fan_in: jax.random.normal(k, shape, jnp.float32) * (fan_in ** -0.5)
    gain = lambda k, shape: 1.0 + 0.02 * jax.random.normal(k, shape, jnp.float32)
    return {
        "x": jax.random.normal(ks[0], (BATCH, SEQ, D_MODEL), jnp.float32),
        "norm_mix": gain(ks[1], (DEPTH_2, D_MODEL)),
        "norm_ffn": gain(ks[2], (DEPTH_2, D_MODEL)),
        "hgrn_w_in": nrm(ks[3], (N_A_LAYERS, D_MODEL, 2 * HGRN_FDIM + 2 * D_MODEL), D_MODEL),
        "hgrn_lb_logits": 1.0 + 0.1 * jax.random.normal(ks[4], (N_A_LAYERS + 1, HGRN_FDIM), jnp.float32),
        "hgrn_out_norm": gain(ks[5], (N_A_LAYERS, D_MODEL)),
        "hgrn_w_out": nrm(ks[6], (N_A_LAYERS, D_MODEL, D_MODEL), D_MODEL),
        "moba_w_in": nrm(ks[7], (N_B_LAYERS, D_MODEL, 3 * D_MODEL), D_MODEL),
        "moba_w_out": nrm(ks[8], (N_B_LAYERS, D_MODEL, D_MODEL), D_MODEL),
        "rel_bias_table": 0.5 * jax.random.normal(ks[9], (REL_BUCKETS, ATTN_HEADS), jnp.float32),
        "ffn_w13": nrm(ks[10], (DEPTH_2, D_MODEL, 2 * D_FF_2), D_MODEL),
        "ffn_w2": nrm(ks[11], (DEPTH_2, D_FF_2, D_MODEL), D_FF_2),
        "final_norm": gain(ks[12], (D_MODEL,)),
    }

def second_block(x, norm_mix, norm_ffn, hgrn_w_in, hgrn_lb_logits, hgrn_out_norm, hgrn_w_out,
              moba_w_in, moba_w_out, rel_bias_table, ffn_w13, ffn_w2, final_norm):
    lb_all = jnp.cumsum(jax.nn.softmax(hgrn_lb_logits.astype(jnp.float32), axis=0), axis=0)[:N_A_LAYERS]
    h = x
    for layer in range(DEPTH_2):
        y = rms_norm_2(h, norm_mix[layer])
        idx = layer // N_MIXERS
        if layer % N_MIXERS == 0:
            y = hgrn2_mixer(y, hgrn_w_in[idx], hgrn_w_out[idx], lb_all[idx], hgrn_out_norm[idx])
        else:
            y = moba_mixer(y, moba_w_in[idx], moba_w_out[idx], rel_bias_table)
        h = h + y
        h = h + swiglu(rms_norm_2(h, norm_ffn[layer]), ffn_w13[layer], ffn_w2[layer])
    return rms_norm_2(h, final_norm)


def setup_inputs(seed=0):
    out = dict(first_inputs(seed))
    for name, value in second_inputs(seed + 1).items():
        if name != "x":
            out[name + "_2"] = value
    return out


def reference(
    x, mix_norm_pre, mix_norm_post, w_in, conv_a_w, conv_a_b, w_rg_a, b_rg_a, w_rg_x, b_rg_x,
    lru_lambda, b_forget, b_merge, w_proj_a, w_proj_b, w_out, ffn_norm_pre, ffn_norm_post, w_up,
    conv_f_w, conv_f_b, w_down, norm_mix_2, norm_ffn_2, hgrn_w_in_2, hgrn_lb_logits_2,
    hgrn_out_norm_2, hgrn_w_out_2, moba_w_in_2, moba_w_out_2, rel_bias_table_2, ffn_w13_2,
    ffn_w2_2, final_norm_2,
):
    x = first_block(
        x, mix_norm_pre, mix_norm_post, w_in, conv_a_w, conv_a_b, w_rg_a, b_rg_a, w_rg_x,
        b_rg_x, lru_lambda, b_forget, b_merge, w_proj_a, w_proj_b, w_out, ffn_norm_pre,
        ffn_norm_post, w_up, conv_f_w, conv_f_b, w_down,
    )
    return second_block(
        x, norm_mix_2, norm_ffn_2, hgrn_w_in_2, hgrn_lb_logits_2, hgrn_out_norm_2, hgrn_w_out_2,
        moba_w_in_2, moba_w_out_2, rel_bias_table_2, ffn_w13_2, ffn_w2_2, final_norm_2,
    )


_drawn_inputs = setup_inputs


def setup_inputs(seed=0):
    import zlib

    import numpy as np

    out = dict(_drawn_inputs(seed))
    spreads = {}
    factors = {'b_rg_a': 8.0,
     'b_rg_x': 8.0,
     'b_merge': 8.0,
     'conv_f_b': 5.976,
     'norm_mix_2': 6.742,
     'norm_ffn_2': 4.567,
     'hgrn_lb_logits_2': 8.0,
     'hgrn_out_norm_2': 8.0,
     'final_norm_2': 2.832}
    for name, (base, spread) in spreads.items():
        noise = np.random.default_rng([zlib.crc32(name.encode()), seed]).standard_normal(out[name].shape)
        drawn = base * np.exp(spread * noise) if base else spread * noise
        out[name] = __import__('jax').numpy.asarray(drawn.astype(out[name].dtype))
    for name, factor in factors.items():
        out[name] = (out[name] * factor).astype(out[name].dtype)
    return out
```

```python
from contextlib import ExitStack

import concourse.bass as bass
from concourse import mybir

F32 = mybir.dt.float32
F32R = mybir.dt.float32r
I32 = mybir.dt.int32
ACT = mybir.ActivationFunctionType
ALU = mybir.AluOpType
AX = mybir.AxisListType

P = 128
S = 256
D = 1024
C = D // P
D_RNN = 1280
R = D_RNN // P
RNN_BLOCK = 80
H_FOX, DH_FOX = 16, 64
H_MOBA, DH_MOBA = 8, 128
BUCKETS = 32
F1 = 3 * D // P
F2 = 2816 // P
EPS = 1e-6
LRU_C = 8.0
NEG = -1.0e30
BLK = 8
RING = 4
BANKS = 4
AHEAD = 3

PHASES = [("xa", 10, 10), ("ga", 10, 10), ("q", 8, 8), ("k", 8, 8), ("gates", 8, 0), ("v", 8, 8),
          ("sa", 8, 8), ("sb", 8, 8), ("pa", 10, 8), ("pb", 8, 8), ("wo", 8, 8), ("up", 2 * F1, 2 * F1),
          ("down", 24, 8), ("hf", 8, 8), ("hq", 8, 8), ("hi", 8, 8), ("hg", 8, 8), ("ho", 8, 8),
          ("up1", 2 * F2, 2 * F2), ("down1", 24, 8), ("mq", 8, 8), ("mk", 8, 8), ("mv", 8, 8), ("mo", 8, 8),
          ("up2", 2 * F2, 2 * F2), ("down2", 24, 8)]
PART, TILE = {}, {}
_p = _t = 0
for _name, _parts, _tiles in PHASES:
    PART[_name], TILE[_name] = _p, _t
    _p, _t = _p + _parts, _t + _tiles
PARTS, TILES = _p, _t

GATE_IN = [[0, 1], [0, 1, 2], [1, 2, 3], [2, 3, 4], [3, 4]]
GATE_PARTS = [[0, 1, 2], [3, 4]]

COLS, NCOL = {}, 0
for _name, _n in [("mix_pre", C), ("mix_post", C), ("conv_w", 4 * R), ("conv_b", R), ("b_a", R), ("b_x", R),
                  ("lam", R), ("b_merge", 2 * C), ("ffn_pre", C), ("ffn_post", C), ("fconv_w", 3 * 2 * F1),
                  ("fconv_b", 2 * F1), ("norm_mix", 2 * C), ("norm_ffn", 2 * C), ("lb", 2 * C), ("out_norm", C),
                  ("final", C), ("b_forget", 1)]:
    COLS[_name] = NCOL
    NCOL += _n

EXT = 3 * P
LEVELS = 8

UNITS = 82


def build(nc, stream, par_d, x_d, wf_d, table_d, onehot_d, ident_d, mask_d, lmask_d, out_d):
    scr = nc.dram_tensor("bias_rows", [H_MOBA, P, EXT], F32, kind="Internal")
    with ExitStack() as ctx:
        def sb(name, shape, dt=F32):
            return ctx.enter_context(nc.sbuf_tensor(name, shape, dt))

        def sem(name):
            return ctx.enter_context(nc.semaphore(name))

        raw = sb("raw", [P, RING, BLK * P])
        w_hi = sb("w_hi", [P, RING, BLK * P], F32R)
        w_lo = sb("w_lo", [P, RING, BLK * P], F32R)
        h_hi = sb("h_hi", [P, C, S], F32R)
        h_lo = sb("h_lo", [P, C, S], F32R)
        u_hi = sb("u_hi", [P, F1, S], F32R)
        u_lo = sb("u_lo", [P, F1, S], F32R)
        F = sb("work", [P, UNITS, S])
        par = sb("par", [P, NCOL])
        der = sb("derived", [P, 64])
        ident = sb("ident", [P, P])
        mask = sb("mask", [P, EXT])
        ones = sb("ones", [P, P])
        wf = sb("wf", [P, C, H_FOX])
        att_s = sb("att_s", [P, 2, EXT])
        att_pt = sb("att_pt", [P, 2, EXT])
        stat_s = sb("att_stat", [P, 2, 8])
        ncum = sb("ncum", [H_FOX, S])
        cum_t = sb("cum_t", [P, 2, H_FOX])
        bank = [ctx.enter_context(nc.psum_tensor(f"bank{i}", [P, 512], F32)) for i in range(8)]

        X = F[:, 52:60, :]
        HT, SQ, M = F[:, 20:28, :], F[:, 60:68, :], F[:, 12:20, :]
        RS, RSTD = F[:, 28, :], F[:, 29, :]
        XA, XC = F[:, 0:10, :], F[:, 10:20, :]
        GA = XA
        Q, K, V = F[:, 20:28, :], F[:, 28:36, :], F[:, 36:44, :]
        SGA, SGB = F[:, 44:52, :], F[:, 52:60, :]
        RG, IG, DEN = F[:, 60:70, :], F[:, 70:80, :], F[:, 80:82, :]
        PRA, PRB = F[:, 70:78, :], F[:, 0:8, :]
        ext = F[:, 30:42, :].rearrange("p u t -> p (u t)").rearrange("p (h e) -> p h e", h=H_MOBA)
        onehot = F[0:BUCKETS, 42:44, :].rearrange("p u t -> p (u t)")[:, 0:EXT]
        table = F[0:BUCKETS, 44, 0:H_MOBA]
        UB, YB, GB, PB = F[:, 0:4, :], F[:, 4:8, :], F[:, 8:10, :], F[:, 10:12, :]
        FG, CUM, KK, QS = F[:, 0:8, :], F[:, 8:16, :], F[:, 16:24, :], F[:, 24:32, :]
        INP, OG = F[:, 32:40, :], F[:, 40:48, :]
        LM = F[:, 48:52, :].rearrange("p u t -> p (u t)").bitcast(I32).rearrange("p (l t) -> p l t", l=LEVELS)
        EB = [F[:, 0:8, :], F[:, 60:68, :]]
        PD = F[:, 68:76, :].rearrange("p u (z t) -> p (u z) t", z=2)
        PX = F[:, 76:80, :].rearrange("p u (z t) -> p (u z) t", z=2)
        ONES_ROW = F[:, 80, :]
        OH = F[:, 8:16, :]
        MQ, MK, MV = F[:, 0:8, :], F[:, 8:16, :], F[:, 32:40, :]
        BIAS = F[:, 68:80, :].rearrange("p u t -> p (u t)").rearrange("p (h e) -> p h e", h=H_MOBA)

        def col(name, c=0):
            return par[:, COLS[name] + c:COLS[name] + c + 1]

        def dcol(name, e):
            return par[:, bass.ds(e + COLS[name], 1)]

        D_SP, D_NSP, D_LB, D_1LB, D_T = 0, 10, 20, 28, 36

        landed = [sem(f"part_landed{i}") for i in range(RING)]
        hi_ready, lo_ready = sem("hi_ready"), sem("lo_ready")
        part_done, evacuated = sem("part_done"), sem("evacuated")
        par_in, x_in, wf_in, tab_in, cst_in, x_back, lm_in, bias_in = (
            sem(n) for n in ("par_in", "x_in", "wf_in", "table_in", "const_in", "x_back", "lmask_in", "bias_in"))
        ext_out, out_done = sem("bias_rows_out"), sem("out_done")
        ones_ready = sem("ones_ready")
        sq_ready, stat_done, rms_ready, rstd_ready = (
            sem(n) for n in ("square_ready", "stat_done", "rms_ready", "rstd_ready"))
        ht_ready, hh_ready, hl_ready, x_ready = sem("h_ready"), sem("h_hi_ready"), sem("h_lo_ready"), sem("x_ready")
        post_t = sem("post_scaled")
        ext_mm, ext_ready = sem("bias_rows_made"), sem("bias_rows_ready")
        act_step, dve_step, pool_step = sem("act_step"), sem("dve_step"), sem("pool_step")
        der_ready, sp_ln, lb_exp = sem("derived_ready"), sem("softplus_ln"), sem("lb_exp")
        f_mm, f_ln, cum_ready, cumt_mm, cumt_ready = (
            sem(n) for n in ("f_mm", "f_ln", "cum_ready", "cum_t_mm", "cum_t_ready"))
        tap_done, taps_done, xch_ready, xcl_ready = (
            sem(n) for n in ("tap_done", "taps_done", "xc_hi_ready", "xc_lo_ready"))
        gates_evac, ix_done, tanh_done, decay_done, gain_done, root_done, scan_done, ya_done, yah, yal = (
            sem(n) for n in ("gates_evac", "ix_done", "tanh_done", "decay_done", "gain_done", "root_done",
                             "scan_done", "ya_done", "ya_hi_ready", "ya_lo_ready"))
        s_mm, s_evac, mx_done, negmax, exp_done, rsum_done, p_ready, pt_mm, pt_copied, pv_mm, y_hi, y_lo = (
            sem(n) for n in ("scores_mm", "scores_evac", "max_done", "negmax_ready", "exp_done", "rsum_ready",
                             "probs_ready", "probs_t_mm", "probs_t_copied", "pv_mm", "y_hi_ready", "y_lo_ready"))
        merge_step, merged, mh, ml = sem("merge_step"), sem("merged"), sem("merged_hi"), sem("merged_lo")
        pair_free, gate_ready, prod_done, uh_ready, ul_ready = (
            sem(n) for n in ("pair_free", "gate_ready", "product_done", "u_hi_ready", "u_lo_ready"))
        f_ready, k_ready, logf_ready, hcum_ready = sem("f_ready"), sem("k_ready"), sem("logf_ready"), sem("hcum_ready")
        pd_zero, one_row = sem("pd_zeroed"), sem("ones_row_ready")
        arg_ready, dec_ready, x_low, x_up, lev_mm, lev_sel, px_copied = (
            sem(n) for n in ("level_arg", "level_decay", "level_keys", "level_queries", "level_mm", "level_taken",
                             "cross_copied"))
        o_mm, o_evac, o_norm, o_gated = sem("o_mm"), sem("o_evac"), sem("o_normed"), sem("o_gated")
        bias_masked = sem("bias_masked")
        res_in = sem("branch_out")

        block = ctx.enter_context(nc.Block())

        def lin(i, m, c):
            return c if isinstance(i, int) else i * m + c

        class Chain:

            def __init__(self, eng, s):
                self.eng, self.s, self.n = eng, s, 0

            def wait(self, ins):
                ins.then_inc(self.s, 1)
                self.n += 1
                self.eng.wait_ge(self.s, self.n)

        NORMS = {n: i for i, n in enumerate(["mix", "post", "ffn", "post2", "n0", "o", "f0", "n1", "f1", "final"])}
        X_COUNT = {"mix": 0, "ffn": 8, "n0": 16, "f0": 24, "n1": 32, "f1": 40, "final": 48}
        H_COUNT = {n: 8 * i for i, n in enumerate(["mix", "ffn", "n0", "f0", "n1", "f1"])}

        @block.sync
        def _(sp):
            sp.dma_start(X, x_d).then_inc(x_in, 16)
            sp.dma_start(par[:, :], par_d).then_inc(par_in, 16)
            for n in range(RING):
                sp.dma_start(raw[:, n, :], stream[n]).then_inc(landed[n], 16)
            loops = (PARTS - RING) // RING

            def load(i, c):
                sp.wait_ge(lo_ready, lin(i, RING, c) - RING + 1)
                src = (stream[bass.ds(lin(i, RING, c), 1), :, :].rearrange("o p f -> p (o f)")
                       if not isinstance(i, int) else stream[c])
                sp.dma_start(raw[:, c % RING, :], src).then_inc(landed[c % RING], 16)

            with sp.Fori(1, 1 + loops) as i:
                for c in range(RING):
                    load(i, c)
            for c in range(RING * (1 + loops), PARTS):
                load(0, c)

        @block.scalar
        def _(act):
            A = nc.scalar.activation
            chain = Chain(act, act_step)

            def hi(i, m, c):
                slot = c % RING
                if isinstance(i, int) and c >= PARTS:
                    return
                act.wait_ge(landed[slot], lin(i, 16 * m // RING, 16 * (c // RING + 1)))
                if c >= RING or not isinstance(i, int):
                    act.wait_ge(part_done, lin(i, m, c - RING + 1))
                A(w_hi[:, slot, :], raw[:, slot, :], ACT.Copy).then_inc(hi_ready, 1)

            def step(name, j, i=0, m=0):
                c = PART[name] + j
                hi(i, m, c + AHEAD)
                act.wait_ge(part_done, lin(i, m, c + 1))

            def out_of(t):
                return bank[t % BANKS][:, 0:S]

            def squares(norm, src_wait=None):
                b = 8 * NORMS[norm]
                for c in range(C):
                    if norm == "mix":
                        if c == 0:
                            act.wait_ge(x_in, 16)
                    else:
                        act.wait_ge(x_ready, X_COUNT[norm] - 8 + c + 1)
                    A(SQ[:, c, :], X[:, c, :], ACT.Square).then_inc(sq_ready, 1)

            def rms(norm):
                n = NORMS[norm]
                act.wait_ge(stat_done, n + 1)
                A(RS, bank[4][:, 0:S], ACT.Sqrt, scale=1.0 / D, bias=der[:, 63:64]).then_inc(rms_ready, 1)

            def split_h(norm):
                b = H_COUNT[norm]
                for c in range(C):
                    act.wait_ge(ht_ready, b + c + 1)
                    A(h_hi[:, c, :], HT[:, c, :], ACT.Copy).then_inc(hh_ready, 1)

            act.wait_ge(par_in, 16)
            act.wait_ge(der_ready, 1)
            squares("mix")
            lam = par[:, COLS["lam"]:COLS["lam"] + R]
            chain.wait(A(der[:, D_T:D_T + R], lam, ACT.Abs))
            chain.wait(A(der[:, D_T:D_T + R], der[:, D_T:D_T + R], ACT.Exp, scale=-1.0))
            A(der[:, D_SP:D_SP + R], der[:, D_T:D_T + R], ACT.Ln, bias=1.0).then_inc(sp_ln, 1)
            act.wait_ge(der_ready, 3)
            for r in range(2):
                A(der[:, 46 + 8 * r:54 + 8 * r], der[:, 46 + 8 * r:54 + 8 * r], ACT.Exp).then_inc(lb_exp, 1)
            rms("mix")
            for h in range(H_MOBA):
                act.wait_ge(ext_mm, h + 1)
                A(ext[:, h, :], bank[5 + h % 2][:, 0:EXT], ACT.Copy).then_inc(ext_ready, 1)
            split_h("mix")
            for n in range(AHEAD):
                hi(0, 0, n)
            act.wait_ge(f_mm, 1)
            z, az = att_s[0:H_FOX, 0, 0:S], att_s[0:H_FOX, 1, 0:S]
            chain.wait(A(z, bank[7][0:H_FOX, 0:S], ACT.Identity, bias=par[0:H_FOX, COLS["b_forget"]:COLS["b_forget"] + 1]))
            chain.wait(A(az, z, ACT.Abs))
            chain.wait(A(az, az, ACT.Exp, scale=-1.0))
            A(az, az, ACT.Ln, bias=1.0).then_inc(f_ln, 1)
            for t in range(R):
                step("xa", t)
                A(XA[:, t, :], out_of(TILE["xa"] + t), ACT.Copy)
                A(XC[:, t, :], out_of(TILE["xa"] + t), ACT.Identity, scale=col("conv_w", 3 * R + t),
                  bias=col("conv_b", t)).then_inc(evacuated, 1)
                if t >= 1:
                    act.wait_ge(taps_done, t)
                    A(u_hi[:, t - 1, :], XC[:, t - 1, :], ACT.Copy).then_inc(xch_ready, 1)
            act.wait_ge(taps_done, R)
            A(u_hi[:, R - 1, :], XC[:, R - 1, :], ACT.Copy).then_inc(xch_ready, 1)
            for t in range(R):
                step("ga", t)
                A(GA[:, t, :], out_of(TILE["ga"] + t), ACT.Gelu_apprx_tanh).then_inc(evacuated, 1)
            for t in range(C):
                step("q", t)
                A(Q[:, t, :], out_of(TILE["q"] + t), ACT.Copy, scale=DH_FOX ** -0.5).then_inc(evacuated, 1)
            act.wait_ge(ext_out, 16)
            for t in range(C):
                step("k", t)
                A(K[:, t, :], out_of(TILE["k"] + t), ACT.Copy).then_inc(evacuated, 1)
            for n in range(8):
                step("gates", n)
                m, g = n // 4, n // 2 % 2
                for j, o in enumerate(GATE_PARTS[n % 2]):
                    src = bank[4 + 2 * (n % 2) + j // 2][:, j % 2 * S:j % 2 * S + S]
                    dst, b = (IG, "b_x") if m == 0 else (RG, "b_a")
                    A(dst[:, 5 * g + o, :], src, ACT.Sigmoid, bias=col(b, 5 * g + o)).then_inc(gates_evac, 1)

            def lru_decay(t):
                act.wait_ge(gates_evac, R + t + 1)
                act.wait_ge(ix_done, t + 1)
                A(XC[:, t, :], RG[:, t, :], ACT.Tanh, scale=der[:, D_SP + t:D_SP + t + 1]).then_inc(tanh_done, 1)
                act.wait_ge(tanh_done, t + 1)
                A(RG[:, t, :], RG[:, t, :], ACT.Exp, scale=der[:, D_NSP + t:D_NSP + t + 1]).then_inc(decay_done, 1)

            def lru_root():
                act.wait_ge(gain_done, R)
                A(XC, XC, ACT.Sqrt).then_inc(root_done, 1)

            def lru_out(t):
                act.wait_ge(ya_done, t + 1)
                A(u_hi[:, R + t, :], GA[:, t, :], ACT.Copy).then_inc(yah, 1)

            act.wait_ge(sp_ln, 1)
            act.wait_ge(der_ready, 5)
            for n in range(0, 8, 2):
                step("v", n)
                step("v", n + 1)
                for tok in range(2):
                    A(V[:, 4 * tok + n // 2, :], out_of(TILE["v"] + n + tok), ACT.Copy).then_inc(evacuated, 1)
                for t in {0: [0, 1], 2: [2, 3, 4], 4: [5, 6], 6: [7, 8, 9]}[n]:
                    lru_decay(t)
            for n in range(2 * C):
                name = "sa" if n < C else "sb"
                step(name, n % C)
                dst = SGA if n < C else SGB
                A(dst[:, n % C, :], out_of(TILE["sa"] + n), ACT.Sigmoid, bias=col("b_merge", n)).then_inc(evacuated, 1)
                if n == 2:
                    lru_root()
                if 4 <= n < 4 + R:
                    lru_out(n - 4)

            def attention(H, first, y_of, out_of_head, heads_out):
                for s in range(H + 2):
                    if s < H:
                        n, b = first + s, s % 2
                        act.wait_ge(negmax, n + 1)
                        for j, (a, e) in enumerate([(0, P), (P, EXT)]):
                            A(att_s[:, b, a:e], att_s[:, b, a:e], ACT.Exp, bias=stat_s[:, b, 2 + j:3 + j],
                              accum_out=stat_s[:, b, 4 + j:5 + j]).then_inc(exp_done, 1)
                    if 1 <= s <= H:
                        n, b = first + s - 1, (s - 1) % 2
                        act.wait_ge(pt_mm, n + 1)
                        if n >= 2:
                            act.wait_ge(pv_mm, n - 1)
                        A(att_pt[:, b, :], bank[6][:, 0:EXT], ACT.Copy).then_inc(pt_copied, 1)
                    if s >= 2 and (s - 2) % heads_out == heads_out - 1:
                        act.wait_ge(pv_mm, first + s - 1)
                        A(y_of((s - 2) // heads_out), bank[7][:, 0:S], ACT.Copy).then_inc(y_hi, 1)

            attention(H_FOX, 0, lambda t: u_hi[:, t, :], None, 2)

            for t in range(C):
                last = (10 * t + 9) // BLK
                for n in range((10 * t - 1) // BLK + 1 if t else 0, last + 1):
                    step("pa", n)
                A(PRA[:, t, :], out_of(TILE["pa"] + t), ACT.Copy).then_inc(evacuated, 1)
            for t in range(C):
                step("pb", t)
                A(PRB[:, t, :], out_of(TILE["pb"] + t), ACT.Copy).then_inc(evacuated, 1)
                if t >= 1:
                    act.wait_ge(merged, t)
                    A(h_hi[:, t - 1, :], PRA[:, t - 1, :], ACT.Copy).then_inc(mh, 1)
            act.wait_ge(merged, C)
            A(h_hi[:, C - 1, :], PRA[:, C - 1, :], ACT.Copy).then_inc(mh, 1)

            def branch_tile(t, tile, square):
                if square:
                    A(SQ[:, t, :], out_of(tile), ACT.Square).then_inc(sq_ready, 1)
                A(M[:, t, :], out_of(tile), ACT.Copy).then_inc(evacuated, 1)

            def down(name, square):
                base = PART[name]

                def body(i, c0):
                    for j in range(12):
                        if not (name == "down2" and c0 + j + AHEAD >= 24):
                            hi(i, 12, base + c0 + j + AHEAD)
                        if j % 3 == 2:
                            act.wait_ge(part_done, lin(i, 12, base + c0 + j + 1))
                            t = TILE[name] + (c0 + j) // 3
                            dst = (bass.ds(i * 4 + (c0 + j) // 3, 1) if not isinstance(i, int)
                                   else slice((c0 + j) // 3, (c0 + j) // 3 + 1))
                            src = out_of(t).rearrange("p (o t) -> p o t", o=1)
                            if square:
                                A(SQ[:, dst, :], src, ACT.Square).then_inc(sq_ready, 1)
                            A(M[:, dst, :], src, ACT.Copy).then_inc(evacuated, 1)

                body(0, 0)
                body(0, 12)

            for t in range(C):
                step("wo", t)
                branch_tile(t, TILE["wo"] + t, True)
            rms("post")
            squares("ffn")
            rms("ffn")
            split_h("ffn")

            with act.Fori(0, 2 * F1 // 4) as i:
                for j in range(4):
                    c = PART["up"] + j
                    hi(i, 4, c + AHEAD)
                    act.wait_ge(part_done, lin(i, 4, c + 1))
                    act.wait_ge(taps_done, lin(i, 4, R + j - 3))
                    act.wait_ge(pair_free, lin(i, 2, j // 2 + 1))
                    src = out_of(TILE["up"] + j)
                    A(UB[:, j, :], src, ACT.Copy)
                    A(YB[:, j, :], src, ACT.Identity, scale=dcol("fconv_w", i * 4 + (2 * 2 * F1 + j)),
                      bias=dcol("fconv_b", i * 4 + j)).then_inc(evacuated, 1)
                    if j % 2:
                        act.wait_ge(taps_done, lin(i, 4, R + j))
                        A(GB[:, j // 2, :], YB[:, j - 1, :], ACT.Gelu_apprx_tanh).then_inc(gate_ready, 1)
            down("down", True)
            rms("post2")
            squares("n0")
            rms("n0")
            split_h("n0")

            for t in range(C):
                step("hf", t)
                A(FG[:, t, :], out_of(TILE["hf"] + t), ACT.Sigmoid).then_inc(evacuated, 1)
            for t in range(C):
                step("hq", t)
                A(QS[:, t, :], out_of(TILE["hq"] + t), ACT.Silu).then_inc(evacuated, 1)
            act.wait_ge(k_ready, C)
            A(CUM, FG, ACT.Ln).then_inc(logf_ready, 1)
            for n in range(0, 8, 2):
                step("hi", n)
                step("hi", n + 1)
                for tok in range(2):
                    A(INP[:, 4 * tok + n // 2, :], out_of(TILE["hi"] + n + tok), ACT.Copy).then_inc(evacuated, 1)
            for t in range(C):
                step("hg", t)
                A(OG[:, t, :], out_of(TILE["hg"] + t), ACT.Sigmoid).then_inc(evacuated, 1)
            for l in range(1, LEVELS + 1):
                e = EB[l % 2]
                act.wait_ge(arg_ready, 2 * l)
                A(e, e, ACT.Exp).then_inc(dec_ready, 1)
            for g in range(2):
                act.wait_ge(lev_mm, 4 * LEVELS + g + 1)
                A(PX[:, 4 * g:4 * g + 4, :], bank[4 + g][:, :].rearrange("p (h t) -> p h t", h=4),
                  ACT.Copy).then_inc(px_copied, 1)
            for c in range(C):
                act.wait_ge(o_mm, c + 1)
                src = bank[5 + c % 3][:, 0:S]
                A(SQ[:, c, :], src, ACT.Square).then_inc(sq_ready, 1)
                A(OH[:, c, :], src, ACT.Copy).then_inc(o_evac, 1)
            rms("o")
            for c in range(C):
                act.wait_ge(o_gated, c + 1)
                A(h_hi[:, c, :], OH[:, c, :], ACT.Copy).then_inc(mh, 1)
            for t in range(C):
                step("ho", t)
                branch_tile(t, TILE["ho"] + t, False)

            def swiglu(name, norm, pairs0, evac0):
                squares(norm)
                rms(norm)
                split_h(norm)
                with act.Fori(0, 2 * F2 // 4) as i:
                    for j in range(4):
                        c = PART[name] + j
                        hi(i, 4, c + AHEAD)
                        act.wait_ge(part_done, lin(i, 4, c + 1))
                        act.wait_ge(pair_free, lin(i, 2, pairs0 + j // 2 + 1))
                        src = out_of(TILE[name] + j)
                        if j % 2 == 0:
                            A(GB[:, j // 2, :], src, ACT.Silu).then_inc(evacuated, 1)
                        else:
                            A(YB[:, j, :], src, ACT.Copy).then_inc(evacuated, 1)

            swiglu("up1", "f0", F1, None)
            down("down1", False)
            squares("n1")
            rms("n1")
            split_h("n1")
            for t in range(C):
                step("mq", t)
                A(MQ[:, t, :], out_of(TILE["mq"] + t), ACT.Copy).then_inc(evacuated, 1)
            for t in range(C):
                step("mk", t)
                A(MK[:, t, :], out_of(TILE["mk"] + t), ACT.Copy).then_inc(evacuated, 1)
            for n in range(0, 8, 2):
                step("mv", n)
                step("mv", n + 1)
                for tok in range(2):
                    A(MV[:, 4 * tok + n // 2, :], out_of(TILE["mv"] + n + tok), ACT.Copy).then_inc(evacuated, 1)
            attention(H_MOBA, H_FOX, lambda t: h_hi[:, t, :], None, 1)
            for t in range(C):
                step("mo", t)
                branch_tile(t, TILE["mo"] + t, False)
            swiglu("up2", "f1", F1 + F2, None)
            down("down2", False)
            squares("final")
            rms("final")
            for c in range(0, C, 4):
                act.wait_ge(ht_ready, 48 + c + 4)
                act.dma_start(out_d[:, c:c + 4, :], HT[:, c:c + 4, :]).then_inc(out_done, 16)
            act.wait_ge(out_done, 32)

        @block.vector
        def _(dve):
            v = nc.vector
            chain = Chain(dve, dve_step)

            def lo(i, m, c):
                slot = c % RING
                if isinstance(i, int) and c >= PARTS:
                    return
                dve.wait_ge(hi_ready, lin(i, m, c + 1))
                v.tensor_tensor(w_lo[:, slot, :], raw[:, slot, :], w_hi[:, slot, :].bitcast(F32),
                                ALU.subtract).then_inc(lo_ready, 1)

            def step(name, j):
                lo(0, 0, PART[name] + j + AHEAD)

            def rstd(norm):
                dve.wait_ge(rms_ready, NORMS[norm] + 1)
                v.reciprocal(RSTD, RS).then_inc(rstd_ready, 1)
                dve.wait_ge(rstd_ready, NORMS[norm] + 1)

            def make_h(norm, gain, c0=0, split=True):
                rstd(norm)
                for c in range(C):
                    v.scalar_tensor_tensor(out=HT[:, c, :], in0=X[:, c, :], scalar=col(gain, c0 + c), in1=RSTD,
                                           op0=ALU.mult, op1=ALU.mult).then_inc(ht_ready, 1)
                if split:
                    b = H_COUNT[norm]
                    for c in range(C):
                        dve.wait_ge(hh_ready, b + c + 1)
                        v.tensor_tensor(h_lo[:, c, :], HT[:, c, :], h_hi[:, c, :].bitcast(F32),
                                        ALU.subtract).then_inc(hl_ready, 1)

            def add_normed(norm, gain, evac0):
                rstd(norm)
                n0 = 8 * (norm == "post2")
                for c in range(C):
                    v.scalar_tensor_tensor(out=M[:, c, :], in0=M[:, c, :], scalar=col(gain, c), in1=RSTD,
                                           op0=ALU.mult, op1=ALU.mult).then_inc(post_t, 1)
                for c in range(C):
                    dve.wait_ge(post_t, n0 + c + 1)
                    v.tensor_tensor(X[:, c, :], X[:, c, :], M[:, c, :], ALU.add).then_inc(x_ready, 1)

            v.memset(der[:, 63:64], EPS).then_inc(der_ready, 1)
            v.memset(ones[:, :], 1.0).then_inc(ones_ready, 1)
            dve.wait_ge(par_in, 16)
            l0, l1 = (par[:, COLS["lb"] + C * r:COLS["lb"] + C * r + C] for r in range(2))
            chain.wait(v.tensor_tensor(der[:, D_LB:D_LB + C], l0, l1, ALU.max))
            for r, l in enumerate((l0, l1)):
                v.tensor_tensor(der[:, 46 + 8 * r:54 + 8 * r], l, der[:, D_LB:D_LB + C],
                                ALU.subtract).then_inc(der_ready, 1)
            make_h("mix", "mix_pre")
            for n in range(AHEAD):
                lo(0, 0, n)
            lam = par[:, COLS["lam"]:COLS["lam"] + R]
            dve.wait_ge(sp_ln, 1)
            chain.wait(v.tensor_scalar(der[:, D_NSP:D_NSP + R], lam, -1.0, 0.0, ALU.mult, ALU.max))
            chain.wait(v.tensor_tensor(der[:, D_SP:D_SP + R], der[:, D_SP:D_SP + R], der[:, D_NSP:D_NSP + R], ALU.add))
            chain.wait(v.tensor_scalar(der[:, D_NSP:D_NSP + R], der[:, D_SP:D_SP + R], -LRU_C, None, ALU.mult))
            v.tensor_scalar(der[:, D_SP:D_SP + R], der[:, D_SP:D_SP + R], LRU_C, None, ALU.mult).then_inc(der_ready, 1)
            dve.wait_ge(lb_exp, 2)
            e0, e1 = der[:, 46:54], der[:, 54:62]
            chain.wait(v.tensor_tensor(e1, e0, e1, ALU.add))
            chain.wait(v.reciprocal(e1, e1))
            chain.wait(v.tensor_tensor(der[:, D_LB:D_LB + C], e0, e1, ALU.mult))
            v.tensor_scalar(der[:, D_1LB:D_1LB + C], der[:, D_LB:D_LB + C], -1.0, 1.0, ALU.mult,
                            ALU.add).then_inc(der_ready, 1)
            dve.wait_ge(f_ln, 1)
            z, az = att_s[0:H_FOX, 0, 0:S], att_s[0:H_FOX, 1, 0:S]
            chain.wait(v.tensor_scalar(z, z, 0.0, None, ALU.min))
            chain.wait(v.tensor_tensor(az, az, z, ALU.subtract))
            chain.wait(v.memset(z, 1.0))
            v.tensor_tensor_scan(ncum[:, :], z, az, 0.0, ALU.mult, ALU.add).then_inc(cum_ready, 1)
            for t in range(R):
                step("xa", t)
                dve.wait_ge(evacuated, TILE["xa"] + t + 1)
                for j in (1, 2, 3):
                    ins = v.scalar_tensor_tensor(out=XC[:, t, j:S], in0=XA[:, t, 0:S - j],
                                                 scalar=col("conv_w", (3 - j) * R + t), in1=XC[:, t, j:S],
                                                 op0=ALU.mult, op1=ALU.add)
                    if j < 3:
                        chain.wait(ins)
                    else:
                        ins.then_inc(taps_done, 1)
                if t == 5:
                    dve.wait_ge(cumt_mm, 1)
                    v.tensor_scalar(cum_t[:, :, :], bank[5][:, 0:2 * H_FOX].rearrange("p (b h) -> p b h", b=2), -1.0,
                                    None, ALU.mult).then_inc(cumt_ready, 1)
                if t >= 1:
                    dve.wait_ge(xch_ready, t)
                    v.tensor_tensor(u_lo[:, t - 1, :], XC[:, t - 1, :], u_hi[:, t - 1, :].bitcast(F32),
                                    ALU.subtract).then_inc(xcl_ready, 1)
            dve.wait_ge(xch_ready, R)
            v.tensor_tensor(u_lo[:, R - 1, :], XC[:, R - 1, :], u_hi[:, R - 1, :].bitcast(F32),
                            ALU.subtract).then_inc(xcl_ready, 1)
            for name, n in (("ga", R), ("q", C), ("k", C), ("gates", 8)):
                for t in range(n):
                    step(name, t)

            def lru_ix(t):
                dve.wait_ge(gates_evac, t + 1)
                dve.wait_ge(xcl_ready, R)
                v.tensor_tensor(IG[:, t, :], IG[:, t, :], XC[:, t, :], ALU.mult).then_inc(ix_done, 1)

            def lru_gain(t):
                d = DEN[:, t % 2, :]
                dve.wait_ge(tanh_done, t + 1)
                chain.wait(v.tensor_scalar(d, XC[:, t, :], 1.0, None, ALU.add))
                chain.wait(v.reciprocal(d, d))
                v.scalar_tensor_tensor(out=XC[:, t, :], in0=XC[:, t, :], scalar=2.0, in1=d, op0=ALU.mult,
                                       op1=ALU.mult).then_inc(gain_done, 1)

            def lru_scan(t):
                dve.wait_ge(root_done, 1)
                dve.wait_ge(decay_done, t + 1)
                chain.wait(v.tensor_tensor(IG[:, t, :], IG[:, t, :], XC[:, t, :], ALU.mult))
                chain.wait(v.tensor_tensor_scan(XC[:, t, :], RG[:, t, :], IG[:, t, :], 0.0, ALU.mult, ALU.add))
                dve.wait_ge(evacuated, TILE["ga"] + t + 1)
                v.tensor_tensor(GA[:, t, :], GA[:, t, :], XC[:, t, :], ALU.mult).then_inc(ya_done, 1)

            def lru_lo(t):
                dve.wait_ge(yah, t + 1)
                v.tensor_tensor(u_lo[:, R + t, :], GA[:, t, :], u_hi[:, R + t, :].bitcast(F32),
                                ALU.subtract).then_inc(yal, 1)

            lru_ix(0)
            for n in range(8):
                step("v", n)
                for t in {1: [0, 1], 3: [2, 3, 4], 5: [5, 6], 7: [7, 8, 9]}.get(n, []):
                    if t + 1 < R:
                        lru_ix(t + 1)
                    lru_gain(t)
            for n in range(2 * C):
                step("sa", n)
                if 3 <= n < 3 + R:
                    lru_scan(n - 3)
                if 5 <= n < 5 + R:
                    lru_lo(n - 5)

            def attention(H, first, s_shift, y_of_hi, y_of_lo, heads_out):
                for s in range(H + 2):
                    if s < H:
                        n, b = first + s, s % 2
                        dve.wait_ge(s_mm, n + 1)
                        src = bank[4 + b]
                        s_shift(s, b, src)
                        dve.wait_ge(s_evac, 2 * n + 2)
                        for j, (a, e) in enumerate([(0, P), (P, EXT)]):
                            v.tensor_reduce(stat_s[:, b, j:j + 1], att_s[:, b, a:e], AX.X, ALU.max).then_inc(mx_done, 1)
                        dve.wait_ge(mx_done, 2 * n + 2)
                        v.tensor_scalar(stat_s[:, b, 2:4], stat_s[:, b, 0:2], -1.0, None, ALU.mult).then_inc(negmax, 1)
                    if 1 <= s <= H:
                        n, b = first + s - 1, (s - 1) % 2
                        dve.wait_ge(exp_done, 2 * n + 2)
                        v.reciprocal(stat_s[:, b, 6:8], stat_s[:, b, 4:6]).then_inc(rsum_done, 1)
                        dve.wait_ge(rsum_done, n + 1)
                        for j, (a, e) in enumerate([(0, P), (P, EXT)]):
                            v.tensor_scalar(att_s[:, b, a:e], att_s[:, b, a:e], stat_s[:, b, 6 + j:7 + j], None,
                                            ALU.mult).then_inc(p_ready, 1)
                    if s >= 2 and (s - 2) % heads_out == heads_out - 1:
                        t = (s - 2) // heads_out
                        dve.wait_ge(y_hi, (C if first else 0) + t + 1)
                        v.tensor_tensor(y_of_lo(t), bank[7][:, 0:S], y_of_hi(t).bitcast(F32),
                                        ALU.subtract).then_inc(y_lo, 1)

            def fox_shift(s, b, src):
                if s == 0:
                    dve.wait_ge(cumt_ready, 1)
                for j, (a, e) in enumerate([(0, P), (P, EXT)]):
                    if s >= 2 and j == 0:
                        dve.wait_ge(pt_mm, s - 1)
                    v.scalar_tensor_tensor(out=att_s[:, b, a:e], in0=src[:, a:e], scalar=cum_t[:, j, s:s + 1],
                                           in1=mask[:, a:e], op0=ALU.add, op1=ALU.add).then_inc(s_evac, 1)

            dve.wait_ge(cst_in, 32)
            attention(H_FOX, 0, fox_shift, lambda t: u_hi[:, t, :], lambda t: u_lo[:, t, :], 2)
            for n in range(10):
                step("pa", n)
            for t in range(C):
                step("pb", t)
                dve.wait_ge(evacuated, TILE["pa"] + t + 1)
                v.tensor_tensor(PRA[:, t, :], PRA[:, t, :], SGA[:, t, :], ALU.mult).then_inc(merge_step, 1)
                dve.wait_ge(evacuated, TILE["pb"] + t + 1)
                v.tensor_tensor(PRB[:, t, :], PRB[:, t, :], SGB[:, t, :], ALU.mult).then_inc(merge_step, 1)
                dve.wait_ge(merge_step, 2 * t + 2)
                v.tensor_tensor(PRA[:, t, :], PRA[:, t, :], PRB[:, t, :], ALU.add).then_inc(merged, 1)
                if t >= 1:
                    dve.wait_ge(mh, t)
                    v.tensor_tensor(h_lo[:, t - 1, :], PRA[:, t - 1, :], h_hi[:, t - 1, :].bitcast(F32),
                                    ALU.subtract).then_inc(ml, 1)
            dve.wait_ge(mh, C)
            v.tensor_tensor(h_lo[:, C - 1, :], PRA[:, C - 1, :], h_hi[:, C - 1, :].bitcast(F32),
                            ALU.subtract).then_inc(ml, 1)
            for t in range(C):
                step("wo", t)
            dve.wait_ge(x_back, 16)
            add_normed("post", "mix_post", 0)
            make_h("ffn", "ffn_pre")

            with dve.Fori(0, 2 * F1 // 4) as i:
                for j in range(4):
                    lo(i, 4, PART["up"] + j + AHEAD)
                    dve.wait_ge(evacuated, lin(i, 4, TILE["up"] + j + 1))
                    v.scalar_tensor_tensor(out=YB[:, j, 1:S], in0=UB[:, j, 0:S - 1],
                                           scalar=dcol("fconv_w", i * 4 + (2 * F1 + j)), in1=YB[:, j, 1:S],
                                           op0=ALU.mult, op1=ALU.add).then_inc(tap_done, 1)
                    dve.wait_ge(tap_done, lin(i, 4, j + 1))
                    v.scalar_tensor_tensor(out=YB[:, j, 2:S], in0=UB[:, j, 0:S - 2],
                                           scalar=dcol("fconv_w", i * 4 + j), in1=YB[:, j, 2:S],
                                           op0=ALU.mult, op1=ALU.add).then_inc(taps_done, 1)

            def down(name):
                for j in range(24):
                    step(name, j)

            down("down")
            dve.wait_ge(evacuated, TILE["down"] + C)
            add_normed("post2", "ffn_post", 0)
            make_h("n0", "norm_mix", 0)

            for t in range(C):
                step("hf", t)
                dve.wait_ge(evacuated, TILE["hf"] + t + 1)
                v.tensor_scalar(FG[:, t, :], FG[:, t, :], der[:, D_1LB + t:D_1LB + t + 1],
                                der[:, D_LB + t:D_LB + t + 1], ALU.mult, ALU.add).then_inc(f_ready, 1)
                dve.wait_ge(f_ready, t + 1)
                v.tensor_scalar(KK[:, t, :], FG[:, t, :], -1.0, 1.0, ALU.mult, ALU.add).then_inc(k_ready, 1)
            for t in range(C):
                step("hq", t)
            v.memset(ONES_ROW, 1.0).then_inc(one_row, 1)
            v.memset(PD, 0.0).then_inc(pd_zero, 1)
            dve.wait_ge(one_row, 1)
            dve.wait_ge(logf_ready, 1)
            for n in range(8):
                step("hi", n)
                v.tensor_tensor_scan(CUM[:, n, :], ONES_ROW, CUM[:, n, :], 0.0, ALU.mult, ALU.add).then_inc(hcum_ready, 1)
            for t in range(C):
                step("hg", t)

            def halves(ap, l):
                w = ap.rearrange("p u t -> p (u t)").rearrange("p (n b) -> p n b", b=2 ** l)
                return w[:, :, 0:2 ** (l - 1)], w[:, :, 2 ** (l - 1):]

            def level_args(l):
                low, up = halves(CUM, l)
                elow, eup = halves(EB[l % 2], l)
                n, h = low.shape[1], low.shape[2]
                mid = low[:, :, h - 1:h].to_broadcast([P, n, h])
                if l >= 3:
                    dve.wait_ge(lev_mm, 4 * (l - 1))
                v.tensor_tensor(elow, mid, low, ALU.subtract).then_inc(arg_ready, 1)
                v.tensor_tensor(eup, up, mid, ALU.subtract).then_inc(arg_ready, 1)

            def level_keys(l):
                klow, _ = halves(KK, l)
                elow, _ = halves(EB[l % 2], l)
                dve.wait_ge(dec_ready, l)
                v.tensor_tensor(elow, elow, klow, ALU.mult).then_inc(x_low, 1)

            def take(l):
                for g in range(4):
                    dve.wait_ge(lev_mm, 4 * l + g + 1)
                    v.copy_predicated(PD[:, 4 * g:4 * g + 4, :], LM[:, l:l + 1, :].to_broadcast([P, 4, P]),
                                      bank[4 + g][:, :].rearrange("p (n t) -> p n t", n=4)).then_inc(lev_sel, 1)

            dve.wait_ge(hcum_ready, C)
            dve.wait_ge(lm_in, 16)
            dve.wait_ge(pd_zero, 1)
            level_args(1)
            for l in range(1, LEVELS + 1):
                if l < LEVELS:
                    level_args(l + 1)
                level_keys(l)
                take(l - 1)
            rstd("o")
            for c in range(C):
                v.scalar_tensor_tensor(out=OH[:, c, :], in0=OH[:, c, :], scalar=col("out_norm", c), in1=RSTD,
                                       op0=ALU.mult, op1=ALU.mult).then_inc(o_norm, 1)
            for c in range(C):
                dve.wait_ge(o_norm, c + 1)
                v.tensor_tensor(OH[:, c, :], OH[:, c, :], OG[:, c, :], ALU.mult).then_inc(o_gated, 1)
            for c in range(C):
                dve.wait_ge(mh, C + c + 1)
                v.tensor_tensor(h_lo[:, c, :], OH[:, c, :], h_hi[:, c, :].bitcast(F32), ALU.subtract).then_inc(ml, 1)

            def add_branch(name):
                for c in range(C):
                    dve.wait_ge(evacuated, TILE[name] + c + 1)
                    v.tensor_tensor(X[:, c, :], X[:, c, :], M[:, c, :], ALU.add).then_inc(x_ready, 1)

            def swiglu(name):
                with dve.Fori(0, 2 * F2 // 4) as i:
                    for j in range(4):
                        lo(i, 4, PART[name] + j + AHEAD)

            for t in range(C):
                step("ho", t)
            add_branch("ho")
            make_h("f0", "norm_ffn", 0)
            swiglu("up1")
            down("down1")
            add_branch("down1")
            make_h("n1", "norm_mix", C)
            for name in ("mq", "mk", "mv"):
                for t in range(C):
                    step(name, t)
            dve.wait_ge(bias_in, 32)
            v.tensor_tensor(BIAS, BIAS, mask[:, :].rearrange("p (o e) -> p o e", o=1).to_broadcast([P, H_MOBA, EXT]),
                            ALU.add).then_inc(bias_masked, 1)
            dve.wait_ge(bias_masked, 1)

            def moba_shift(s, b, src):
                for j, (a, e) in enumerate([(0, P), (P, EXT)]):
                    if j == 0:
                        dve.wait_ge(pt_mm, H_FOX + s - 1)
                    v.scalar_tensor_tensor(out=att_s[:, b, a:e], in0=src[:, a:e], scalar=DH_MOBA ** -0.5,
                                           in1=BIAS[:, s, a:e], op0=ALU.mult, op1=ALU.add).then_inc(s_evac, 1)

            attention(H_MOBA, H_FOX, moba_shift, lambda t: h_hi[:, t, :], lambda t: h_lo[:, t, :], 1)
            for t in range(C):
                step("mo", t)
            add_branch("mo")
            make_h("f1", "norm_ffn", C)
            swiglu("up2")
            down("down2")
            add_branch("down2")
            make_h("final", "final", 0, split=False)

        @block.gpsimd
        def _(pool):
            g = nc.gpsimd
            pool.dma_start(onehot, onehot_d).then_inc(tab_in, 16)
            pool.dma_start(table, table_d).then_inc(tab_in, 16)
            pool.dma_start(wf[:, :, :], wf_d).then_inc(wf_in, 16)
            pool.dma_start(ident[:, :], ident_d).then_inc(cst_in, 16)
            pool.dma_start(mask[:, :], mask_d).then_inc(cst_in, 16)
            pool.wait_ge(ext_ready, H_MOBA)
            pool.dma_start(bass.AP(tensor=scr, offset=0, ap=[[EXT, P], [P * EXT, H_MOBA], [1, EXT]]),
                           ext).then_inc(ext_out, 16)
            pool.wait_ge(merged, C)
            pool.dma_start(X, x_d).then_inc(x_back, 16)
            pool.wait_ge(merged, C)
            pool.dma_start(LM, lmask_d).then_inc(lm_in, 16)

            def products(n, i, pair, pairs0, f, wait_gate, wait_val):
                wait_gate()
                wait_val()
                g.tensor_tensor(PB[:, pair, :], GB[:, pair, :], YB[:, 2 * pair + 1, :], ALU.mult).then_inc(pair_free, 1)
                pool.wait_ge(pair_free, lin(i, 2, 2 + pairs0 + pair + 1))
                o = slice(None)
                dst_h, dst_l = u_hi[:, bass.ds(i * 2 + pair, 1), :], u_lo[:, bass.ds(i * 2 + pair, 1), :]
                g.tensor_copy(dst_h, PB[:, pair:pair + 1, :]).then_inc(uh_ready, 1)
                pool.wait_ge(uh_ready, lin(i, 2, pairs0 + pair + 1))
                g.tensor_tensor(dst_l, PB[:, pair:pair + 1, :], dst_h.bitcast(F32), ALU.subtract).then_inc(ul_ready, 1)

            g.memset(PB[:, 0, 0:1], 0.0).then_inc(pair_free, 1)
            g.memset(PB[:, 1, 0:1], 0.0).then_inc(pair_free, 1)
            with pool.Fori(0, F1 // 2) as i:
                for pair in range(2):
                    products(F1, i, pair, 0, None,
                             lambda: pool.wait_ge(gate_ready, lin(i, 2, pair + 1)),
                             lambda: pool.wait_ge(taps_done, lin(i, 4, R + 2 * pair + 2)))
            for l in range(1, LEVELS + 1):
                w = EB[l % 2].rearrange("p u t -> p (u t)").rearrange("p (n b) -> p n b", b=2 ** l)[:, :, 2 ** (l - 1):]
                q = QS.rearrange("p u t -> p (u t)").rearrange("p (n b) -> p n b", b=2 ** l)[:, :, 2 ** (l - 1):]
                pool.wait_ge(dec_ready, l)
                g.tensor_tensor(w, w, q, ALU.mult).then_inc(x_up, 1)

            def swiglu(name, pairs0):
                with pool.Fori(0, F2 // 2) as i:
                    for pair in range(2):
                        products(F2, i, pair, pairs0, None,
                                 lambda: pool.wait_ge(evacuated, lin(i, 4, TILE[name] + 2 * pair + 2)),
                                 lambda: None)

            swiglu("up1", F1)
            pool.wait_ge(ext_out, 16)
            for j, (a, e) in enumerate([(0, P), (P, EXT)]):
                pool.dma_start(BIAS[:, :, a:e], bass.AP(tensor=scr, offset=255 - P * j,
                               ap=[[EXT - 1, P], [P * EXT, H_MOBA], [1, e - a]])).then_inc(bias_in, 16)
            swiglu("up2", F1 + F2)

        @block.tensor
        def _(pe):
            mm = nc.tensor.matmul

            def three(out, slot, b, r_hi, r_lo, start, stop):
                s = slice(b * P, (b + 1) * P)
                mm(out, w_hi[:, slot, s], r_hi, start=start, stop=False)
                mm(out, w_hi[:, slot, s], r_lo, start=False, stop=False)
                return mm(out, w_lo[:, slot, s], r_hi, start=False, stop=stop)

            def free_bank(i, m, t):
                if t >= BANKS or not isinstance(i, int):
                    pe.wait_ge(evacuated, lin(i, m, t - BANKS + 1))

            def tile(i, c, t):
                pe.wait_ge(lo_ready, lin(i, 4, c + 1))
                free_bank(i, 4, t)
                for b in range(BLK):
                    last = three(bank[t % BANKS][:, 0:S], c % RING, b, h_hi[:, b, :], h_lo[:, b, :], b == 0, b == BLK - 1)
                last.then_inc(part_done, 1)

            def tiles(c, t, n):
                with pe.Fori(0, n // 4) as i:
                    for j in range(4):
                        tile(i, c + j, t + j)

            def token_tiles(c, t):
                for n in range(0, 8, 2):
                    s0 = (c + n) % RING
                    assert s0 % 2 == 0
                    for tok in range(2):
                        if tok == 0:
                            pe.wait_ge(lo_ready, c + n + 2)
                        free_bank(0, 0, t + n + tok)
                        out = bank[(t + n + tok) % BANKS][:, 0:S].rearrange("p (z f) -> p z f", z=2)
                        ts = slice(tok * P, (tok + 1) * P)
                        for b in range(BLK):
                            f = slice(b * P, (b + 1) * P)
                            mm(out, h_hi[:, b, ts], w_hi[:, s0:s0 + 2, f], start=(b == 0), stop=False)
                            mm(out, h_lo[:, b, ts], w_hi[:, s0:s0 + 2, f], start=False, stop=False)
                            last = mm(out, h_hi[:, b, ts], w_lo[:, s0:s0 + 2, f], start=False, stop=(b == BLK - 1))
                    last.then_inc(part_done, 2)

            def down(name, KT):
                def body(c0):
                    for j in range(12):
                        c, t = PART[name] + c0 + j, TILE[name] + (c0 + j) // 3
                        pe.wait_ge(lo_ready, c + 1)
                        if j % 3 == 0:
                            free_bank(0, 0, t)
                        for b in range(min(BLK, KT - BLK * (j % 3))):
                            k = BLK * (j % 3) + b
                            last = three(bank[t % BANKS][:, 0:S], c % RING, b, u_hi[:, k, :], u_lo[:, k, :],
                                         k == 0, k == KT - 1)
                        last.then_inc(part_done, 1)
                body(0)
                body(12)

            def stat(norm):
                n = NORMS[norm]
                for c in range(C):
                    pe.wait_ge(sq_ready, 8 * n + c + 1)
                    last = mm(bank[4][:, 0:S], ones[:, :], SQ[:, c, :], start=(c == 0), stop=(c == C - 1))
                last.then_inc(stat_done, 1)

            def attention(H, first, scores, pv, heads_out):
                for s in range(H + 2):
                    if s < H:
                        n = first + s
                        if n >= 2:
                            pe.wait_ge(s_evac, 2 * n - 2)
                        scores(s, bank[4 + s % 2]).then_inc(s_mm, 1)
                    if 1 <= s <= H:
                        n, b = first + s - 1, (s - 1) % 2
                        pe.wait_ge(p_ready, 2 * n + 2)
                        if n >= 1:
                            pe.wait_ge(pt_copied, n)
                        for j in range(3):
                            last = nc.tensor.transpose(bank[6][:, j * P:(j + 1) * P],
                                                       att_s[:, b, (0, P, 2 * P)[j]:(P, 2 * P, 3 * P)[j]], ident[:, :])
                        last.then_inc(pt_mm, 1)
                    if s >= 2:
                        n, b = first + s - 2, s % 2
                        pe.wait_ge(pt_copied, n + 1)
                        t = (s - 2) // heads_out + (C if first else 0)
                        if t >= 1:
                            pe.wait_ge(y_lo, t)
                        pv(s - 2, att_pt[:, b, :]).then_inc(pv_mm, 1)

            pe.wait_ge(ones_ready, 1)
            stat("mix")
            pe.wait_ge(tab_in, 32)
            for h in range(H_MOBA):
                if h >= 2:
                    pe.wait_ge(ext_ready, h - 1)
                mm(bank[5 + h % 2][:, 0:EXT], table[:, h:h + 1].to_broadcast([BUCKETS, P]), onehot, start=True,
                   stop=True).then_inc(ext_mm, 1)
            pe.wait_ge(wf_in, 16)
            for c in range(C):
                pe.wait_ge(ht_ready, c + 1)
                last = mm(bank[7][0:H_FOX, 0:S], wf[:, c, :], HT[:, c, :], start=(c == 0), stop=(c == C - 1))
            last.then_inc(f_mm, 1)
            pe.wait_ge(hl_ready, C)
            for c in range(4):
                tile(0, c, c)
            pe.wait_ge(cum_ready, 1)
            pe.wait_ge(cst_in, 32)
            pe.wait_ge(ext_ready, H_MOBA)
            for b in range(2):
                last = nc.tensor.transpose(bank[5][:, b * H_FOX:(b + 1) * H_FOX], ncum[:, b * P:(b + 1) * P],
                                           ident[0:H_FOX, 0:H_FOX])
            last.then_inc(cumt_mm, 1)
            tiles(4, 4, 32)
            pe.wait_ge(xcl_ready, R)
            pe.wait_ge(cumt_ready, 1)
            for n in range(8):
                c, g = PART["gates"] + n, n // 2 % 2
                pe.wait_ge(lo_ready, c + 1)
                if n >= 2:
                    pe.wait_ge(gates_evac, 5 * (n // 2) - (2 if n % 2 == 0 else 0))
                b = 0
                for j, o in enumerate(GATE_PARTS[n % 2]):
                    out = bank[4 + 2 * (n % 2) + j // 2][:, j % 2 * S:j % 2 * S + S]
                    for k, f in enumerate(GATE_IN[o]):
                        last = three(out, c % RING, b, u_hi[:, 5 * g + f, :], u_lo[:, 5 * g + f, :], k == 0,
                                     k == len(GATE_IN[o]) - 1)
                        b += 1
                last.then_inc(part_done, 1)
            token_tiles(PART["v"], TILE["v"])
            tiles(PART["sa"], TILE["sa"], 2 * C)

            def fox_scores(h, out):
                t, o = h // 2, h % 2 * DH_FOX
                sel = ident[0:H_FOX, h:h + 1].to_broadcast([H_FOX, P])
                for a, e, qb in ((0, P, 0), (P, EXT, 1)):
                    mm(out[:, a:e], Q[o:o + DH_FOX, t, qb * P:(qb + 1) * P], K[o:o + DH_FOX, t, 0:e - a],
                       start=True, stop=False)
                    last = mm(out[:, a:e], sel, ncum[:, 0:e - a], start=False, stop=True)
                return last

            def fox_pv(h, pt):
                o = h % 2 * DH_FOX
                out = bank[7][o:o + DH_FOX, 0:S]

                def vt(kb):
                    return V[:, 4 * kb:4 * kb + 4, :].rearrange("p u f -> p (u f)")[:, h * DH_FOX:(h + 1) * DH_FOX]
                mm(out[:, 0:P], vt(0), pt[:, 0:P], start=True, stop=True)
                mm(out[:, P:S], vt(0), pt[:, P:2 * P], start=True, stop=False)
                return mm(out[:, P:S], vt(1), pt[:, 2 * P:EXT], start=False, stop=True)

            pe.wait_ge(gates_evac, 4 * 5)
            pe.wait_ge(evacuated, TILE["v"] + 8)
            attention(H_FOX, 0, fox_scores, fox_pv, 2)
            pe.wait_ge(yal, R)
            for t in range(C):
                for k in range(R):
                    n, b = divmod(R * t + k, BLK)
                    if b == 0:
                        pe.wait_ge(lo_ready, PART["pa"] + n + 1)
                    if k == 0:
                        free_bank(0, 0, TILE["pa"] + t)
                    last = three(bank[(TILE["pa"] + t) % BANKS][:, 0:S], (PART["pa"] + n) % RING, b, u_hi[:, R + k, :],
                                 u_lo[:, R + k, :], k == 0, k == R - 1)
                    if b == BLK - 1:
                        last.then_inc(part_done, 1)
            pe.wait_ge(y_lo, C)
            for t in range(C):
                c = PART["pb"] + t
                pe.wait_ge(lo_ready, c + 1)
                free_bank(0, 0, TILE["pb"] + t)
                for b in range(BLK):
                    last = three(bank[(TILE["pb"] + t) % BANKS][:, 0:S], c % RING, b, u_hi[:, b, :], u_lo[:, b, :],
                                 b == 0, b == BLK - 1)
                last.then_inc(part_done, 1)
            pe.wait_ge(ml, C)
            for t in range(C):
                tile(0, PART["wo"] + t, TILE["wo"] + t)
            stat("post")
            stat("ffn")
            pe.wait_ge(hl_ready, H_COUNT["ffn"] + C)
            tiles(PART["up"], TILE["up"], 2 * F1)
            pe.wait_ge(ul_ready, F1)
            down("down", F1)
            stat("post2")
            stat("n0")
            pe.wait_ge(hl_ready, H_COUNT["n0"] + C)
            tiles(PART["hf"], TILE["hf"], 2 * C)
            token_tiles(PART["hi"], TILE["hi"])
            tiles(PART["hg"], TILE["hg"], C)

            def level_mm(l):
                for g in range(4):
                    if l >= 1:
                        pe.wait_ge(lev_sel, 4 * (l - 1) + g + 1)
                    for j in range(4):
                        c, tok = (4 * g + j) // 2, slice(j % 2 * P, (j % 2 + 1) * P)
                        a, b = (KK, QS) if l == 0 else (EB[l % 2], EB[l % 2])
                        last = mm(bank[4 + g][:, j * P:(j + 1) * P], a[:, c, tok], b[:, c, tok], start=True, stop=True)
                    last.then_inc(lev_mm, 1)

            pe.wait_ge(k_ready, C)
            pe.wait_ge(evacuated, TILE["hq"] + C)
            level_mm(0)
            for l in range(1, LEVELS):
                pe.wait_ge(x_low, l)
                pe.wait_ge(x_up, l)
                level_mm(l)
            pe.wait_ge(x_low, LEVELS)
            pe.wait_ge(x_up, LEVELS)
            for g in range(2):
                pe.wait_ge(lev_sel, 4 * (LEVELS - 1) + g + 1)
                for j in range(4):
                    c = 4 * g + j
                    last = mm(bank[4 + g][:, j * P:(j + 1) * P], EB[0][:, c, 0:P], EB[0][:, c, P:S], start=True, stop=True)
                last.then_inc(lev_mm, 1)
            pe.wait_ge(lev_sel, 4 * LEVELS)
            pe.wait_ge(px_copied, 2)
            pe.wait_ge(evacuated, TILE["hi"] + 8)
            for c in range(C):
                out = bank[5 + c % 3]
                if c >= 3:
                    pe.wait_ge(o_evac, c - 2)

                def it(tok):
                    return INP[:, 4 * tok:4 * tok + 4, :].rearrange("p u f -> p (u f)")[:, c * P:(c + 1) * P]
                mm(out[:, 0:P], it(0), PD[:, 2 * c, :], start=True, stop=True)
                mm(out[:, P:S], it(0), PX[:, c, :], start=True, stop=False)
                mm(out[:, P:S], it(1), PD[:, 2 * c + 1, :], start=False, stop=True).then_inc(o_mm, 1)
            stat("o")
            pe.wait_ge(ml, 2 * C)
            tiles(PART["ho"], TILE["ho"], C)
            stat("f0")
            pe.wait_ge(hl_ready, H_COUNT["f0"] + C)
            tiles(PART["up1"], TILE["up1"], 2 * F2)
            pe.wait_ge(ul_ready, F1 + F2)
            down("down1", F2)
            stat("n1")
            pe.wait_ge(hl_ready, H_COUNT["n1"] + C)
            tiles(PART["mq"], TILE["mq"], 2 * C)
            token_tiles(PART["mv"], TILE["mv"])

            def moba_scores(h, out):
                mm(out[:, 0:P], MQ[:, h, 0:P], MK[:, h, 0:P], start=True, stop=True)
                return mm(out[:, P:EXT], MQ[:, h, P:S], MK[:, h, :], start=True, stop=True)

            def moba_pv(h, pt):
                out = bank[7][:, 0:S]

                def vt(kb):
                    return MV[:, 4 * kb:4 * kb + 4, :].rearrange("p u f -> p (u f)")[:, h * P:(h + 1) * P]
                mm(out[:, 0:P], vt(0), pt[:, 0:P], start=True, stop=True)
                mm(out[:, P:S], vt(0), pt[:, P:2 * P], start=True, stop=False)
                return mm(out[:, P:S], vt(1), pt[:, 2 * P:EXT], start=False, stop=True)

            pe.wait_ge(evacuated, TILE["mv"] + 8)
            attention(H_MOBA, H_FOX, moba_scores, moba_pv, 1)
            pe.wait_ge(y_lo, 2 * C)
            tiles(PART["mo"], TILE["mo"], C)
            stat("f1")
            pe.wait_ge(hl_ready, H_COUNT["f1"] + C)
            tiles(PART["up2"], TILE["up2"], 2 * F2)
            pe.wait_ge(ul_ready, F1 + 2 * F2)
            down("down2", F2)
            stat("final")


def bucket_of(dist):
    import math
    import numpy as np
    exact = BUCKETS // 2
    n = np.maximum(dist, 0)
    nf = np.maximum(n, exact).astype(np.float32)
    large = exact + (np.log(nf / np.float32(exact)) / np.float32(math.log(1024 / exact))
                     * np.float32(BUCKETS - exact)).astype(np.int32)
    return np.where(n < exact, n, np.minimum(large, BUCKETS - 1))


def kernel(**inputs):
    import numpy as np
    import concourse.bacc as bacc
    from concourse.bass_utils import run_bass_kernel_spmd

    a = {k: np.asarray(x) for k, x in inputs.items()}

    def parts_of(w):
        k, n = w.shape
        per = -(-k // (BLK * P))
        out = np.zeros((n // P, per, P, BLK, P), np.float32)
        for j in range(per):
            rows = w[j * BLK * P:(j + 1) * BLK * P]
            kb = rows.shape[0] // P
            out[:, j, :, :kb, :] = rows.reshape(kb, P, n // P, P).transpose(2, 1, 0, 3)
        return out.reshape(-1, P, BLK * P)

    def packed(w):
        k, n = w.shape
        b = w.reshape(k // P, P, n // P, P).transpose(2, 0, 1, 3).reshape(-1, BLK, P, P)
        return b.transpose(0, 2, 1, 3).reshape(-1, P, BLK * P)

    def gate_parts(w):
        out = np.zeros((2, 2, P, BLK, P), np.float32)
        for g in range(2):
            dense = np.zeros((5 * P, 5 * P), np.float32)
            for h in range(8):
                s = slice(h * RNN_BLOCK, (h + 1) * RNN_BLOCK)
                dense[s, s] = w[8 * g + h]
            for n, tiles in enumerate(GATE_PARTS):
                blocks = [(f, o) for o in tiles for f in GATE_IN[o]]
                for b, (f, o) in enumerate(blocks):
                    out[g, n, :, b, :] = dense[f * P:(f + 1) * P, o * P:(o + 1) * P]
        return out.reshape(4, P, BLK * P)

    def paired(w):
        k, n = w.shape
        return w.reshape(k, 2, n // (2 * P), P).transpose(0, 2, 1, 3).reshape(k, n)

    w_in = a["w_in"][0]
    o = np.cumsum([0, D_RNN, D_RNN, D, D, D, H_FOX, D, D])
    xa, ga, q, k, v, f, sa, sb_ = (w_in[:, o[i]:o[i + 1]] for i in range(8))
    hq, hf, hi_, hg = (a["hgrn_w_in_2"][0][:, i * D:(i + 1) * D] for i in range(4))
    mq, mk, mv = (a["moba_w_in_2"][0][:, i * D:(i + 1) * D] for i in range(3))
    stream = np.concatenate([
        parts_of(xa), parts_of(ga), parts_of(q), parts_of(k), gate_parts(a["w_rg_x"][0]), gate_parts(a["w_rg_a"][0]),
        parts_of(v), parts_of(sa), parts_of(sb_), packed(a["w_proj_a"][0]), parts_of(a["w_proj_b"][0]),
        parts_of(a["w_out"][0]), parts_of(paired(a["w_up"][0])), parts_of(a["w_down"][0]),
        parts_of(hf), parts_of(hq), parts_of(hi_), parts_of(hg), parts_of(a["hgrn_w_out_2"][0]),
        parts_of(paired(a["ffn_w13_2"][0])), parts_of(a["ffn_w2_2"][0]),
        parts_of(mq), parts_of(mk), parts_of(mv), parts_of(a["moba_w_out_2"][0]),
        parts_of(paired(a["ffn_w13_2"][1])), parts_of(a["ffn_w2_2"][1])])
    assert stream.shape[0] == PARTS

    def cols(x):
        return x.reshape(-1, P).T

    pad = np.zeros(P, np.float32)
    pad[:H_FOX] = a["b_forget"][0]
    par = np.concatenate([
        cols(a["mix_norm_pre"][0]), cols(a["mix_norm_post"][0]), cols(a["conv_a_w"][0]), cols(a["conv_a_b"][0]),
        cols(a["b_rg_a"][0]), cols(a["b_rg_x"][0]), cols(a["lru_lambda"][0]), cols(a["b_merge"][0]),
        cols(a["ffn_norm_pre"][0]), cols(a["ffn_norm_post"][0]), cols(paired(a["conv_f_w"][0])),
        cols(paired(a["conv_f_b"])), cols(a["norm_mix_2"]), cols(a["norm_ffn_2"]), cols(a["hgrn_lb_logits_2"]),
        cols(a["hgrn_out_norm_2"][0]), cols(a["final_norm_2"]), pad[:, None]], axis=1)
    par = np.ascontiguousarray(par)
    assert par.shape == (P, NCOL)

    x_t = np.ascontiguousarray(a["x"][0].T.reshape(C, P, S).transpose(1, 0, 2))
    wf = np.ascontiguousarray(f.reshape(C, P, H_FOX).transpose(1, 0, 2))

    onehot = (np.arange(BUCKETS)[:, None] == bucket_of(255 - np.arange(EXT))[None, :]).astype(np.float32)
    ident = np.eye(P, dtype=np.float32)
    causal = np.where(np.arange(P)[None, :] <= np.arange(P)[:, None], 0.0, NEG).astype(np.float32)
    mask = np.concatenate([causal, np.zeros((P, P), np.float32), causal], axis=1)
    s, t = np.arange(P)[:, None], np.arange(P)[None, :]
    lmask = np.stack([s == t] + [(s >> l == t >> l) & (s >> (l - 1) != t >> (l - 1)) & (s < t)
                                 for l in range(1, LEVELS)], axis=1).astype(np.int32)

    arrays = {"stream": stream, "par": par, "x_t": x_t, "wf": wf,
              "table": np.ascontiguousarray(a["rel_bias_table_2"]), "onehot": onehot, "ident": ident,
              "mask": mask, "lmask": np.ascontiguousarray(lmask)}
    nc = bacc.Bacc("TRN2", target_bir_lowering=False, num_devices=1)
    aps = [nc.dram_tensor("in_" + n, x.shape, mybir.dt.from_np(x.dtype), kind="ExternalInput").ap() for n, x in arrays.items()]
    out = nc.dram_tensor("out", (P, C, S), F32, kind="ExternalOutput").ap()
    build(nc, *aps, out)
    r = run_bass_kernel_spmd(nc, [{"in_" + n: x for n, x in arrays.items()}], core_ids=[0])
    y = r.results[0]["out"]
    return np.ascontiguousarray(y.transpose(2, 1, 0).reshape(1, S, D))
```

```python
from contextlib import ExitStack

import concourse.bass as bass
from concourse import mybir

F32 = mybir.dt.float32
F32R = mybir.dt.float32r
I32 = mybir.dt.int32
ACT = mybir.ActivationFunctionType
ALU = mybir.AluOpType
AX = mybir.AxisListType

P = 128
S = 256
D = 1024
C = D // P
D_RNN = 1280
R = D_RNN // P
RNN_BLOCK = 80
H_FOX, DH_FOX = 16, 64
H_MOBA, DH_MOBA = 8, 128
BUCKETS = 32
F1 = 3 * D // P
F2 = 2816 // P
EPS = 1e-6
LRU_C = 8.0
NEG = -1.0e30
BLK = 8
RING = 4
BANKS = 4
HI_AHEAD, LO_AHEAD = 4, 3

PHASES = [("xa", R, R), ("v", C, C), ("gates", 8, 0), ("ga", R, R), ("qk", 2 * C, 2 * C), ("sa", C, C), ("sb", C, C),
          ("pa", R, C), ("pb", C, C), ("wo", C, C), ("up", 2 * F1, 2 * F1), ("down", F1, C),
          ("hf", C, C), ("hq", C, C), ("hi", C, C), ("hg", C, C), ("ho", C, C),
          ("up1", 2 * F2, 2 * F2), ("down1", 24, C), ("mv", C, C), ("mqk", 2 * C, 2 * C), ("mo", C, C),
          ("up2", 2 * F2, 2 * F2), ("down2", 24, C)]
PART, TILE = {}, {}
_p = _t = 0
for _name, _parts, _tiles in PHASES:
    PART[_name], TILE[_name] = _p, _t
    _p, _t = _p + _parts, _t + _tiles
PARTS, TILES = _p, _t

GATE_IN = [[0, 1], [0, 1, 2], [1, 2, 3], [2, 3, 4], [3, 4]]
GATE_PARTS = [[0, 1, 2], [3, 4]]

COLS, NCOL = {}, 0
for _name, _n in [("mix_pre", C), ("mix_post", C), ("conv_w", 4 * R), ("conv_b", R), ("b_a", R), ("b_x", R),
                  ("lam", R), ("b_merge", 2 * C), ("ffn_pre", C), ("ffn_post", C), ("fconv_w", 3 * 2 * F1),
                  ("fconv_b", 2 * F1), ("norm_mix", 2 * C), ("norm_ffn", 2 * C), ("lb", 2 * C), ("out_norm", C),
                  ("final", C), ("b_forget", 1)]:
    COLS[_name] = NCOL
    NCOL += _n

EXT = 3 * P
LEVELS = 8

UNITS = 82


def build(nc, stream, par_d, x_d, wf_d, table_d, onehot_d, ident_d, mask_d, lmask_d, out_d):
    scr = nc.dram_tensor("bias_rows", [H_MOBA, P, EXT], F32, kind="Internal")
    with ExitStack() as ctx:
        def sb(name, shape, dt=F32):
            return ctx.enter_context(nc.sbuf_tensor(name, shape, dt))

        def sem(name):
            return ctx.enter_context(nc.semaphore(name))

        raw = sb("raw", [P, RING, BLK * P])
        w_hi = sb("w_hi", [P, RING, BLK * P], F32R)
        w_lo = sb("w_lo", [P, RING, BLK * P], F32R)
        h_hi = sb("h_hi", [P, C, S], F32R)
        h_lo = sb("h_lo", [P, C, S], F32R)
        u_hi = sb("u_hi", [P, F1, S], F32R)
        u_lo = sb("u_lo", [P, F1, S], F32R)
        F = sb("work", [P, UNITS, S])
        par = sb("par", [P, NCOL])
        der = sb("derived", [P, 64])
        ident = sb("ident", [P, P])
        mask = sb("mask", [P, EXT])
        ones = sb("ones", [P, P])
        wf = sb("wf", [P, C, H_FOX])
        att_s = sb("att_s", [P, 2, EXT])
        att_pt = sb("att_pt", [P, 2, EXT])
        stat_s = sb("att_stat", [P, 2, 8])
        ncum = sb("ncum", [H_FOX, S])
        cum_t = sb("cum_t", [P, 2, H_FOX])
        bank = [ctx.enter_context(nc.psum_tensor(f"bank{i}", [P, 512], F32)) for i in range(8)]

        def flat(ap):
            return ap.rearrange("p u t -> p (u t)")

        X = F[:, 52:60, :]
        RSTD, SQT, ACC = F[:, 81, :], F[:, 60, :], F[:, 61, :]
        M = F[:, 12:20, :]
        HT, SQ = F[:, 20:28, :], F[:, 60:68, :]
        ext = flat(F[:, 60:72, :]).rearrange("p (h e) -> p h e", h=H_MOBA)
        onehot = flat(F[0:BUCKETS, 44:46, :])[:, 0:EXT]
        table = F[0:BUCKETS, 46, 0:H_MOBA]
        XA, GA, XC = F[:, 0:10, :], F[:, 0:10, :], F[:, 10:20, :]
        Q, K, V = F[:, 20:28, :], F[:, 28:36, :], F[:, 36:44, :]
        SGA, SGB = F[:, 44:52, :], F[:, 52:60, :]
        RG, IG, DEN = F[:, 60:70, :], F[:, 70:80, :], F[:, 48:50, :]
        PRA, PRB = F[:, 70:78, :], F[:, 0:8, :]
        UB, YB, GB, PB, GR = F[:, 0:4, :], F[:, 4:8, :], F[:, 8:10, :], F[:, 10:12, :], F[:, 0:2, :]
        FG, CUM, KK, QS = F[:, 0:8, :], F[:, 8:16, :], F[:, 16:24, :], F[:, 24:32, :]
        INP, OG = F[:, 32:40, :], F[:, 40:48, :]
        LM = flat(F[:, 48:52, :]).bitcast(I32).rearrange("p (l t) -> p l t", l=LEVELS)
        EB = [F[:, 0:8, :], F[:, 60:68, :]]
        PD = F[:, 68:76, :].rearrange("p u (z t) -> p (u z) t", z=2)
        PX = F[:, 76:80, :].rearrange("p u (z t) -> p (u z) t", z=2)
        ONES_ROW = F[:, 80, :]
        OC, OH = F[:, 8:16, :], F[:, 16:24, :]
        MQ, MK, MV = F[:, 0:8, :], F[:, 8:16, :], F[:, 32:40, :]
        BIAS = flat(F[:, 68:80, :]).rearrange("p (h e) -> p h e", h=H_MOBA)

        def col(name, c=0):
            return par[:, COLS[name] + c:COLS[name] + c + 1]

        def dcol(name, e):
            return par[:, bass.ds(e + COLS[name], 1)]

        D_SP, D_NSP, D_LB, D_1LB, D_T, D_E, D_EPS = 0, 10, 20, 28, 36, 46, 63
        touch = der[:, 62:63]
        RCOL = der[:, 36:38]

        landed = [sem(f"part_landed{i}") for i in range(RING)]
        hi_ready, lo_ready = sem("hi_ready"), sem("lo_ready")
        part_done, evacuated = sem("part_done"), sem("evacuated")
        par_in, x_in, wf_in, tab_in, cst_in, x_back, lm_in, bias_in = (
            sem(n) for n in ("par_in", "x_in", "wf_in", "table_in", "const_in", "x_back", "lmask_in", "bias_in"))
        ext_out, out_done = sem("bias_rows_out"), sem("out_done")
        ones_ready = sem("ones_ready")
        sq_ready, stat_done, rms_ready, rstd_ready = (
            sem(n) for n in ("square_ready", "stat_done", "rms_ready", "rstd_ready"))
        ht_ready, hh_ready, hl_ready, x_ready = sem("h_ready"), sem("h_hi_ready"), sem("h_lo_ready"), sem("x_ready")
        post_t, post_pool = sem("post_scaled"), sem("post_scaled_by_pool")
        ext_mm, ext_ready = sem("bias_rows_made"), sem("bias_rows_ready")
        act_step, dve_step, pool_step = sem("act_step"), sem("dve_step"), sem("pool_step")
        der_ready, sp_ln, lb_exp = sem("derived_ready"), sem("softplus_ln"), sem("lb_exp")
        f_mm, f_ln, cum_ready, cumt_mm, cumt_ready = (
            sem(n) for n in ("f_mm", "f_ln", "cum_ready", "cum_t_mm", "cum_t_ready"))
        tap_done, taps_done, xch_ready, xcl_ready = (
            sem(n) for n in ("tap_done", "taps_done", "xc_hi_ready", "xc_lo_ready"))
        gates_evac, ix_done, tanh_done, decay_done, gain_done, root_done, scan_done, ya_done, yah, yal = (
            sem(n) for n in ("gates_evac", "ix_done", "tanh_done", "decay_done", "gain_done", "root_done",
                             "scan_done", "ya_done", "ya_hi_ready", "ya_lo_ready"))
        s_mm, s_evac, mx_done, negmax, exp_done, rsum_done, p_ready, pt_mm, pt_copied, pv_mm, y_hi, y_lo = (
            sem(n) for n in ("scores_mm", "scores_evac", "max_done", "negmax_ready", "exp_done", "rsum_ready",
                             "probs_ready", "probs_t_mm", "probs_t_copied", "pv_mm", "y_hi_ready", "y_lo_ready"))
        merge_step, merged, mh, ml = sem("merge_step"), sem("merged"), sem("merged_hi"), sem("merged_lo")
        pair_free, gate_ready, prod_done, uh_ready, ul_ready = (
            sem(n) for n in ("pair_free", "gate_ready", "product_done", "u_hi_ready", "u_lo_ready"))
        f_ready, k_ready, logf_ready, hcum_ready = sem("f_ready"), sem("k_ready"), sem("logf_ready"), sem("hcum_ready")
        pd_zero, one_row = sem("pd_zeroed"), sem("ones_row_ready")
        arg_ready, dec_ready, x_low, x_up, lev_mm, lev_sel, px_copied = (
            sem(n) for n in ("level_arg", "level_decay", "level_keys", "level_queries", "level_mm", "level_taken",
                             "cross_copied"))
        o_mm, o_evac, o_norm, o_gated = sem("o_mm"), sem("o_evac"), sem("o_normed"), sem("o_gated")
        bias_masked = sem("bias_masked")
        acc_ready, sq_step, col_rms, col_ready = sem("squares_summed"), sem("square_step"), sem("column_rms"), sem("column_rstd")
        u_conv, f_raw, q_ready, og_ready = sem("conv_tap_ready"), sem("forget_sigmoid"), sem("q_ready"), sem("og_ready")
        oh_hi, oh_lo = sem("o_hi_ready"), sem("o_lo_ready")
        den_ready, recip_done, b_done, gelu_done = (
            sem(n) for n in ("one_plus_s_ready", "one_plus_s_inverted", "b_done", "gelu_done"))

        block = ctx.enter_context(nc.Block())

        def lin(i, m, c):
            return c if isinstance(i, int) else i * m + c

        class Chain:

            def __init__(self, eng, s):
                self.eng, self.s, self.n = eng, s, 0

            def wait(self, ins):
                ins.then_inc(self.s, 1)
                self.n += 1
                self.eng.wait_ge(self.s, self.n)

        NORMS = {n: i for i, n in enumerate(["mix", "post", "ffn", "post2", "n0", "o", "f0", "n1", "f1", "final"])}
        X_SRC = {"ffn": (x_ready, 0), "n0": (x_ready, C), "f0": (x_ready, 2 * C), "n1": (evacuated, TILE["down1"]),
                 "f1": (evacuated, TILE["mo"]), "final": (evacuated, TILE["down2"])}
        POOL_SUMS = ["post", "post2", "o", "f0", "n1", "f1", "final"]
        NEXT = {"ffn": "ffn_pre", "n0": "norm_mix", "f0": "norm_ffn", "n1": "norm_mix", "f1": "norm_ffn"}
        GAIN0 = {"ffn": 0, "n0": 0, "f0": 0, "n1": C, "f1": C}
        H_COUNT = {n: 8 * i for i, n in enumerate(["mix", "ffn", "n0", "f0", "n1", "f1"])}

        @block.sync
        def _(sp):
            sp.dma_start(X, x_d).then_inc(x_in, 16)
            sp.dma_start(par[:, :], par_d).then_inc(par_in, 16)
            for n in range(RING):
                sp.dma_start(raw[:, n, :], stream[n]).then_inc(landed[n], 16)
            loops = (PARTS - RING) // RING

            def load(i, c):
                sp.wait_ge(lo_ready, lin(i, RING, c) - RING + 1)
                src = (stream[bass.ds(lin(i, RING, c), 1), :, :].rearrange("o p f -> p (o f)")
                       if not isinstance(i, int) else stream[c])
                sp.dma_start(raw[:, c % RING, :], src).then_inc(landed[c % RING], 16)

            with sp.Fori(1, 1 + loops) as i:
                for c in range(RING):
                    load(i, c)
            for c in range(RING * (1 + loops), PARTS):
                load(0, c)

        @block.scalar
        def _(act):
            A = nc.scalar.activation
            chain = Chain(act, act_step)

            def hi(i, m, c):
                if isinstance(i, int) and c >= PARTS:
                    return
                slot = c % RING
                act.wait_ge(landed[slot], lin(i, 16 * m // RING, 16 * (c // RING + 1)))
                A(w_hi[:, slot, :], raw[:, slot, :], ACT.Copy).then_inc(hi_ready, 1)

            def multiplied(c, i=0, m=0):
                act.wait_ge(part_done, lin(i, m, c + 1))

            def out_of(t):
                return bank[t % BANKS][:, 0:S]

            def rms(norm, columns=False):
                act.wait_ge(stat_done, NORMS[norm] + 1)
                A(RSTD, bank[4][:, 0:S], ACT.Sqrt, scale=1.0 / D, bias=der[:, D_EPS:D_EPS + 1]).then_inc(rms_ready, 1)
                if columns:
                    A(RCOL, bank[4][:, S:S + 2], ACT.Sqrt, scale=1.0 / D, bias=der[:, D_EPS:D_EPS + 1]).then_inc(col_rms, 1)

            def split(norm, c):
                s, n = X_SRC[norm]
                act.wait_ge(s, n + c + 1)
                A(h_hi[:, c, :], X[:, c, :], ACT.Copy, scale=col(NEXT[norm], GAIN0[norm] + c)).then_inc(hh_ready, 1)
                if norm in ("ffn", "n0"):
                    A(SQ[:, c, :], X[:, c, :], ACT.Square).then_inc(sq_ready, 1)

            act.wait_ge(x_in, 16)
            for c in range(C):
                A(SQ[:, c, :], X[:, c, :], ACT.Square).then_inc(sq_ready, 1)
            for n in range(HI_AHEAD - 1):
                hi(0, 0, n)
            act.wait_ge(der_ready, 1)
            rms("mix")
            for c in range(C):
                act.wait_ge(ht_ready, c + 1)
                A(h_hi[:, c, :], HT[:, c, :], ACT.Copy).then_inc(hh_ready, 1)
            hi(0, 0, HI_AHEAD - 1)
            for t in range(R):
                multiplied(PART["xa"] + t)
                A(XA[:, t, :], out_of(TILE["xa"] + t), ACT.Copy)
                A(XC[:, t, :], out_of(TILE["xa"] + t), ACT.Identity, scale=col("conv_w", 3 * R + t),
                  bias=col("conv_b", t)).then_inc(evacuated, 1)
                hi(0, 0, PART["xa"] + t + HI_AHEAD)
                if 1 <= t <= H_MOBA:
                    act.wait_ge(ext_mm, t)
                    A(ext[:, t - 1, :], bank[5 + (t - 1) % 2][:, 0:EXT], ACT.Copy).then_inc(ext_ready, 1)
                if t >= 1:
                    act.wait_ge(taps_done, t)
                    A(u_hi[:, t - 1, :], XC[:, t - 1, :], ACT.Copy).then_inc(xch_ready, 1)
            act.wait_ge(taps_done, R)
            A(u_hi[:, R - 1, :], XC[:, R - 1, :], ACT.Copy).then_inc(xch_ready, 1)

            def parameters():
                lam = par[:, COLS["lam"]:COLS["lam"] + R]
                act.wait_ge(par_in, 16)
                chain.wait(A(der[:, D_T:D_T + R], lam, ACT.Abs))
                chain.wait(A(der[:, D_T:D_T + R], der[:, D_T:D_T + R], ACT.Exp, scale=-1.0))
                act.wait_ge(der_ready, 3)
                for r in range(2):
                    e = der[:, D_E + C * r:D_E + C * r + C]
                    A(e, e, ACT.Exp).then_inc(lb_exp, 1)
                A(der[:, D_SP:D_SP + R], der[:, D_T:D_T + R], ACT.Ln, bias=1.0).then_inc(sp_ln, 1)

            def forget_logits():
                act.wait_ge(f_mm, 1)
                z, az = att_s[0:H_FOX, 0, 0:S], att_s[0:H_FOX, 1, 0:S]
                chain.wait(A(z, bank[7][0:H_FOX, 0:S], ACT.Identity,
                             bias=par[0:H_FOX, COLS["b_forget"]:COLS["b_forget"] + 1]))
                chain.wait(A(az, z, ACT.Abs))
                chain.wait(A(az, az, ACT.Exp, scale=-1.0))
                A(az, az, ACT.Ln, bias=1.0).then_inc(f_ln, 1)

            def token_pair(name, n, dst, scale=None):
                multiplied(PART[name] + n + 1)
                for tok in range(2):
                    src = out_of(TILE[name] + n + tok)
                    if scale is None:
                        A(dst[:, 4 * tok + n // 2, :], src, ACT.Copy).then_inc(evacuated, 1)
                    else:
                        A(dst[:, 4 * tok + n // 2, :], src, ACT.Copy, scale=scale[:, tok:tok + 1]).then_inc(evacuated, 1)
                for j in range(2):
                    hi(0, 0, PART[name] + n + j + HI_AHEAD)

            for n in range(0, C, 2):
                token_pair("v", n, V)
                if n == 0:
                    parameters()
                if n == 2:
                    forget_logits()
            act.wait_ge(ext_out, 16)
            for n in range(8):
                multiplied(PART["gates"] + n)
                m, g = n // 4, n // 2 % 2
                for j, o in enumerate(GATE_PARTS[n % 2]):
                    src = bank[4 + 2 * (n % 2) + j // 2][:, j % 2 * S:j % 2 * S + S]
                    dst, b = (IG, "b_x") if m == 0 else (RG, "b_a")
                    A(dst[:, 5 * g + o, :], src, ACT.Sigmoid, bias=col(b, 5 * g + o)).then_inc(gates_evac, 1)
                hi(0, 0, PART["gates"] + n + HI_AHEAD)
            act.wait_ge(der_ready, 4)

            def lru_decay(t):
                act.wait_ge(ix_done, t + 1)
                act.wait_ge(gates_evac, R + t + 1)
                A(XC[:, t, :], RG[:, t, :], ACT.Tanh, scale=der[:, D_SP + t:D_SP + t + 1]).then_inc(tanh_done, 1)
                act.wait_ge(tanh_done, t + 1)
                A(RG[:, t, :], RG[:, t, :], ACT.Exp, scale=der[:, D_NSP + t:D_NSP + t + 1]).then_inc(decay_done, 1)

            for t in range(R):
                lru_decay(t)
                multiplied(PART["ga"] + t)
                A(GA[:, t, :], out_of(TILE["ga"] + t), ACT.Copy).then_inc(evacuated, 1)
                hi(0, 0, PART["ga"] + t + HI_AHEAD)

            def lru_gelu():
                act.wait_ge(evacuated, TILE["ga"] + R)
                A(GA, GA, ACT.Gelu_apprx_tanh).then_inc(gelu_done, 1)

            def lru_root():
                act.wait_ge(gain_done, R)
                A(XC, XC, ACT.Sqrt, scale=2.0).then_inc(root_done, 1)

            def lru_out(t):
                act.wait_ge(ya_done, t + 1)
                A(u_hi[:, R + t, :], GA[:, t, :], ACT.Copy).then_inc(yah, 1)

            def exps(n):
                b = n % 2
                act.wait_ge(negmax, n + 1)
                for j, (a, e) in enumerate([(0, P), (P, EXT)]):
                    A(att_s[:, b, a:e], att_s[:, b, a:e], ACT.Exp, bias=stat_s[:, b, 2 + j:3 + j],
                      accum_out=stat_s[:, b, 4 + j:5 + j]).then_inc(exp_done, 1)

            def copy_pt(n):
                act.wait_ge(pt_mm, n + 1)
                if n >= 2:
                    act.wait_ge(pv_mm, n - 1)
                A(att_pt[:, n % 2, :], bank[6][:, 0:EXT], ACT.Copy).then_inc(pt_copied, 1)

            def head_out(n, y, t):
                act.wait_ge(pv_mm, n + 1)
                A(u_hi[:, t, :], bank[7][:, 0:S], ACT.Copy).then_inc(y_hi, 1)

            act.wait_ge(der_ready, 5)
            for s in range(4 * C):
                n = s - 6
                if 0 <= n < H_FOX and n % 2:
                    head_out(n, None, n // 2)
                if 0 <= s - 3 < H_FOX:
                    exps(s - 3)
                multiplied(PART["qk"] + s)
                t, src = s // 2 % C, out_of(TILE["qk"] + s)
                if s >= 2 * C:
                    dst = SGA if s < 3 * C else SGB
                    A(dst[:, s % C, :], src, ACT.Sigmoid, bias=col("b_merge", s - 2 * C)).then_inc(evacuated, 1)
                elif s % 2 == 0:
                    A(Q[:, t, :], src, ACT.Copy, scale=DH_FOX ** -0.5).then_inc(evacuated, 1)
                else:
                    A(K[:, t, :], src, ACT.Copy).then_inc(evacuated, 1)
                hi(0, 0, PART["qk"] + s + HI_AHEAD)
                if 0 <= s - 4 < H_FOX:
                    copy_pt(s - 4)
                if s == 0:
                    lru_gelu()
                if s == 2:
                    lru_root()
                if 0 <= s - 7 < R:
                    lru_out(s - 7)

            for t in range(R):
                multiplied(PART["pa"] + t)
                hi(0, 0, PART["pa"] + t + HI_AHEAD)
            for t in range(C):
                multiplied(PART["pb"] + t)
                hi(0, 0, PART["pb"] + t + HI_AHEAD)
                act.wait_ge(merged, t + 1)
                A(h_hi[:, t, :], PRA[:, t, :], ACT.Copy).then_inc(mh, 1)
            for t in range(C):
                multiplied(PART["wo"] + t)
                A(M[:, t, :], out_of(TILE["wo"] + t), ACT.Copy).then_inc(evacuated, 1)
                hi(0, 0, PART["wo"] + t + HI_AHEAD)
            rms("post")
            for c in range(C):
                split("ffn", c)
            rms("ffn")

            with act.Fori(0, 2 * F1 // 4) as i:
                A(touch, touch, ACT.Gelu_apprx_tanh)
                for p in range(2):
                    multiplied(PART["up"] + 2 * p, i, 4)
                    hi(i, 4, PART["up"] + 2 * p + HI_AHEAD)
                    act.wait_ge(evacuated, lin(i, 4, TILE["up"] + 2 * p + 2))
                    act.wait_ge(pair_free, lin(i, 2, p + 1))
                    for j in (2 * p, 2 * p + 1):
                        A(YB[:, j, :], UB[:, j, :], ACT.Identity, scale=dcol("fconv_w", i * 4 + (2 * 2 * F1 + j)),
                          bias=dcol("fconv_b", i * 4 + j)).then_inc(u_conv, 1)
                    multiplied(PART["up"] + 2 * p + 1, i, 4)
                    hi(i, 4, PART["up"] + 2 * p + 1 + HI_AHEAD)
                    act.wait_ge(taps_done, lin(i, 4, R + 2 * p + 1))
                    A(GB[:, p, :], YB[:, 2 * p, :], ACT.Gelu_apprx_tanh).then_inc(gate_ready, 1)
            for j in range(F1):
                multiplied(PART["down"] + j)
                if j % 3 == 2:
                    A(M[:, j // 3, :], out_of(TILE["down"] + j // 3), ACT.Copy).then_inc(evacuated, 1)
                hi(0, 0, PART["down"] + j + HI_AHEAD)
            rms("post2")
            for c in range(C):
                split("n0", c)
            rms("n0", columns=True)

            for t in range(C):
                act.wait_ge(evacuated, TILE["hf"] + t + 1)
                A(FG[:, t, :], FG[:, t, :], ACT.Sigmoid).then_inc(f_raw, 1)
                multiplied(PART["hf"] + t)
                hi(0, 0, PART["hf"] + t + HI_AHEAD)
            for t in range(C):
                if t == 2:
                    act.wait_ge(k_ready, C)
                    A(CUM, FG, ACT.Ln).then_inc(logf_ready, 1)
                act.wait_ge(evacuated, TILE["hq"] + t + 1)
                A(QS[:, t, :], QS[:, t, :], ACT.Silu).then_inc(q_ready, 1)
                multiplied(PART["hq"] + t)
                hi(0, 0, PART["hq"] + t + HI_AHEAD)
            act.wait_ge(col_ready, 1)
            for l in range(1, LEVELS + 1):
                e, n = EB[l % 2], 2 * (l - 1)
                act.wait_ge(arg_ready, 2 * l)
                A(e, e, ACT.Exp).then_inc(dec_ready, 1)
                if l == LEVELS:
                    act.wait_ge(evacuated, TILE["hg"] + C - 2)
                    A(OG[:, 0:C - 2, :], OG[:, 0:C - 2, :], ACT.Sigmoid).then_inc(og_ready, 1)
                if n < C:
                    token_pair("hi", n, INP, RCOL)
                else:
                    for j in range(2):
                        multiplied(PART["hg"] + n - C + j)
                        hi(0, 0, PART["hg"] + n - C + j + HI_AHEAD)
            for g in range(2):
                act.wait_ge(lev_mm, 4 * LEVELS + g + 1)
                A(PX[:, 4 * g:4 * g + 4, :], bank[4 + g][:, :].rearrange("p (h t) -> p h t", h=4),
                  ACT.Copy).then_inc(px_copied, 1)
            act.wait_ge(evacuated, TILE["hg"] + C)
            A(OG[:, C - 2:C, :], OG[:, C - 2:C, :], ACT.Sigmoid).then_inc(og_ready, 1)
            for c in range(C):
                act.wait_ge(o_mm, c + 1)
                A(OC[:, c, :], bank[5 + c % 3][:, 0:S], ACT.Copy).then_inc(o_evac, 1)
                if c >= 1:
                    act.wait_ge(o_gated, c)
                    A(u_hi[:, c - 1, :], OH[:, c - 1, :], ACT.Copy).then_inc(oh_hi, 1)
            act.wait_ge(o_gated, C)
            A(u_hi[:, C - 1, :], OH[:, C - 1, :], ACT.Copy).then_inc(oh_hi, 1)
            rms("o")

            def feed(name, per, norm):
                for j in range(per * C):
                    multiplied(PART[name] + j)
                    if j < per * C - 1:
                        hi(0, 0, PART[name] + j + HI_AHEAD)
                    if j % per == per - 1 and norm != "final":
                        split(norm, j // per)
                hi(0, 0, PART[name] + per * C - 1 + HI_AHEAD)

            def swiglu(name, pairs0):
                with act.Fori(0, 2 * F2 // 4) as i:
                    A(touch, touch, ACT.Silu)
                    for j in range(4):
                        multiplied(PART[name] + j, i, 4)
                        if j % 2:
                            act.wait_ge(evacuated, lin(i, 4, TILE[name] + j))
                            A(GB[:, j // 2, :], GR[:, j // 2, :], ACT.Silu).then_inc(gate_ready, 1)
                        hi(i, 4, PART[name] + j + HI_AHEAD)

            feed("ho", 1, "f0")
            rms("f0")
            swiglu("up1", F1)
            feed("down1", 3, "n1")
            rms("n1", columns=True)
            act.wait_ge(col_ready, 2)
            for n in range(0, C, 2):
                token_pair("mv", n, MV, RCOL)
            for s in range(2 * C):
                n = (s - 2) // 2
                if s % 2 == 0 and s >= 6:
                    head_out(H_FOX + n - 2, None, n - 2)
                if s % 2 and s >= 3:
                    exps(H_FOX + (s - 3) // 2)
                multiplied(PART["mqk"] + s)
                hi(0, 0, PART["mqk"] + s + HI_AHEAD)
                if s % 2 == 0 and s >= 4:
                    copy_pt(H_FOX + n - 1)
            head_out(H_FOX + 5, None, 5)
            copy_pt(H_FOX + 6)
            exps(H_FOX + 7)
            head_out(H_FOX + 6, None, 6)
            copy_pt(H_FOX + 7)
            head_out(H_FOX + 7, None, 7)
            feed("mo", 1, "f1")
            rms("f1")
            swiglu("up2", F1 + F2)
            feed("down2", 3, "final")
            rms("final")
            for c in range(0, C, 4):
                act.wait_ge(ht_ready, C + c + 4)
                act.dma_start(out_d[:, c:c + 4, :], HT[:, c:c + 4, :]).then_inc(out_done, 16)
            act.wait_ge(out_done, 32)

        @block.vector
        def _(dve):
            v = nc.vector
            chain = Chain(dve, dve_step)

            def lo(i, m, c):
                if isinstance(i, int) and c >= PARTS:
                    return
                slot = c % RING
                dve.wait_ge(hi_ready, lin(i, m, c + 1))
                v.tensor_tensor(w_lo[:, slot, :], raw[:, slot, :], w_hi[:, slot, :].bitcast(F32),
                                ALU.subtract).then_inc(lo_ready, 1)

            def multiplied(c, i=0, m=0):
                dve.wait_ge(part_done, lin(i, m, c + 1))

            def out_of(t):
                return bank[t % BANKS][:, 0:S]

            def step(name, j):
                lo(0, 0, PART[name] + j + LO_AHEAD)

            def rstd(norm, columns=0):
                dve.wait_ge(rms_ready, NORMS[norm] + 1)
                v.reciprocal(RSTD, RSTD).then_inc(rstd_ready, 1)
                if columns:
                    dve.wait_ge(col_rms, columns)
                    v.reciprocal(RCOL, RCOL).then_inc(col_ready, 1)
                dve.wait_ge(rstd_ready, NORMS[norm] + 1)

            def h_low(norm, c):
                dve.wait_ge(hh_ready, H_COUNT[norm] + c + 1)
                v.scalar_tensor_tensor(out=h_lo[:, c, :], in0=X[:, c, :], scalar=col(NEXT[norm], GAIN0[norm] + c),
                                       in1=h_hi[:, c, :].bitcast(F32), op0=ALU.mult,
                                       op1=ALU.subtract).then_inc(hl_ready, 1)

            def normed(dst, t):
                v.tensor_tensor(dst, out_of(t), RSTD, ALU.mult).then_inc(evacuated, 1)

            def add_normed(norm, gain, n0, after):
                rstd(norm)

                def scaled(c):
                    if c % 2 == 0:
                        dve.wait_ge(evacuated, TILE["wo" if norm == "post" else "down"] + c + 1)
                        v.tensor_tensor(M[:, c, :], M[:, c, :], RSTD, ALU.mult).then_inc(post_t, 1)
                scaled(0)
                for c in range(C):
                    if c + 1 < C:
                        scaled(c + 1)
                    if c % 2:
                        dve.wait_ge(post_pool, (n0 + c + 1) // 2)
                    else:
                        dve.wait_ge(post_t, (n0 + c) // 2 + 1)
                    v.scalar_tensor_tensor(out=X[:, c, :], in0=M[:, c, :], scalar=col(gain, c), in1=X[:, c, :],
                                           op0=ALU.mult, op1=ALU.add).then_inc(x_ready, 1)
                    if c >= 1:
                        h_low(after, c - 1)
                h_low(after, C - 1)

            v.memset(der[:, D_EPS - 1:D_EPS + 1], EPS).then_inc(der_ready, 1)
            v.memset(ones[:, :], 1.0).then_inc(ones_ready, 1)
            for n in range(LO_AHEAD):
                lo(0, 0, n)
            dve.wait_ge(par_in, 16)
            rstd("mix")
            for c in range(C + 1):
                if c < C:
                    v.scalar_tensor_tensor(out=HT[:, c, :], in0=X[:, c, :], scalar=col("mix_pre", c), in1=RSTD,
                                           op0=ALU.mult, op1=ALU.mult).then_inc(ht_ready, 1)
                if c >= 1:
                    dve.wait_ge(hh_ready, c)
                    v.tensor_tensor(h_lo[:, c - 1, :], HT[:, c - 1, :], h_hi[:, c - 1, :].bitcast(F32),
                                    ALU.subtract).then_inc(hl_ready, 1)
            l0, l1 = (par[:, COLS["lb"] + C * r:COLS["lb"] + C * r + C] for r in range(2))
            chain.wait(v.tensor_tensor(der[:, D_LB:D_LB + C], l0, l1, ALU.max))
            for r, l in enumerate((l0, l1)):
                v.tensor_tensor(der[:, D_E + C * r:D_E + C * r + C], l, der[:, D_LB:D_LB + C],
                                ALU.subtract).then_inc(der_ready, 1)
            for t in range(R):
                step("xa", t)
                dve.wait_ge(evacuated, TILE["xa"] + t + 1)
                for j in (1, 2, 3):
                    ins = v.scalar_tensor_tensor(out=XC[:, t, j:S], in0=XA[:, t, 0:S - j],
                                                 scalar=col("conv_w", (3 - j) * R + t), in1=XC[:, t, j:S],
                                                 op0=ALU.mult, op1=ALU.add)
                    if j < 3:
                        chain.wait(ins)
                    else:
                        ins.then_inc(taps_done, 1)
                if t >= 1:
                    dve.wait_ge(xch_ready, t)
                    v.tensor_tensor(u_lo[:, t - 1, :], XC[:, t - 1, :], u_hi[:, t - 1, :].bitcast(F32),
                                    ALU.subtract).then_inc(xcl_ready, 1)
            dve.wait_ge(xch_ready, R)
            v.tensor_tensor(u_lo[:, R - 1, :], XC[:, R - 1, :], u_hi[:, R - 1, :].bitcast(F32),
                            ALU.subtract).then_inc(xcl_ready, 1)

            def parameters():
                lam = par[:, COLS["lam"]:COLS["lam"] + R]
                dve.wait_ge(sp_ln, 1)
                chain.wait(v.tensor_scalar(der[:, D_NSP:D_NSP + R], lam, -1.0, 0.0, ALU.mult, ALU.max))
                chain.wait(v.tensor_tensor(der[:, D_SP:D_SP + R], der[:, D_SP:D_SP + R], der[:, D_NSP:D_NSP + R],
                                           ALU.add))
                chain.wait(v.tensor_scalar(der[:, D_NSP:D_NSP + R], der[:, D_SP:D_SP + R], -LRU_C, None, ALU.mult))
                v.tensor_scalar(der[:, D_SP:D_SP + R], der[:, D_SP:D_SP + R], LRU_C, None,
                                ALU.mult).then_inc(der_ready, 1)
                dve.wait_ge(lb_exp, 2)
                e0, e1 = (der[:, D_E + C * r:D_E + C * r + C] for r in range(2))
                chain.wait(v.tensor_tensor(e1, e0, e1, ALU.add))
                chain.wait(v.reciprocal(e1, e1))
                chain.wait(v.tensor_tensor(der[:, D_LB:D_LB + C], e0, e1, ALU.mult))
                v.tensor_scalar(der[:, D_1LB:D_1LB + C], der[:, D_LB:D_LB + C], -1.0, 1.0, ALU.mult,
                                ALU.add).then_inc(der_ready, 1)

            def forget_sums():
                dve.wait_ge(f_ln, 1)
                z, az = att_s[0:H_FOX, 0, 0:S], att_s[0:H_FOX, 1, 0:S]
                chain.wait(v.tensor_scalar(z, z, 0.0, None, ALU.min))
                chain.wait(v.tensor_tensor(az, az, z, ALU.subtract))
                chain.wait(v.memset(z, 1.0))
                v.tensor_tensor_scan(ncum[:, :], z, az, 0.0, ALU.mult, ALU.add).then_inc(cum_ready, 1)

            for n in range(C):
                step("v", n)
                if n == 3:
                    parameters()
                if n == 5:
                    forget_sums()
            for n in range(8):
                step("gates", n)
                if n == 1:
                    dve.wait_ge(cumt_mm, 1)
                    v.tensor_scalar(cum_t[:, :, :], bank[7][:, 0:2 * H_FOX].rearrange("p (b h) -> p b h", b=2), -1.0,
                                    None, ALU.mult).then_inc(cumt_ready, 1)

            def lru_recip(t):
                dve.wait_ge(den_ready, t + 1)
                v.reciprocal(DEN[:, t % 2, :], DEN[:, t % 2, :]).then_inc(recip_done, 1)

            def lru_scan(t):
                dve.wait_ge(b_done, t + 1)
                v.tensor_tensor_scan(XC[:, t, :], RG[:, t, :], IG[:, t, :], 0.0, ALU.mult, ALU.add).then_inc(scan_done, 1)

            def lru_lo(t):
                dve.wait_ge(yah, t + 1)
                v.tensor_tensor(u_lo[:, R + t, :], GA[:, t, :], u_hi[:, R + t, :].bitcast(F32),
                                ALU.subtract).then_inc(yal, 1)

            def maxima(n):
                b = n % 2
                dve.wait_ge(s_evac, 2 * n + 2)
                for j, (a, e) in enumerate([(0, P), (P, EXT)]):
                    v.tensor_reduce(stat_s[:, b, j:j + 1], att_s[:, b, a:e], AX.X, ALU.max).then_inc(mx_done, 1)
                dve.wait_ge(mx_done, 2 * n + 2)
                v.tensor_scalar(stat_s[:, b, 2:4], stat_s[:, b, 0:2], -1.0, None, ALU.mult).then_inc(negmax, 1)

            def probabilities(n):
                b = n % 2
                dve.wait_ge(exp_done, 2 * n + 2)
                v.reciprocal(stat_s[:, b, 6:8], stat_s[:, b, 4:6]).then_inc(rsum_done, 1)
                dve.wait_ge(rsum_done, n + 1)
                for j, (a, e) in enumerate([(0, P), (P, EXT)]):
                    v.tensor_scalar(att_s[:, b, a:e], att_s[:, b, a:e], stat_s[:, b, 6 + j:7 + j], None,
                                    ALU.mult).then_inc(p_ready, 1)

            def head_low(t, count):
                dve.wait_ge(y_hi, count)
                v.tensor_tensor(u_lo[:, t, :], bank[7][:, 0:S], u_hi[:, t, :].bitcast(F32),
                                ALU.subtract).then_inc(y_lo, 1)

            def fox_shift(n):
                b = n % 2
                dve.wait_ge(s_mm, n + 1)
                if n >= 2:
                    dve.wait_ge(pt_mm, n - 1)
                for j, (a, e) in enumerate([(0, P), (P, EXT)]):
                    v.scalar_tensor_tensor(out=att_s[:, b, a:e], in0=bank[4 + b][:, a:e], scalar=cum_t[:, j, n:n + 1],
                                           in1=mask[:, a:e], op0=ALU.add, op1=ALU.add).then_inc(s_evac, 1)

            dve.wait_ge(cst_in, 32)
            dve.wait_ge(cumt_ready, 1)
            for t in range(R):
                step("ga", t)
                if t >= 1:
                    lru_recip(t - 1)
            for s in range(4 * C):
                step("qk", s)
                if 0 <= s - 3 < H_FOX:
                    probabilities(s - 3)
                if 0 <= s - 6 < H_FOX and s % 2:
                    head_low((s - 6) // 2, (s - 6) // 2 + 1)
                if s == 0:
                    lru_recip(R - 1)
                if 0 <= s - 5 < R:
                    lru_scan(s - 5)
                if 0 <= s - 8 < R:
                    lru_lo(s - 8)
                if 0 <= s - 2 < H_FOX:
                    fox_shift(s - 2)
                    maxima(s - 2)

            dve.wait_ge(evacuated, TILE["pa"])
            for t in range(C):
                last = (R * t + R - 1) // BLK
                for n in range((R * t - 1) // BLK + 1 if t else 0, last + 1):
                    step("pa", n)
                multiplied(PART["pa"] + last)
                v.tensor_tensor(PRA[:, t, :], out_of(TILE["pa"] + t), SGA[:, t, :], ALU.mult).then_inc(evacuated, 1)

            def merged_low(t):
                dve.wait_ge(mh, t + 1)
                v.tensor_tensor(h_lo[:, t, :], PRA[:, t, :], h_hi[:, t, :].bitcast(F32), ALU.subtract).then_inc(ml, 1)

            for t in range(C):
                step("pb", t)
                if t >= 1:
                    merged_low(t - 1)
                multiplied(PART["pb"] + t)
                v.tensor_tensor(PRB[:, t, :], out_of(TILE["pb"] + t), SGB[:, t, :], ALU.mult).then_inc(evacuated, 1)
                dve.wait_ge(evacuated, TILE["pb"] + t + 1)
                v.tensor_tensor(PRA[:, t, :], PRA[:, t, :], PRB[:, t, :], ALU.add).then_inc(merged, 1)
            merged_low(C - 1)
            for t in range(C):
                step("wo", t)
            dve.wait_ge(x_back, 16)
            add_normed("post", "mix_post", 0, "ffn")

            def up_pair(i, p, first=False):
                pair = (2 * p, 2 * p + 1)
                for j in pair:
                    multiplied(PART["up"] + j, i, 4)
                    normed(UB[:, j, :], TILE["up"] + j)
                for j in pair:
                    if not (first and j == 0):
                        lo(i, 4, PART["up"] + j + LO_AHEAD)
                for j in pair:
                    dve.wait_ge(u_conv, lin(i, 4, j + 1))
                    v.scalar_tensor_tensor(out=YB[:, j, 1:S], in0=UB[:, j, 0:S - 1],
                                           scalar=dcol("fconv_w", lin(i, 4, 2 * F1 + j)), in1=YB[:, j, 1:S],
                                           op0=ALU.mult, op1=ALU.add).then_inc(tap_done, 1)
                for j in pair:
                    dve.wait_ge(tap_done, lin(i, 4, j + 1))
                    v.scalar_tensor_tensor(out=YB[:, j, 2:S], in0=UB[:, j, 0:S - 2],
                                           scalar=dcol("fconv_w", lin(i, 4, j)), in1=YB[:, j, 2:S],
                                           op0=ALU.mult, op1=ALU.add).then_inc(taps_done, 1)

            step("up", 0)
            rstd("ffn")
            up_pair(0, 0, first=True)
            up_pair(0, 1)
            with dve.Fori(1, 2 * F1 // 4) as i:
                up_pair(i, 0)
                up_pair(i, 1)
            for j in range(F1):
                step("down", j)
            add_normed("post2", "ffn_post", C, "n0")

            def gate_key(t):
                dve.wait_ge(f_raw, t + 1)
                v.tensor_scalar(FG[:, t, :], FG[:, t, :], der[:, D_1LB + t:D_1LB + t + 1],
                                der[:, D_LB + t:D_LB + t + 1], ALU.mult, ALU.add).then_inc(f_ready, 1)
                dve.wait_ge(f_ready, t + 1)
                v.tensor_scalar(KK[:, t, :], FG[:, t, :], -1.0, 1.0, ALU.mult, ALU.add).then_inc(k_ready, 1)

            step("hf", 0)
            rstd("n0", columns=1)
            for t in range(C):
                multiplied(PART["hf"] + t)
                normed(FG[:, t, :], TILE["hf"] + t)
                if t >= 1:
                    step("hf", t)
                    gate_key(t - 1)
            for t in range(C):
                multiplied(PART["hq"] + t)
                normed(QS[:, t, :], TILE["hq"] + t)
                step("hq", t)
                if t == 0:
                    gate_key(C - 1)
                if t == 2:
                    dve.wait_ge(one_row, 1)
                    dve.wait_ge(logf_ready, 1)
                for c in {2: [0, 1], 3: [2], 4: [3], 5: [4, 5], 6: [6], 7: [7]}.get(t, []):
                    v.tensor_tensor_scan(CUM[:, c, :], ONES_ROW, CUM[:, c, :], 0.0, ALU.mult,
                                         ALU.add).then_inc(hcum_ready, 1)

            def halves(ap, l):
                w = flat(ap).rearrange("p (n b) -> p n b", b=2 ** l)
                return w[:, :, 0:2 ** (l - 1)], w[:, :, 2 ** (l - 1):]

            def level_args(l):
                low, up = halves(CUM, l)
                elow, eup = halves(EB[l % 2], l)
                n, h = low.shape[1], low.shape[2]
                mid = low[:, :, h - 1:h].to_broadcast([P, n, h])
                if l >= 3:
                    dve.wait_ge(lev_mm, 4 * (l - 1))
                v.tensor_tensor(elow, mid, low, ALU.subtract).then_inc(arg_ready, 1)
                v.tensor_tensor(eup, up, mid, ALU.subtract).then_inc(arg_ready, 1)

            def level_keys(l):
                klow, _ = halves(KK, l)
                elow, _ = halves(EB[l % 2], l)
                dve.wait_ge(dec_ready, l)
                v.tensor_tensor(elow, elow, klow, ALU.mult).then_inc(x_low, 1)

            def take(l):
                for g in range(4):
                    dve.wait_ge(lev_mm, 4 * l + g + 1)
                    v.copy_predicated(PD[:, 4 * g:4 * g + 4, :], LM[:, l:l + 1, :].to_broadcast([P, 4, P]),
                                      bank[4 + g][:, :].rearrange("p (n t) -> p n t", n=4)).then_inc(lev_sel, 1)

            dve.wait_ge(hcum_ready, C)
            dve.wait_ge(lm_in, 16)
            dve.wait_ge(pd_zero, 1)
            level_args(1)
            for l in range(1, LEVELS + 1):
                n = 2 * (l - 1)
                step("hi", n)
                if l < LEVELS:
                    level_args(l + 1)
                level_keys(l)
                take(l - 1)
                step("hi", n + 1)
                if n == C:
                    dve.wait_ge(evacuated, TILE["hg"])
                for t in (n - C, n - C + 1):
                    if t >= 0:
                        multiplied(PART["hg"] + t)
                        normed(OG[:, t, :], TILE["hg"] + t)
            for c in range(C + 1):
                if c < C:
                    dve.wait_ge(og_ready, 1 if c < C - 2 else 2)
                    dve.wait_ge(o_evac, c + 1)
                    v.scalar_tensor_tensor(out=OH[:, c, :], in0=OC[:, c, :], scalar=col("out_norm", c), in1=OG[:, c, :],
                                           op0=ALU.mult, op1=ALU.mult).then_inc(o_gated, 1)
                if c >= 1:
                    dve.wait_ge(oh_hi, c)
                    v.tensor_tensor(u_lo[:, c - 1, :], OH[:, c - 1, :], u_hi[:, c - 1, :].bitcast(F32),
                                    ALU.subtract).then_inc(oh_lo, 1)
            step("ho", 0)
            rstd("o")
            for t in range(C):
                multiplied(PART["ho"] + t)
                normed(M[:, t, :], TILE["ho"] + t)
                if t >= 1:
                    step("ho", t)
                dve.wait_ge(evacuated, TILE["ho"] + t + 1)
                v.tensor_tensor(X[:, t, :], X[:, t, :], M[:, t, :], ALU.add).then_inc(x_ready, 1)
                if t >= 1:
                    h_low("f0", t - 1)
            h_low("f0", C - 1)

            def add_branch(name, per, norm):
                for j in range(per * C):
                    step(name, j)
                    t = j // per
                    if j % per == 0 and t >= 1 and norm != "final":
                        h_low(norm, t - 1)
                    if j % per == per - 1:
                        multiplied(PART[name] + j)
                        v.tensor_tensor(X[:, t, :], X[:, t, :], out_of(TILE[name] + t), ALU.add).then_inc(evacuated, 1)
                if norm != "final":
                    h_low(norm, C - 1)

            def swiglu(name, norm, pairs0):
                step(name, 0)
                rstd(norm)

                def pair_tile(i, j, first=False):
                    multiplied(PART[name] + j, i, 4)
                    if j % 2 == 0:
                        dve.wait_ge(pair_free, lin(i, 2, pairs0 + j // 2 + 1))
                    normed(YB[:, j, :] if j % 2 else GR[:, j // 2, :], TILE[name] + j)
                    if not first:
                        lo(i, 4, PART[name] + j + LO_AHEAD)

                for j in range(4):
                    pair_tile(0, j, j == 0)
                with dve.Fori(1, 2 * F2 // 4) as i:
                    for j in range(4):
                        pair_tile(i, j)

            swiglu("up1", "f0", F1)
            add_branch("down1", 3, "n1")
            step("mv", 0)
            rstd("n1", columns=2)
            dve.wait_ge(bias_in, 32)
            v.tensor_tensor(BIAS, BIAS, mask[:, :].rearrange("p (o e) -> p o e", o=1).to_broadcast([P, H_MOBA, EXT]),
                            ALU.add).then_inc(bias_masked, 1)
            for n in range(1, C):
                step("mv", n)

            def moba_shift(h):
                n, b = H_FOX + h, h % 2
                dve.wait_ge(s_mm, n + 1)
                dve.wait_ge(pt_mm, n - 1)
                for j, (a, e) in enumerate([(0, P), (P, EXT)]):
                    v.scalar_tensor_tensor(out=att_s[:, b, a:e], in0=bank[4 + b][:, a:e], scalar=DH_MOBA ** -0.5,
                                           in1=BIAS[:, h, a:e], op0=ALU.mult, op1=ALU.add).then_inc(s_evac, 1)

            dve.wait_ge(bias_masked, 1)
            dve.wait_ge(evacuated, TILE["mqk"])
            for s in range(2 * C):
                step("mqk", s)
                h = (s - 2) // 2
                if s % 2 and s >= 3:
                    probabilities(H_FOX + (s - 3) // 2)
                if s % 2 == 0 and s >= 6:
                    head_low(h - 2, C + h - 1)
                multiplied(PART["mqk"] + s)
                normed((MK if s % 2 else MQ)[:, s // 2, :], TILE["mqk"] + s)
                if s % 2 == 0 and s >= 2:
                    moba_shift(h)
                    maxima(H_FOX + h)
            head_low(5, C + 6)
            moba_shift(7)
            maxima(H_FOX + 7)
            probabilities(H_FOX + 7)
            head_low(6, C + 7)
            head_low(7, C + 8)
            add_branch("mo", 1, "f1")
            swiglu("up2", "f1", F1 + F2)
            add_branch("down2", 3, "final")
            rstd("final")
            for c in range(C):
                v.scalar_tensor_tensor(out=HT[:, c, :], in0=X[:, c, :], scalar=col("final", c), in1=RSTD,
                                       op0=ALU.mult, op1=ALU.mult).then_inc(ht_ready, 1)

        @block.gpsimd
        def _(pool):
            g = nc.gpsimd
            chain = Chain(pool, pool_step)
            pool.dma_start(onehot, onehot_d).then_inc(tab_in, 16)
            pool.dma_start(table, table_d).then_inc(tab_in, 16)
            pool.dma_start(wf[:, :, :], wf_d).then_inc(wf_in, 16)
            pool.dma_start(ident[:, :], ident_d).then_inc(cst_in, 16)
            pool.dma_start(mask[:, :], mask_d).then_inc(cst_in, 16)
            g.memset(ONES_ROW, 1.0).then_inc(one_row, 1)
            pool.wait_ge(ext_ready, H_MOBA)
            pool.dma_start(bass.AP(tensor=scr, offset=0, ap=[[EXT, P], [P * EXT, H_MOBA], [1, EXT]]),
                           ext).then_inc(ext_out, 16)
            for t in range(R):
                pool.wait_ge(gates_evac, t + 1)
                pool.wait_ge(xcl_ready, R)
                g.tensor_tensor(IG[:, t, :], IG[:, t, :], XC[:, t, :], ALU.mult).then_inc(ix_done, 1)
            pool.wait_ge(one_row, 1)
            for t in range(R + 1):
                if t < R:
                    pool.wait_ge(tanh_done, t + 1)
                    if t >= 2:
                        pool.wait_ge(gain_done, t - 1)
                    g.tensor_tensor(DEN[:, t % 2, :], XC[:, t, :], ONES_ROW, ALU.add).then_inc(den_ready, 1)
                if t >= 1:
                    pool.wait_ge(recip_done, t)
                    g.tensor_tensor(XC[:, t - 1, :], XC[:, t - 1, :], DEN[:, (t - 1) % 2, :],
                                    ALU.mult).then_inc(gain_done, 1)
            pool.wait_ge(root_done, 1)
            for t in range(R + 2):
                if t < R:
                    pool.wait_ge(decay_done, t + 1)
                    g.tensor_tensor(IG[:, t, :], IG[:, t, :], XC[:, t, :], ALU.mult).then_inc(b_done, 1)
                if t >= 2:
                    pool.wait_ge(scan_done, t - 1)
                    pool.wait_ge(gelu_done, 1)
                    g.tensor_tensor(GA[:, t - 2, :], GA[:, t - 2, :], XC[:, t - 2, :], ALU.mult).then_inc(ya_done, 1)
            pool.wait_ge(merged, C)
            pool.dma_start(X, x_d).then_inc(x_back, 16)
            pool.dma_start(LM, lmask_d).then_inc(lm_in, 16)
            pool.wait_ge(ml, C)
            g.memset(PD, 0.0).then_inc(pd_zero, 1)
            for pair in range(2):
                g.memset(PB[:, pair, 0:1], 0.0).then_inc(pair_free, 1)

            def squares(norm, src, count, n0):
                for c in range(C):
                    pool.wait_ge(count, n0 + c + 1)
                    if c == 0:
                        chain.wait(g.tensor_tensor(ACC, src[:, c, :], src[:, c, :], ALU.mult))
                    else:
                        chain.wait(g.tensor_tensor(SQT, src[:, c, :], src[:, c, :], ALU.mult))
                        ins = g.tensor_tensor(ACC, ACC, SQT, ALU.add)
                        if c < C - 1:
                            chain.wait(ins)
                        else:
                            ins.then_inc(acc_ready, 1)

            def half_scaled(norm):
                pool.wait_ge(rstd_ready, NORMS[norm] + 1)
                for c in range(1, C, 2):
                    g.tensor_tensor(M[:, c, :], M[:, c, :], RSTD, ALU.mult).then_inc(post_pool, 1)

            def products(i, pair, pairs0, tiles_ready, t0):
                pool.wait_ge(gate_ready, lin(i, 2, pairs0 + pair + 1))
                pool.wait_ge(tiles_ready, lin(i, 4, t0 + 2 * pair + 2))
                g.tensor_tensor(PB[:, pair, :], GB[:, pair, :], YB[:, 2 * pair + 1, :], ALU.mult).then_inc(pair_free, 1)
                pool.wait_ge(pair_free, lin(i, 2, 2 + pairs0 + pair + 1))
                dst_h, dst_l = u_hi[:, bass.ds(i * 2 + pair, 1), :], u_lo[:, bass.ds(i * 2 + pair, 1), :]
                g.tensor_copy(dst_h, PB[:, pair:pair + 1, :]).then_inc(uh_ready, 1)
                pool.wait_ge(uh_ready, lin(i, 2, pairs0 + pair + 1))
                g.tensor_tensor(dst_l, PB[:, pair:pair + 1, :], dst_h.bitcast(F32), ALU.subtract).then_inc(ul_ready, 1)

            def swiglu(name, pairs0):
                with pool.Fori(0, F2 // 2) as i:
                    for pair in range(2):
                        products(i, pair, pairs0, evacuated, TILE[name])

            squares("post", M, evacuated, TILE["wo"])
            half_scaled("post")
            with pool.Fori(0, F1 // 2) as i:
                for pair in range(2):
                    products(i, pair, 0, taps_done, R)
            squares("post2", M, evacuated, TILE["down"])
            half_scaled("post2")
            for l in range(1, LEVELS + 1):
                w = flat(EB[l % 2]).rearrange("p (n b) -> p n b", b=2 ** l)[:, :, 2 ** (l - 1):]
                q = flat(QS).rearrange("p (n b) -> p n b", b=2 ** l)[:, :, 2 ** (l - 1):]
                pool.wait_ge(dec_ready, l)
                g.tensor_tensor(w, w, q, ALU.mult).then_inc(x_up, 1)
            squares("o", OC, o_evac, 0)
            squares("f0", X, *X_SRC["f0"])
            swiglu("up1", F1)
            pool.wait_ge(ext_out, 16)
            for j, (a, e) in enumerate([(0, P), (P, EXT)]):
                pool.dma_start(BIAS[:, :, a:e], bass.AP(tensor=scr, offset=255 - P * j,
                               ap=[[EXT - 1, P], [P * EXT, H_MOBA], [1, e - a]])).then_inc(bias_in, 16)
            squares("n1", X, *X_SRC["n1"])
            squares("f1", X, *X_SRC["f1"])
            swiglu("up2", F1 + F2)
            squares("final", X, *X_SRC["final"])

        @block.tensor
        def _(pe):
            mm = nc.tensor.matmul

            def three(out, slot, b, r_hi, r_lo, start, stop):
                s = slice(b * P, (b + 1) * P)
                mm(out, w_hi[:, slot, s], r_hi, start=start, stop=False)
                mm(out, w_hi[:, slot, s], r_lo, start=False, stop=False)
                return mm(out, w_lo[:, slot, s], r_hi, start=False, stop=stop)

            def free_bank(i, m, t):
                if t >= BANKS or not isinstance(i, int):
                    pe.wait_ge(evacuated, lin(i, m, t - BANKS + 1))

            def tile(i, c, t, x_hi=h_hi, x_lo=h_lo, low=None, n0=0, blocks=range(BLK), sums=0):
                if blocks[0] == 0:
                    pe.wait_ge(lo_ready, lin(i, 4, c + 1))
                    free_bank(i, 4, t)
                for b in blocks:
                    if low is not None:
                        pe.wait_ge(low, n0 + b + 1)
                    last = three(bank[t % BANKS][:, 0:S], c % RING, b, x_hi[:, b, :], x_lo[:, b, :], b == 0, b == BLK - 1)
                    if sums:
                        pe.wait_ge(sq_ready, sums + b + 1)
                        square = mm(bank[4][:, 0:S], ones[:, :], SQ[:, b, :], start=(b == 0), stop=(b == BLK - 1))
                if blocks[-1] == BLK - 1:
                    last.then_inc(part_done, 1)
                return square if sums else None

            def tiles(c, t, n, x_hi=h_hi, x_lo=h_lo):
                with pe.Fori(0, n // 4) as i:
                    for j in range(4):
                        tile(i, c + j, t + j, x_hi, x_lo)

            def stat(norm, columns=False):
                pe.wait_ge(acc_ready, POOL_SUMS.index(norm) + 1)
                last = mm(bank[4][:, 0:S], ones[:, :], ACC, start=True, stop=True)
                if columns:
                    for tok in range(2):
                        last = mm(bank[4][:, S + tok:S + tok + 1], ACC[:, tok * P:(tok + 1) * P], ones[:, 0:1],
                                  start=True, stop=True)
                last.then_inc(stat_done, 1)

            def after_norm(norm, name, n, columns=False):
                c, t = PART[name], TILE[name]
                if norm in ("ffn", "n0"):
                    sums = tile(0, c, t, low=hl_ready, n0=H_COUNT[norm], sums=C if norm == "ffn" else 2 * C)
                    if columns:
                        for tok in range(2):
                            for b in range(C):
                                sums = mm(bank[4][:, S + tok:S + tok + 1], SQ[:, b, tok * P:(tok + 1) * P], ones[:, 0:1],
                                          start=(b == 0), stop=(b == C - 1))
                    sums.then_inc(stat_done, 1)
                else:
                    tile(0, c, t, low=hl_ready, n0=H_COUNT[norm])
                    stat(norm, columns)
                for j in range(1, 4):
                    tile(0, c + j, t + j)
                tiles(c + 4, t + 4, n - 4)

            def token_tile(c, t, n, tok, low=None, n0=0):
                s0 = (c + n) % RING
                if tok == 0:
                    pe.wait_ge(lo_ready, c + n + 2)
                free_bank(0, 0, t + n + tok)
                out = bank[(t + n + tok) % BANKS][:, 0:S].rearrange("p (z f) -> p z f", z=2)
                ts = slice(tok * P, (tok + 1) * P)
                for b in range(BLK):
                    if low is not None:
                        pe.wait_ge(low, n0 + b + 1)
                    f = slice(b * P, (b + 1) * P)
                    mm(out, h_hi[:, b, ts], w_hi[:, s0:s0 + 2, f], start=(b == 0), stop=False)
                    mm(out, h_lo[:, b, ts], w_hi[:, s0:s0 + 2, f], start=False, stop=False)
                    last = mm(out, h_hi[:, b, ts], w_lo[:, s0:s0 + 2, f], start=False, stop=(b == BLK - 1))
                if tok == 1:
                    last.then_inc(part_done, 2)

            def down(name, KT, n0):
                for j in range(24):
                    c, t = PART[name] + j, TILE[name] + j // 3
                    pe.wait_ge(lo_ready, c + 1)
                    if j % 3 == 0:
                        free_bank(0, 0, t)
                    for b in range(min(BLK, KT - BLK * (j % 3))):
                        k = BLK * (j % 3) + b
                        if j < 3:
                            pe.wait_ge(ul_ready, n0 + k + 1)
                        last = three(bank[t % BANKS][:, 0:S], c % RING, b, u_hi[:, k, :], u_lo[:, k, :],
                                     k == 0, k == KT - 1)
                    last.then_inc(part_done, 1)

            pe.wait_ge(ones_ready, 1)
            for c in range(C):
                pe.wait_ge(sq_ready, c + 1)
                last = mm(bank[4][:, 0:S], ones[:, :], SQ[:, c, :], start=(c == 0), stop=(c == C - 1))
            last.then_inc(stat_done, 1)
            tile(0, 0, 0, low=hl_ready)
            for t in range(1, R):
                tile(0, PART["xa"] + t, TILE["xa"] + t)
                if t <= H_MOBA:
                    h = t - 1
                    if h == 0:
                        pe.wait_ge(tab_in, 32)
                    if h >= 2:
                        pe.wait_ge(ext_ready, h - 1)
                    mm(bank[5 + h % 2][:, 0:EXT], table[:, h:h + 1].to_broadcast([BUCKETS, P]), onehot, start=True,
                       stop=True).then_inc(ext_mm, 1)
            pe.wait_ge(wf_in, 16)
            for c in range(C):
                last = mm(bank[7][0:H_FOX, 0:S], wf[:, c, :], HT[:, c, :], start=(c == 0), stop=(c == C - 1))
            last.then_inc(f_mm, 1)
            for n in range(0, C, 2):
                for tok in range(2):
                    token_tile(PART["v"], TILE["v"], n, tok)
            pe.wait_ge(cst_in, 32)
            pe.wait_ge(cum_ready, 1)
            for b in range(2):
                last = nc.tensor.transpose(bank[7][:, b * H_FOX:(b + 1) * H_FOX], ncum[:, b * P:(b + 1) * P],
                                           ident[0:H_FOX, 0:H_FOX])
            last.then_inc(cumt_mm, 1)
            pe.wait_ge(xcl_ready, R)
            pe.wait_ge(ext_ready, H_MOBA)
            for n in range(8):
                c, g = PART["gates"] + n, n // 2 % 2
                pe.wait_ge(lo_ready, c + 1)
                if n >= 2:
                    pe.wait_ge(gates_evac, 5 * (n // 2) - (2 if n % 2 == 0 else 0))
                b = 0
                for j, o in enumerate(GATE_PARTS[n % 2]):
                    out = bank[4 + 2 * (n % 2) + j // 2][:, j % 2 * S:j % 2 * S + S]
                    for k, f in enumerate(GATE_IN[o]):
                        last = three(out, c % RING, b, u_hi[:, 5 * g + f, :], u_lo[:, 5 * g + f, :], k == 0,
                                     k == len(GATE_IN[o]) - 1)
                        b += 1
                last.then_inc(part_done, 1)
            tiles(PART["ga"], TILE["ga"], 8)
            for t in range(8, R):
                tile(0, PART["ga"] + t, TILE["ga"] + t)

            def transposes(n):
                b = n % 2
                pe.wait_ge(p_ready, 2 * n + 2)
                if n >= 1:
                    pe.wait_ge(pt_copied, n)
                for j in range(3):
                    last = nc.tensor.transpose(bank[6][:, j * P:(j + 1) * P], att_s[:, b, j * P:(j + 1) * P], ident[:, :])
                last.then_inc(pt_mm, 1)

            def fox_scores(h):
                t, o, out = h // 2, h % 2 * DH_FOX, bank[4 + h % 2]
                pe.wait_ge(evacuated, TILE["qk"] + 2 * t + 2)
                if h >= 2:
                    pe.wait_ge(s_evac, 2 * h - 2)
                sel = ident[0:H_FOX, h:h + 1].to_broadcast([H_FOX, P])
                for a, e, qb in ((0, P, 0), (P, EXT, 1)):
                    mm(out[:, a:e], Q[o:o + DH_FOX, t, qb * P:(qb + 1) * P], K[o:o + DH_FOX, t, 0:e - a],
                       start=True, stop=False)
                    last = mm(out[:, a:e], sel, ncum[:, 0:e - a], start=False, stop=True)
                last.then_inc(s_mm, 1)

            def values(n, out, vt):
                pe.wait_ge(pt_copied, n + 1)
                pt = att_pt[:, n % 2, :]
                mm(out[:, 0:P], vt(0), pt[:, 0:P], start=True, stop=True)
                mm(out[:, P:S], vt(0), pt[:, P:2 * P], start=True, stop=False)
                mm(out[:, P:S], vt(1), pt[:, 2 * P:EXT], start=False, stop=True).then_inc(pv_mm, 1)

            def fox_values(h):
                if h >= 2 and h % 2 == 0:
                    pe.wait_ge(y_lo, h // 2)
                o = h % 2 * DH_FOX
                values(h, bank[7][o:o + DH_FOX, 0:S],
                       lambda kb: flat(V[:, 4 * kb:4 * kb + 4, :])[:, h * DH_FOX:(h + 1) * DH_FOX])

            pe.wait_ge(gates_evac, 4 * 5)
            pe.wait_ge(cumt_ready, 1)
            for s in range(3 * C):
                tile(0, PART["qk"] + s, TILE["qk"] + s)
                if 0 <= s - 4 < H_FOX:
                    transposes(s - 4)
                if 0 <= s - 2 < H_FOX:
                    fox_scores(s - 2)
                if 0 <= s - 5 < H_FOX:
                    fox_values(s - 5)
            tiles(PART["sb"], TILE["sb"], C)
            for t in range(C):
                for k in range(R):
                    n, b = divmod(R * t + k, BLK)
                    if b == 0:
                        pe.wait_ge(lo_ready, PART["pa"] + n + 1)
                    if t == 0:
                        pe.wait_ge(yal, k + 1)
                    if k == 0:
                        free_bank(0, 0, TILE["pa"] + t)
                    last = three(bank[(TILE["pa"] + t) % BANKS][:, 0:S], (PART["pa"] + n) % RING, b, u_hi[:, R + k, :],
                                 u_lo[:, R + k, :], k == 0, k == R - 1)
                    if b == BLK - 1:
                        last.then_inc(part_done, 1)
            pe.wait_ge(y_lo, C)
            tiles(PART["pb"], TILE["pb"], C, u_hi, u_lo)
            tile(0, PART["wo"], TILE["wo"], low=ml)
            for t in range(1, C):
                tile(0, PART["wo"] + t, TILE["wo"] + t)
            stat("post")
            after_norm("ffn", "up", 2 * F1)
            down("down", F1, 0)
            stat("post2")
            after_norm("n0", "hf", 2 * C, columns=True)

            def level_mm(l):
                for g in range(4):
                    if l >= 1:
                        pe.wait_ge(lev_sel, 4 * (l - 1) + g + 1)
                    for j in range(4):
                        c, tok = (4 * g + j) // 2, slice(j % 2 * P, (j % 2 + 1) * P)
                        a, b = (KK, QS) if l == 0 else (EB[l % 2], EB[l % 2])
                        last = mm(bank[4 + g][:, j * P:(j + 1) * P], a[:, c, tok], b[:, c, tok], start=True, stop=True)
                    last.then_inc(lev_mm, 1)

            for l in range(1, LEVELS + 1):
                n = 2 * (l - 1)
                if n < C:
                    token_tile(PART["hi"], TILE["hi"], n, 0)
                    if l == 1:
                        pe.wait_ge(k_ready, C)
                        pe.wait_ge(q_ready, C)
                        pe.wait_ge(col_rms, 1)
                        level_mm(0)
                    token_tile(PART["hi"], TILE["hi"], n, 1)
                else:
                    for t in (n - C, n - C + 1):
                        tile(0, PART["hg"] + t, TILE["hg"] + t)
                pe.wait_ge(x_low, l)
                pe.wait_ge(x_up, l)
                if l < LEVELS:
                    level_mm(l)
            for g in range(2):
                pe.wait_ge(lev_sel, 4 * (LEVELS - 1) + g + 1)
                for j in range(4):
                    c = 4 * g + j
                    last = mm(bank[4 + g][:, j * P:(j + 1) * P], EB[0][:, c, 0:P], EB[0][:, c, P:S], start=True, stop=True)
                last.then_inc(lev_mm, 1)
            pe.wait_ge(lev_sel, 4 * LEVELS)
            pe.wait_ge(px_copied, 2)
            for c in range(C):
                out = bank[5 + c % 3]
                if c >= 3:
                    pe.wait_ge(o_evac, c - 2)

                def it(tok):
                    return flat(INP[:, 4 * tok:4 * tok + 4, :])[:, c * P:(c + 1) * P]
                mm(out[:, 0:P], it(0), PD[:, 2 * c, :], start=True, stop=True)
                mm(out[:, P:S], it(0), PX[:, c, :], start=True, stop=False)
                mm(out[:, P:S], it(1), PD[:, 2 * c + 1, :], start=False, stop=True).then_inc(o_mm, 1)
            tile(0, PART["ho"], TILE["ho"], u_hi, u_lo, low=oh_lo)
            tile(0, PART["ho"] + 1, TILE["ho"] + 1, u_hi, u_lo)
            stat("o")
            for t in range(2, C):
                tile(0, PART["ho"] + t, TILE["ho"] + t, u_hi, u_lo)
            after_norm("f0", "up1", 2 * F2)
            down("down1", F2, F1)
            for n in range(0, C, 2):
                for tok in range(2):
                    token_tile(PART["mv"], TILE["mv"], n, tok, hl_ready if n + tok == 0 else None, H_COUNT["n1"])
                    if n + tok == 0:
                        stat("n1", columns=True)

            def moba_scores(h):
                out = bank[4 + h % 2]
                pe.wait_ge(evacuated, TILE["mqk"] + 2 * h + 2)
                pe.wait_ge(s_evac, 2 * (H_FOX + h) - 2)
                mm(out[:, 0:P], MQ[:, h, 0:P], MK[:, h, 0:P], start=True, stop=True)
                mm(out[:, P:EXT], MQ[:, h, P:S], MK[:, h, :], start=True, stop=True).then_inc(s_mm, 1)

            def moba_values(h):
                pe.wait_ge(y_lo, C + h)
                values(H_FOX + h, bank[7][:, 0:S], lambda kb: flat(MV[:, 4 * kb:4 * kb + 4, :])[:, h * P:(h + 1) * P])

            for s in range(2 * C):
                tile(0, PART["mqk"] + s, TILE["mqk"] + s)
                if s % 2 == 0 and s >= 4:
                    transposes(H_FOX + (s - 4) // 2)
                if s % 2 == 0 and s >= 2:
                    moba_scores((s - 2) // 2)
                if s % 2 and s >= 5:
                    moba_values((s - 5) // 2)
            transposes(H_FOX + 6)
            moba_scores(7)
            moba_values(6)
            first = (0, PART["mo"], TILE["mo"], u_hi, u_lo, y_lo, C)
            tile(*first, blocks=range(0, 6))
            transposes(H_FOX + 7)
            tile(*first, blocks=range(6, 7))
            moba_values(7)
            tile(*first, blocks=range(7, BLK))
            for t in range(1, C):
                tile(0, PART["mo"] + t, TILE["mo"] + t, u_hi, u_lo)
            after_norm("f1", "up2", 2 * F2)
            down("down2", F2, F1 + F2)
            stat("final")


def bucket_of(dist):
    import math
    import numpy as np
    exact = BUCKETS // 2
    n = np.maximum(dist, 0)
    nf = np.maximum(n, exact).astype(np.float32)
    large = exact + (np.log(nf / np.float32(exact)) / np.float32(math.log(1024 / exact))
                     * np.float32(BUCKETS - exact)).astype(np.int32)
    return np.where(n < exact, n, np.minimum(large, BUCKETS - 1))


def kernel(**inputs):
    import numpy as np
    import concourse.bacc as bacc
    from concourse.bass_utils import run_bass_kernel_spmd

    a = {k: np.asarray(x) for k, x in inputs.items()}

    def parts_of(w):
        k, n = w.shape
        per = -(-k // (BLK * P))
        out = np.zeros((n // P, per, P, BLK, P), np.float32)
        for j in range(per):
            rows = w[j * BLK * P:(j + 1) * BLK * P]
            kb = rows.shape[0] // P
            out[:, j, :, :kb, :] = rows.reshape(kb, P, n // P, P).transpose(2, 1, 0, 3)
        return out.reshape(-1, P, BLK * P)

    def packed(w):
        k, n = w.shape
        b = w.reshape(k // P, P, n // P, P).transpose(2, 0, 1, 3).reshape(-1, BLK, P, P)
        return b.transpose(0, 2, 1, 3).reshape(-1, P, BLK * P)

    def gate_parts(w):
        out = np.zeros((2, 2, P, BLK, P), np.float32)
        for g in range(2):
            dense = np.zeros((5 * P, 5 * P), np.float32)
            for h in range(8):
                s = slice(h * RNN_BLOCK, (h + 1) * RNN_BLOCK)
                dense[s, s] = w[8 * g + h]
            for n, tiles in enumerate(GATE_PARTS):
                blocks = [(f, o) for o in tiles for f in GATE_IN[o]]
                for b, (f, o) in enumerate(blocks):
                    out[g, n, :, b, :] = dense[f * P:(f + 1) * P, o * P:(o + 1) * P]
        return out.reshape(4, P, BLK * P)

    def paired(w):
        k, n = w.shape
        return w.reshape(k, 2, n // (2 * P), P).transpose(0, 2, 1, 3).reshape(k, n)

    w_in = a["w_in"][0]
    o = np.cumsum([0, D_RNN, D_RNN, D, D, D, H_FOX, D, D])
    xa, ga, q, k, v, f, sa, sb_ = (w_in[:, o[i]:o[i + 1]] for i in range(8))
    hq, hf, hi_, hg = (a["hgrn_w_in_2"][0][:, i * D:(i + 1) * D] for i in range(4))
    mq, mk, mv = (a["moba_w_in_2"][0][:, i * D:(i + 1) * D] for i in range(3))
    stream = np.concatenate([
        parts_of(xa), parts_of(v), gate_parts(a["w_rg_x"][0]), gate_parts(a["w_rg_a"][0]), parts_of(ga),
        parts_of(paired(np.concatenate([q, k], axis=1))), parts_of(sa), parts_of(sb_), packed(a["w_proj_a"][0]), parts_of(a["w_proj_b"][0]),
        parts_of(a["w_out"][0]), parts_of(paired(a["w_up"][0])), parts_of(a["w_down"][0]),
        parts_of(hf), parts_of(hq), parts_of(hi_), parts_of(hg), parts_of(a["hgrn_w_out_2"][0]),
        parts_of(paired(a["ffn_w13_2"][0])), parts_of(a["ffn_w2_2"][0]),
        parts_of(mv), parts_of(paired(np.concatenate([mq, mk], axis=1))), parts_of(a["moba_w_out_2"][0]),
        parts_of(paired(a["ffn_w13_2"][1])), parts_of(a["ffn_w2_2"][1])])
    assert stream.shape[0] == PARTS

    def cols(x):
        return x.reshape(-1, P).T

    pad = np.zeros(P, np.float32)
    pad[:H_FOX] = a["b_forget"][0]
    par = np.concatenate([
        cols(a["mix_norm_pre"][0]), cols(a["mix_norm_post"][0]), cols(a["conv_a_w"][0]), cols(a["conv_a_b"][0]),
        cols(a["b_rg_a"][0]), cols(a["b_rg_x"][0]), cols(a["lru_lambda"][0]), cols(a["b_merge"][0]),
        cols(a["ffn_norm_pre"][0]), cols(a["ffn_norm_post"][0]), cols(paired(a["conv_f_w"][0])),
        cols(paired(a["conv_f_b"])), cols(a["norm_mix_2"]), cols(a["norm_ffn_2"]), cols(a["hgrn_lb_logits_2"]),
        cols(a["hgrn_out_norm_2"][0]), cols(a["final_norm_2"]), pad[:, None]], axis=1)
    par = np.ascontiguousarray(par)
    assert par.shape == (P, NCOL)

    x_t = np.ascontiguousarray(a["x"][0].T.reshape(C, P, S).transpose(1, 0, 2))
    wf = np.ascontiguousarray(f.reshape(C, P, H_FOX).transpose(1, 0, 2))

    onehot = (np.arange(BUCKETS)[:, None] == bucket_of(255 - np.arange(EXT))[None, :]).astype(np.float32)
    ident = np.eye(P, dtype=np.float32)
    causal = np.where(np.arange(P)[None, :] <= np.arange(P)[:, None], 0.0, NEG).astype(np.float32)
    mask = np.concatenate([causal, np.zeros((P, P), np.float32), causal], axis=1)
    s, t = np.arange(P)[:, None], np.arange(P)[None, :]
    lmask = np.stack([s == t] + [(s >> l == t >> l) & (s >> (l - 1) != t >> (l - 1)) & (s < t)
                                 for l in range(1, LEVELS)], axis=1).astype(np.int32)

    arrays = {"stream": stream, "par": par, "x_t": x_t, "wf": wf,
              "table": np.ascontiguousarray(a["rel_bias_table_2"]), "onehot": onehot, "ident": ident,
              "mask": mask, "lmask": np.ascontiguousarray(lmask)}
    nc = bacc.Bacc("TRN2", target_bir_lowering=False, num_devices=1)
    aps = [nc.dram_tensor("in_" + n, x.shape, mybir.dt.from_np(x.dtype), kind="ExternalInput").ap() for n, x in arrays.items()]
    out = nc.dram_tensor("out", (P, C, S), F32, kind="ExternalOutput").ap()
    build(nc, *aps, out)
    r = run_bass_kernel_spmd(nc, [{"in_" + n: x for n, x in arrays.items()}], core_ids=[0])
    y = r.results[0]["out"]
    return np.ascontiguousarray(y.transpose(2, 1, 0).reshape(1, S, D))
```

```python
from contextlib import ExitStack

import concourse.bass as bass
from concourse import mybir

F32 = mybir.dt.float32
F32R = mybir.dt.float32r
I32 = mybir.dt.int32
ACT = mybir.ActivationFunctionType
ALU = mybir.AluOpType
AX = mybir.AxisListType

P = 128
S = 256
D = 1024
C = D // P
D_RNN = 1280
R = D_RNN // P
RNN_BLOCK = 80
H_FOX, DH_FOX = 16, 64
H_MOBA, DH_MOBA = 8, 128
BUCKETS = 32
F1 = 3 * D // P
F2 = 2816 // P
EPS = 1e-6
LRU_C = 8.0
NEG = -1.0e30
BLK = 8
RING = 4
BANKS = 4
HI_AHEAD, LO_AHEAD = 4, 3

PHASES = [("xa", R, R), ("v", C, C), ("gates", 8, 0), ("ga", R, R), ("qk", 2 * C, 2 * C), ("sa", C, C), ("sb", C, C),
          ("pa", R, C), ("pb", C, C), ("wo", C, C), ("up", 2 * F1, 2 * F1), ("down", F1, C),
          ("hf", C, C), ("hq", C, C), ("hi", C, C), ("hg", C, C), ("ho", C, C),
          ("up1", 2 * F2, 2 * F2), ("down1", 24, C), ("mv", C, C), ("mqk", 2 * C, 2 * C), ("mo", C, C),
          ("up2", 2 * F2, 2 * F2), ("down2", 24, C)]
PART, TILE = {}, {}
_p = _t = 0
for _name, _parts, _tiles in PHASES:
    PART[_name], TILE[_name] = _p, _t
    _p, _t = _p + _parts, _t + _tiles
PARTS, TILES = _p, _t

GATE_IN = [[0, 1], [0, 1, 2], [1, 2, 3], [2, 3, 4], [3, 4]]
GATE_PARTS = [[0, 1, 2], [3, 4]]

COLS, NCOL = {}, 0
for _name, _n in [("mix_pre", C), ("mix_post", C), ("conv_w", 4 * R), ("conv_b", R), ("b_a", R), ("b_x", R),
                  ("lam", R), ("b_merge", 2 * C), ("ffn_pre", C), ("ffn_post", C), ("fconv_w", 3 * 2 * F1),
                  ("fconv_b", 2 * F1), ("norm_mix", 2 * C), ("norm_ffn", 2 * C), ("lb", 2 * C), ("out_norm", C),
                  ("final", C), ("b_forget", 1)]:
    COLS[_name] = NCOL
    NCOL += _n

EXT = 3 * P
LEVELS = 8

UNITS = 82


def build(nc, stream, par_d, x_d, wf_d, table_d, onehot_d, ident_d, mask_d, lmask_d, out_d):
    scr = nc.dram_tensor("bias_rows", [H_MOBA, P, EXT], F32, kind="Internal")
    with ExitStack() as ctx:
        def sb(name, shape, dt=F32):
            return ctx.enter_context(nc.sbuf_tensor(name, shape, dt))

        def sem(name):
            return ctx.enter_context(nc.semaphore(name))

        raw = sb("raw", [P, RING, BLK * P])
        w_hi = sb("w_hi", [P, RING, BLK * P], F32R)
        w_lo = sb("w_lo", [P, RING, BLK * P], F32R)
        h_hi = sb("h_hi", [P, C, S], F32R)
        h_lo = sb("h_lo", [P, C, S], F32R)
        u_hi = sb("u_hi", [P, F1, S], F32R)
        u_lo = sb("u_lo", [P, F1, S], F32R)
        F = sb("work", [P, UNITS, S])
        par = sb("par", [P, NCOL])
        der = sb("derived", [P, 66])
        ident = sb("ident", [P, P])
        mask = sb("mask", [P, EXT])
        ones = sb("ones", [P, P])
        wf = sb("wf", [P, C * H_FOX])
        att_s = sb("att_s", [P, 2, EXT])
        att_pt = sb("att_pt", [P, 2, EXT])
        stat_s = sb("att_stat", [P, 2, 8])
        ncum = sb("ncum", [H_FOX, S])
        cum_t = sb("cum_t", [P, 2, H_FOX])
        bank = [ctx.enter_context(nc.psum_tensor(f"bank{i}", [P, 512], F32)) for i in range(8)]

        def flat(ap):
            return ap.rearrange("p u t -> p (u t)")

        X = F[:, 52:60, :]
        RSTD = F[:, 81, :]
        SQT, ACC, SQL = F[:, 24, :], F[:, 25, :], F[:, 26, :]
        M = F[:, 12:20, :]
        SQ, HT = F[:, 60:68, :], F[:, 32:40, :]
        ext = flat(F[0:H_MOBA, 60:62, :])[:, 0:EXT]
        onehot = flat(F[0:BUCKETS, 44:46, :])[:, 0:EXT]
        table = F[0:BUCKETS, 46, 0:H_MOBA]
        XA, GA, XC = F[:, 0:10, :], F[:, 0:10, :], F[:, 10:20, :]
        Q, K, V = F[:, 20:28, :], F[:, 28:36, :], F[:, 36:44, :]
        WF_HI, WF_LO = (u[:, 2 * R + 2, 0:C * H_FOX] for u in (u_hi, u_lo))
        CUM_HI, CUM_LO = u_hi[0:H_FOX, 2 * R, :], u_lo[0:H_FOX, 2 * R, :]
        EYE_R = u_hi[0:H_FOX, 2 * R + 1, 0:H_FOX]
        SGA, SGB = F[:, 44:52, :], F[:, 52:60, :]
        RG, IG, ASQ = F[:, 60:70, :], F[:, 70:80, :], F[:, 48:50, :]
        PRA, PRB = F[:, 70:78, :], F[:, 0:8, :]
        UB, YB, GB, PB, GR = F[:, 0:4, :], F[:, 4:8, :], F[:, 8:10, :], F[:, 10:12, :], F[:, 0:2, :]
        FG, CUM, KK, QS = F[:, 0:8, :], F[:, 8:16, :], F[:, 16:24, :], F[:, 24:32, :]
        INP, OG = F[:, 32:40, :], F[:, 40:48, :]
        LM = flat(F[:, 48:52, :]).bitcast(I32).rearrange("p (l t) -> p l t", l=LEVELS)
        EB = [F[:, 0:8, :], F[:, 60:68, :]]
        PD = F[:, 68:76, :].rearrange("p u (z t) -> p (u z) t", z=2)
        PX = F[:, 76:80, :].rearrange("p u (z t) -> p (u z) t", z=2)
        ONES_ROW = F[:, 80, :]
        OC, OH = F[:, 8:16, :], F[:, 16:24, :]
        MQ, MK, MV = F[:, 0:8, :], F[:, 8:16, :], F[:, 32:40, :]
        BIAS = flat(F[:, 68:80, :]).rearrange("p (h e) -> p h e", h=H_MOBA)

        def col(name, c=0):
            return par[:, COLS[name] + c:COLS[name] + c + 1]

        def dcol(name, e):
            return par[:, bass.ds(e + COLS[name], 1)]

        D_SP, D_NSP, D_LB, D_1LB, D_T, D_E, D_EPS = 0, 10, 20, 28, 36, 46, 63
        touch = der[:, 62:63]
        RCOL = der[:, 64:66]

        landed = [sem(f"part_landed{i}") for i in range(RING)]
        hi_ready, lo_ready = sem("hi_ready"), sem("lo_ready")
        part_done, evacuated = sem("part_done"), sem("evacuated")
        x_in = [sem(f"x_half_in{i}") for i in range(2)]
        par_in, wf_in, tab_in, cst_in, x_back, lm_in, bias_in = (
            sem(n) for n in ("par_in", "wf_in", "table_in", "const_in", "x_back", "lmask_in", "bias_in"))
        ext_out, out_done = sem("bias_rows_out"), sem("out_done")
        ones_ready = sem("ones_ready")
        sq_ready, stat_done, rms_ready, rstd_ready = (
            sem(n) for n in ("square_ready", "stat_done", "rms_ready", "rstd_ready"))
        ht_ready, hh_ready, hl_ready, x_ready = sem("h_ready"), sem("h_hi_ready"), sem("h_lo_ready"), sem("x_ready")
        post_t, post_pool = sem("post_scaled"), sem("post_scaled_by_pool")
        ext_mm, ext_ready = sem("bias_rows_made"), sem("bias_rows_ready")
        act_step, dve_step, pool_step = sem("act_step"), sem("dve_step"), sem("pool_step")
        der_ready, sp_ln, lb_exp = sem("derived_ready"), sem("softplus_ln"), sem("lb_exp")
        f_mm, f_ln, cum_ready, cumt_mm, cumt_ready, cum_split = (
            sem(n) for n in ("f_mm", "f_ln", "cum_ready", "cum_t_mm", "cum_t_ready", "cum_split"))
        tap_done, taps_done, xch_ready, xcl_ready = (
            sem(n) for n in ("tap_done", "taps_done", "xc_hi_ready", "xc_lo_ready"))
        gates_evac, ix_done, tanh_done, decay_done, gain_done, root_done, scan_done, ya_done, yah, yal = (
            sem(n) for n in ("gates_evac", "ix_done", "tanh_done", "decay_done", "gain_done", "root_done",
                             "scan_done", "ya_done", "ya_hi_ready", "ya_lo_ready"))
        s_mm, s_evac, mx_done, negmax, exp_done, rsum_done, p_ready, pt_mm, pt_copied, pv_mm, y_hi, y_lo = (
            sem(n) for n in ("scores_mm", "scores_evac", "max_done", "negmax_ready", "exp_done", "rsum_ready",
                             "probs_ready", "probs_t_mm", "probs_t_copied", "pv_mm", "y_hi_ready", "y_lo_ready"))
        merged, mh, ml = sem("merged"), sem("merged_hi"), sem("merged_lo")
        pair_free, gate_ready, uh_ready, ul_ready = (
            sem(n) for n in ("pair_free", "gate_ready", "u_hi_ready", "u_lo_ready"))
        f_ready, k_ready, logf_ready, hcum_ready = sem("f_ready"), sem("k_ready"), sem("logf_ready"), sem("hcum_ready")
        pd_zero, one_row = sem("pd_zeroed"), sem("ones_row_ready")
        arg_ready, dec_ready, x_low, x_up, lev_mm, lev_sel, px_copied = (
            sem(n) for n in ("level_arg", "level_decay", "level_keys", "level_queries", "level_mm", "level_taken",
                             "cross_copied"))
        o_mm, o_evac, o_gated = sem("o_mm"), sem("o_evac"), sem("o_gated")
        bias_masked = sem("bias_masked")
        acc_ready, col_rms, col_ready = sem("squares_summed"), sem("column_rms"), sem("column_rstd")
        u_conv, f_raw, q_ready, og_ready = sem("conv_tap_ready"), sem("forget_sigmoid"), sem("q_ready"), sem("og_ready")
        oh_hi, oh_lo = sem("o_hi_ready"), sem("o_lo_ready")
        tap_step, col_mm, ga_normed = sem("tap_step"), sem("column_mm"), sem("ga_normed")
        arg_up, last_sq, pair_sum, xc_tap = (
            sem(n) for n in ("level_arg_later", "last_square", "squares_paired", "xc_tap_ready"))
        wf_split, f_normed, sg_ready, ht_pool, fin_scaled = (
            sem(n) for n in ("wf_split", "f_normed", "merge_gate_ready", "result_by_pool", "result_scaled"))
        square_done, b_done, gelu_done = (sem(n) for n in ("decay_squared", "b_done", "gelu_done"))

        block = ctx.enter_context(nc.Block())

        def lin(i, m, c):
            return c if isinstance(i, int) else i * m + c

        class Chain:

            def __init__(self, eng, s):
                self.eng, self.s, self.n = eng, s, 0

            def wait(self, ins):
                ins.then_inc(self.s, 1)
                self.n += 1
                self.eng.wait_ge(self.s, self.n)

        NORMS = {n: i for i, n in enumerate(["mix", "post", "ffn", "post2", "n0", "o", "f0", "n1", "f1", "final"])}
        X_SRC = {"ffn": (x_ready, 0), "n0": (x_ready, C), "f0": (x_ready, 2 * C), "n1": (evacuated, TILE["down1"]),
                 "f1": (evacuated, TILE["mo"]), "final": (evacuated, TILE["down2"])}
        PAIR_SUMS = ["mix", "ffn", "n0"]
        POOL_SUMS = ["post", "post2", "o", "f0", "n1", "f1", "final"]
        LAST_BY_ACT = ["post", "post2", "final"]
        NEXT = {"mix": "mix_pre", "ffn": "ffn_pre", "n0": "norm_mix", "f0": "norm_ffn", "n1": "norm_mix",
                "f1": "norm_ffn"}
        GAIN0 = {"mix": 0, "ffn": 0, "n0": 0, "f0": 0, "n1": C, "f1": C}
        SCANS = {}
        for t in range(R):
            SCANS.setdefault(H_FOX + 5 + (2 * t + 1) // 3, []).append(t)
        H_COUNT = {n: 8 * i for i, n in enumerate(["mix", "ffn", "n0", "f0", "n1", "f1"])}

        @block.sync
        def _(sp):
            sp.dma_start(par[:, :], par_d).then_inc(par_in, 16)
            for n in range(RING):
                if n < 2:
                    half = slice(n * C // 2, (n + 1) * C // 2)
                    sp.dma_start(X[:, half, :], x_d[:, half, :]).then_inc(x_in[n], 16)
                sp.dma_start(raw[:, n, :], stream[n]).then_inc(landed[n], 16)
            loops = (PARTS - RING) // RING

            def load(i, c):
                sp.wait_ge(lo_ready, lin(i, RING, c) - RING + 1)
                src = (stream[bass.ds(lin(i, RING, c), 1), :, :].rearrange("o p f -> p (o f)")
                       if not isinstance(i, int) else stream[c])
                sp.dma_start(raw[:, c % RING, :], src).then_inc(landed[c % RING], 16)

            with sp.Fori(1, 1 + loops) as i:
                for c in range(RING):
                    load(i, c)
            for c in range(RING * (1 + loops), PARTS):
                load(0, c)

        @block.scalar
        def _(act):
            A = nc.scalar.activation

            def hi(i, m, c):
                if isinstance(i, int) and c >= PARTS:
                    return
                slot = c % RING
                act.wait_ge(landed[slot], lin(i, 16 * m // RING, 16 * (c // RING + 1)))
                A(w_hi[:, slot, :], raw[:, slot, :], ACT.Copy).then_inc(hi_ready, 1)

            def multiplied(c, i=0, m=0):
                act.wait_ge(part_done, lin(i, m, c + 1))

            def out_of(t):
                return bank[t % BANKS][:, 0:S]

            def rms(norm, columns=False):
                act.wait_ge(stat_done, NORMS[norm] + 1)
                A(RSTD, bank[4][:, 0:S], ACT.Sqrt, scale=1.0 / D, bias=der[:, D_EPS:D_EPS + 1]).then_inc(rms_ready, 1)
                if columns:
                    A(RCOL, bank[4][:, S:S + 2], ACT.Sqrt, scale=1.0 / D,
                      bias=der[:, D_EPS:D_EPS + 1]).then_inc(col_rms, 1)

            def split(norm, c):
                if norm == "mix":
                    act.wait_ge(x_in[2 * c // C], 16)
                else:
                    act.wait_ge(X_SRC[norm][0], X_SRC[norm][1] + c + 1)
                A(h_hi[:, c, :], X[:, c, :], ACT.Copy, scale=col(NEXT[norm], GAIN0[norm] + c)).then_inc(hh_ready, 1)
                if norm in ("ffn", "n0"):
                    A(SQ[:, c, :], X[:, c, :], ACT.Square).then_inc(sq_ready, 1)

            act.wait_ge(der_ready, 1)
            A(touch, touch, ACT.Sqrt)
            act.wait_ge(par_in, 16)
            for c in range(C):
                split("mix", c)
                if c % 4 == 3:
                    hi(0, 0, c // 4)
            for c in range(C):
                A(SQ[:, c, :], X[:, c, :], ACT.Square).then_inc(sq_ready, 1)
                if c % 4 == 3:
                    hi(0, 0, 2 + c // 4)
            rms("mix")
            for p in range(R // 2):
                pair = (2 * p, 2 * p + 1)
                multiplied(PART["xa"] + 2 * p)
                hi(0, 0, PART["xa"] + 2 * p + HI_AHEAD)
                for t in pair:
                    act.wait_ge(evacuated, TILE["xa"] + t + 1)
                    A(XC[:, t, :], XA[:, t, :], ACT.Identity, scale=col("conv_w", 3 * R + t),
                      bias=col("conv_b", t)).then_inc(xc_tap, 1)
                multiplied(PART["xa"] + 2 * p + 1)
                hi(0, 0, PART["xa"] + 2 * p + 1 + HI_AHEAD)
                if p == 0:
                    act.wait_ge(ext_mm, 1)
                    A(ext, bank[5][0:H_MOBA, 0:EXT], ACT.Copy).then_inc(ext_ready, 1)
                for t in pair:
                    if p >= 1:
                        act.wait_ge(taps_done, t - 1)
                        A(u_hi[:, t - 2, :], XC[:, t - 2, :], ACT.Copy).then_inc(xch_ready, 1)
            for t in (R - 2, R - 1):
                act.wait_ge(taps_done, t + 1)
                A(u_hi[:, t, :], XC[:, t, :], ACT.Copy).then_inc(xch_ready, 1)

            def exponentials():
                act.wait_ge(f_normed, 1)
                A(e_lam, lam, ACT.Abs).then_inc(act_step, 1)
                A(z, z, ACT.Identity, bias=par[0:H_FOX, COLS["b_forget"]:COLS["b_forget"] + 1]).then_inc(act_step, 1)
                act.wait_ge(act_step, 2)
                A(az, z, ACT.Abs).then_inc(act_step, 1)
                act.wait_ge(der_ready, 3)
                for r in range(2):
                    e = der[:, D_E + C * r:D_E + C * r + C]
                    A(e, e, ACT.Exp).then_inc(lb_exp, 1)
                act.wait_ge(act_step, 3)
                A(e_lam, e_lam, ACT.Exp, scale=-1.0).then_inc(act_step, 1)
                A(az, az, ACT.Exp, scale=-1.0).then_inc(act_step, 1)

            def logarithms():
                act.wait_ge(act_step, 5)
                A(az, az, ACT.Ln, bias=1.0).then_inc(f_ln, 1)
                A(der[:, D_SP:D_SP + R], e_lam, ACT.Ln, bias=1.0).then_inc(sp_ln, 1)

            lam, e_lam = par[:, COLS["lam"]:COLS["lam"] + R], der[:, D_T:D_T + R]
            z, az = att_s[0:H_FOX, 0, 0:S], att_s[0:H_FOX, 1, 0:S]

            def token_pair(name, n, dst, scale):
                multiplied(PART[name] + n + 1)
                for tok in range(2):
                    src = out_of(TILE[name] + n + tok)
                    A(dst[:, 4 * tok + n // 2, :], src, ACT.Copy, scale=scale[:, tok:tok + 1]).then_inc(evacuated, 1)
                for j in range(2):
                    hi(0, 0, PART[name] + n + j + HI_AHEAD)

            act.wait_ge(col_ready, 1)
            for n in range(0, C, 2):
                token_pair("v", n, V, RCOL)
                if n == 2:
                    exponentials()
                if n == 4:
                    logarithms()
                    A(touch, touch, ACT.Sigmoid)
            act.wait_ge(ext_out, 16)
            for n in range(8):
                multiplied(PART["gates"] + n)
                m, g = n // 4, n // 2 % 2
                for j, o in enumerate(GATE_PARTS[n % 2]):
                    src = bank[4 + 2 * (n % 2) + j // 2][:, j % 2 * S:j % 2 * S + S]
                    dst, b = (IG, "b_x") if m == 0 else (RG, "b_a")
                    A(dst[:, 5 * g + o, :], src, ACT.Sigmoid, bias=col(b, 5 * g + o)).then_inc(gates_evac, 1)
                hi(0, 0, PART["gates"] + n + HI_AHEAD)
            act.wait_ge(der_ready, 4)

            def lru_decay(t):
                act.wait_ge(ix_done, t + 1)
                act.wait_ge(gates_evac, R + t + 1)
                A(XC[:, t, :], RG[:, t, :], ACT.Tanh, scale=der[:, D_SP + t:D_SP + t + 1]).then_inc(tanh_done, 1)
                act.wait_ge(tanh_done, t + 1)
                A(RG[:, t, :], RG[:, t, :], ACT.Exp, scale=der[:, D_NSP + t:D_NSP + t + 1]).then_inc(decay_done, 1)

            for t in range(R):
                lru_decay(t)
                multiplied(PART["ga"] + t)
                A(GA[:, t, :], out_of(TILE["ga"] + t), ACT.Copy).then_inc(evacuated, 1)
                hi(0, 0, PART["ga"] + t + HI_AHEAD)

            def lru_gelu():
                act.wait_ge(ga_normed, R)
                A(GA, GA, ACT.Gelu_apprx_tanh).then_inc(gelu_done, 1)

            def lru_root():
                act.wait_ge(gain_done, R)
                A(XC, XC, ACT.Sqrt).then_inc(root_done, 1)

            def lru_out(t):
                act.wait_ge(ya_done, t + 1)
                A(u_hi[:, R + t, :], GA[:, t, :], ACT.Copy).then_inc(yah, 1)

            def exps(n):
                b = n % 2
                act.wait_ge(negmax, n + 1)
                for j, (a, e) in enumerate([(0, P), (P, EXT)]):
                    A(att_s[:, b, a:e], att_s[:, b, a:e], ACT.Exp, bias=stat_s[:, b, 2 + j:3 + j],
                      accum_out=stat_s[:, b, 4 + j:5 + j]).then_inc(exp_done, 1)

            def copy_pt(n):
                act.wait_ge(pt_mm, n + 1)
                if n >= 2:
                    act.wait_ge(pv_mm, n - 1)
                A(att_pt[:, n % 2, :], bank[6][:, 0:EXT], ACT.Copy).then_inc(pt_copied, 1)

            def head_out(n, t):
                act.wait_ge(pv_mm, n + 1)
                A(u_hi[:, t, :], bank[7][:, 0:S], ACT.Copy).then_inc(y_hi, 1)

            def merge_gate(n):
                act.wait_ge(evacuated, TILE["sa"] + n + 1)
                dst = (SGA if n < C else SGB)[:, n % C, :]
                A(dst, dst, ACT.Sigmoid, bias=col("b_merge", n)).then_inc(sg_ready, 1)

            act.wait_ge(der_ready, 5)
            gates_done = 0
            for s in range(4 * C):
                n = s - 6
                if 0 <= n < H_FOX and n % 2:
                    head_out(n, n // 2)
                if 0 <= s - 3 < H_FOX:
                    exps(s - 3)
                multiplied(PART["qk"] + s)
                hi(0, 0, PART["qk"] + s + HI_AHEAD)
                for n in range(gates_done, min(gates_done + 2, s - 2 * C + 1) if s > H_FOX + 3 else 0):
                    merge_gate(n)
                    gates_done = n + 1
                if 0 <= s - 4 < H_FOX:
                    copy_pt(s - 4)
                if s == 1:
                    lru_gelu()
                if s == H_FOX + 3:
                    lru_root()
                for t in SCANS.get(s - 2, []):
                    lru_out(t)

            for t in range(R):
                multiplied(PART["pa"] + t)
                hi(0, 0, PART["pa"] + t + HI_AHEAD)
            for t in range(C):
                multiplied(PART["pb"] + t)
                hi(0, 0, PART["pb"] + t + HI_AHEAD)
                act.wait_ge(merged, t + 1)
                A(h_hi[:, t, :], PRA[:, t, :], ACT.Copy).then_inc(mh, 1)
            for t in range(C):
                multiplied(PART["wo"] + t)
                if t == 0:
                    A(touch, touch, ACT.Sqrt)
                if t == C - 1:
                    A(SQL, out_of(TILE["wo"] + t), ACT.Square).then_inc(last_sq, 1)
                A(M[:, t, :], out_of(TILE["wo"] + t), ACT.Copy).then_inc(evacuated, 1)
                if t == C - 1:
                    rms("post")
                hi(0, 0, PART["wo"] + t + HI_AHEAD)
            for c in range(C):
                split("ffn", c)
            rms("ffn")

            with act.Fori(0, 2 * F1 // 4) as i:
                A(touch, touch, ACT.Gelu_apprx_tanh)
                for p in range(2):
                    multiplied(PART["up"] + 2 * p, i, 4)
                    hi(i, 4, PART["up"] + 2 * p + HI_AHEAD)
                    act.wait_ge(evacuated, lin(i, 4, TILE["up"] + 2 * p + 2))
                    act.wait_ge(pair_free, lin(i, 2, p + 1))
                    for j in (2 * p, 2 * p + 1):
                        A(YB[:, j, :], UB[:, j, :], ACT.Identity, scale=dcol("fconv_w", i * 4 + (2 * 2 * F1 + j)),
                          bias=dcol("fconv_b", i * 4 + j)).then_inc(u_conv, 1)
                    multiplied(PART["up"] + 2 * p + 1, i, 4)
                    hi(i, 4, PART["up"] + 2 * p + 1 + HI_AHEAD)
                    act.wait_ge(taps_done, lin(i, 4, R + 2 * p + 1))
                    A(GB[:, p, :], YB[:, 2 * p, :], ACT.Gelu_apprx_tanh).then_inc(gate_ready, 1)
            for j in range(F1):
                multiplied(PART["down"] + j)
                if j == F1 - 1:
                    A(SQL, out_of(TILE["down"] + j // 3), ACT.Square).then_inc(last_sq, 1)
                if j % 3 == 2:
                    A(M[:, j // 3, :], out_of(TILE["down"] + j // 3), ACT.Copy).then_inc(evacuated, 1)
                if j == 0:
                    A(touch, touch, ACT.Sqrt)
                if j == F1 - 1:
                    rms("post2")
                hi(0, 0, PART["down"] + j + HI_AHEAD)
            for c in range(C):
                split("n0", c)
            rms("n0")

            for t in range(C):
                act.wait_ge(evacuated, TILE["hf"] + t + 1)
                A(FG[:, t, :], FG[:, t, :], ACT.Sigmoid).then_inc(f_raw, 1)
                multiplied(PART["hf"] + t)
                hi(0, 0, PART["hf"] + t + HI_AHEAD)
            for t in range(C):
                if t == 2:
                    act.wait_ge(k_ready, C)
                    A(CUM, FG, ACT.Ln).then_inc(logf_ready, 1)
                act.wait_ge(evacuated, TILE["hq"] + t + 1)
                A(QS[:, t, :], QS[:, t, :], ACT.Silu).then_inc(q_ready, 1)
                multiplied(PART["hq"] + t)
                hi(0, 0, PART["hq"] + t + HI_AHEAD)
            A(touch, touch, ACT.Exp)
            act.wait_ge(col_ready, 2)
            for l in range(1, LEVELS + 1):
                e, n = EB[l % 2], 2 * (l - 1)
                act.wait_ge(arg_ready, l)
                act.wait_ge(arg_up, l)
                A(e, e, ACT.Exp).then_inc(dec_ready, 1)
                if l == LEVELS:
                    act.wait_ge(evacuated, TILE["hg"] + C - 2)
                    A(OG[:, 0:C - 2, :], OG[:, 0:C - 2, :], ACT.Sigmoid).then_inc(og_ready, 1)
                if n < C:
                    token_pair("hi", n, INP, RCOL)
                else:
                    for j in range(2):
                        if l == LEVELS and j == 1:
                            for g in range(2):
                                act.wait_ge(lev_mm, 4 + 2 * (LEVELS - 1) + g + 1)
                                A(PX[:, 4 * g:4 * g + 4, :], bank[4 + g][:, :].rearrange("p (h t) -> p h t", h=4),
                                  ACT.Copy).then_inc(px_copied, 1)
                        multiplied(PART["hg"] + n - C + j)
                        hi(0, 0, PART["hg"] + n - C + j + HI_AHEAD)
            act.wait_ge(evacuated, TILE["hg"] + C)
            A(OG[:, C - 2:C, :], OG[:, C - 2:C, :], ACT.Sigmoid).then_inc(og_ready, 1)
            for c in range(C):
                act.wait_ge(o_mm, c + 1)
                A(OC[:, c, :], bank[5 + c % 3][:, 0:S], ACT.Copy).then_inc(o_evac, 1)
                if c >= 1:
                    act.wait_ge(o_gated, c)
                    A(u_hi[:, c - 1, :], OH[:, c - 1, :], ACT.Copy).then_inc(oh_hi, 1)
            act.wait_ge(o_gated, C)
            A(u_hi[:, C - 1, :], OH[:, C - 1, :], ACT.Copy).then_inc(oh_hi, 1)

            def feed(name, per, norm):
                for j in range(per * C):
                    multiplied(PART[name] + j)
                    if j < per * C - 1:
                        hi(0, 0, PART[name] + j + HI_AHEAD)
                    if j % per == per - 1:
                        split(norm, j // per)
                hi(0, 0, PART[name] + per * C - 1 + HI_AHEAD)

            def swiglu(name):
                with act.Fori(0, 2 * F2 // 4) as i:
                    A(touch, touch, ACT.Silu)
                    for j in range(4):
                        multiplied(PART[name] + j, i, 4)
                        if j % 2:
                            act.wait_ge(evacuated, lin(i, 4, TILE[name] + j))
                            A(GB[:, j // 2, :], GR[:, j // 2, :], ACT.Silu).then_inc(gate_ready, 1)
                        hi(i, 4, PART[name] + j + HI_AHEAD)

            for j in range(2):
                multiplied(PART["ho"] + j)
                hi(0, 0, PART["ho"] + j + HI_AHEAD)
            rms("o")
            for j in range(C):
                if j >= 2:
                    multiplied(PART["ho"] + j)
                    if j < C - 1:
                        hi(0, 0, PART["ho"] + j + HI_AHEAD)
                split("f0", j)
            hi(0, 0, PART["ho"] + C - 1 + HI_AHEAD)
            rms("f0")
            swiglu("up1")
            feed("down1", 3, "n1")
            rms("n1", columns=True)
            act.wait_ge(col_ready, 3)
            for n in range(0, C, 2):
                token_pair("mv", n, MV, RCOL)
            for s in range(2 * C):
                n = (s - 2) // 2
                if s % 2 == 0 and s >= 6:
                    head_out(H_FOX + n - 2, n - 2)
                if s % 2 and s >= 3:
                    exps(H_FOX + (s - 3) // 2)
                multiplied(PART["mqk"] + s)
                hi(0, 0, PART["mqk"] + s + HI_AHEAD)
                if s % 2 == 0 and s >= 4:
                    copy_pt(H_FOX + n - 1)
            head_out(H_FOX + 5, 5)
            copy_pt(H_FOX + 6)
            exps(H_FOX + 7)
            head_out(H_FOX + 6, 6)
            copy_pt(H_FOX + 7)
            head_out(H_FOX + 7, 7)
            feed("mo", 1, "f1")
            rms("f1")
            swiglu("up2")
            for j in range(3 * C):
                multiplied(PART["down2"] + j)
                hi(0, 0, PART["down2"] + j + HI_AHEAD)
                if j == 3 * C - 4:
                    A(touch, touch, ACT.Sqrt)
                if j % 3 == 2:
                    c = j // 3
                    act.wait_ge(evacuated, TILE["down2"] + c + 1)
                    if c == C - 1:
                        A(SQL, X[:, c, :], ACT.Square).then_inc(last_sq, 1)
                    A(HT[:, c, :], X[:, c, :], ACT.Copy, scale=col("final", c)).then_inc(fin_scaled, 1)
            rms("final")
            for c in range(0, C, 2):
                act.wait_ge(ht_ready, len([x for x in range(c + 2) if x % 4 != 3]))
                if c + 1 >= 3:
                    act.wait_ge(ht_pool, (c + 2) // 4)
                act.dma_start(out_d[:, c:c + 2, :], HT[:, c:c + 2, :]).then_inc(out_done, 16)
            act.wait_ge(out_done, 16 * (C // 2))

        @block.vector
        def _(dve):
            v = nc.vector
            chain = Chain(dve, dve_step)

            def lo(i, m, c):
                if isinstance(i, int) and c >= PARTS:
                    return
                slot = c % RING
                dve.wait_ge(hi_ready, lin(i, m, c + 1))
                v.tensor_tensor(w_lo[:, slot, :], raw[:, slot, :], w_hi[:, slot, :].bitcast(F32),
                                ALU.subtract).then_inc(lo_ready, 1)

            def multiplied(c, i=0, m=0):
                dve.wait_ge(part_done, lin(i, m, c + 1))

            def out_of(t):
                return bank[t % BANKS][:, 0:S]

            def step(name, j):
                lo(0, 0, PART[name] + j + LO_AHEAD)

            def columns(n):
                dve.wait_ge(col_mm, n)
                v.tensor_copy(RCOL, bank[4][:, S:S + 2]).then_inc(col_ready, 1)

            def rstd(norm, with_columns=False):
                dve.wait_ge(rms_ready, NORMS[norm] + 1)
                v.reciprocal(RSTD, RSTD).then_inc(rstd_ready, 1)
                if with_columns:
                    dve.wait_ge(col_rms, 1)
                    v.reciprocal(RCOL, RCOL).then_inc(col_ready, 1)
                dve.wait_ge(rstd_ready, NORMS[norm] + 1)

            def h_low(norm, c):
                dve.wait_ge(hh_ready, H_COUNT[norm] + c + 1)
                v.scalar_tensor_tensor(out=h_lo[:, c, :], in0=X[:, c, :], scalar=col(NEXT[norm], GAIN0[norm] + c),
                                       in1=h_hi[:, c, :].bitcast(F32), op0=ALU.mult,
                                       op1=ALU.subtract).then_inc(hl_ready, 1)

            def normed(dst, t):
                v.tensor_tensor(dst, out_of(t), RSTD, ALU.mult).then_inc(evacuated, 1)

            def add_normed(norm, gain, n0, after):
                rstd(norm)

                def scaled(c):
                    if c % 2 == 0:
                        dve.wait_ge(evacuated, TILE["wo" if norm == "post" else "down"] + c + 1)
                        v.tensor_tensor(M[:, c, :], M[:, c, :], RSTD, ALU.mult).then_inc(post_t, 1)
                scaled(0)
                for c in range(C):
                    if c + 1 < C:
                        scaled(c + 1)
                    if c % 2:
                        dve.wait_ge(post_pool, (n0 + c + 1) // 2)
                    else:
                        dve.wait_ge(post_t, (n0 + c) // 2 + 1)
                    v.scalar_tensor_tensor(out=X[:, c, :], in0=M[:, c, :], scalar=col(gain, c), in1=X[:, c, :],
                                           op0=ALU.mult, op1=ALU.add).then_inc(x_ready, 1)
                    if c >= 1:
                        h_low(after, c - 1)
                h_low(after, C - 1)

            v.memset(der[:, D_EPS - 1:D_EPS + 1], EPS).then_inc(der_ready, 1)
            v.memset(ones[:, :], 1.0).then_inc(ones_ready, 1)
            dve.wait_ge(par_in, 16)
            for c in range(C):
                h_low("mix", c)
                if c % 4 == 3:
                    lo(0, 0, c // 4)
            l0, l1 = (par[:, COLS["lb"] + C * r:COLS["lb"] + C * r + C] for r in range(2))
            chain.wait(v.tensor_tensor(der[:, D_LB:D_LB + C], l0, l1, ALU.max))
            for r, l in enumerate((l0, l1)):
                v.tensor_tensor(der[:, D_E + C * r:D_E + C * r + C], l, der[:, D_LB:D_LB + C],
                                ALU.subtract).then_inc(der_ready, 1)
            dve.wait_ge(wf_in, 16)
            v.tensor_copy(WF_HI, wf[:, :]).then_inc(wf_split, 1)
            dve.wait_ge(wf_split, 1)
            v.tensor_tensor(WF_LO, wf[:, :], WF_HI.bitcast(F32), ALU.subtract).then_inc(wf_split, 1)
            lo(0, 0, 2)
            step("xa", 0)
            rstd("mix")
            for p in range(R // 2):
                pair = (2 * p, 2 * p + 1)
                for t in pair:
                    multiplied(PART["xa"] + t)
                    normed(XA[:, t, :], TILE["xa"] + t)
                for t in pair:
                    if t >= 1:
                        step("xa", t)
                if p == 3:
                    columns(1)
                for j in (1, 2, 3):
                    for t in pair:
                        if j == 1:
                            dve.wait_ge(xc_tap, t + 1)
                        else:
                            dve.wait_ge(tap_step, 4 * p + 2 * (j - 2) + t % 2 + 1)
                        ins = v.scalar_tensor_tensor(out=XC[:, t, j:S], in0=XA[:, t, 0:S - j],
                                                     scalar=col("conv_w", (3 - j) * R + t), in1=XC[:, t, j:S],
                                                     op0=ALU.mult, op1=ALU.add)
                        ins.then_inc(taps_done if j == 3 else tap_step, 1)

            def parameters():
                lam = par[:, COLS["lam"]:COLS["lam"] + R]
                dve.wait_ge(sp_ln, 1)
                chain.wait(v.tensor_scalar(der[:, D_NSP:D_NSP + R], lam, -1.0, 0.0, ALU.mult, ALU.max))
                chain.wait(v.tensor_tensor(der[:, D_SP:D_SP + R], der[:, D_SP:D_SP + R], der[:, D_NSP:D_NSP + R],
                                           ALU.add))
                chain.wait(v.tensor_scalar(der[:, D_NSP:D_NSP + R], der[:, D_SP:D_SP + R], -LRU_C, None, ALU.mult))
                v.tensor_scalar(der[:, D_SP:D_SP + R], der[:, D_SP:D_SP + R], LRU_C, None,
                                ALU.mult).then_inc(der_ready, 1)
                dve.wait_ge(lb_exp, 2)
                e0, e1 = (der[:, D_E + C * r:D_E + C * r + C] for r in range(2))
                chain.wait(v.tensor_tensor(e1, e0, e1, ALU.add))
                chain.wait(v.reciprocal(e1, e1))
                chain.wait(v.tensor_tensor(der[:, D_LB:D_LB + C], e0, e1, ALU.mult))
                v.tensor_scalar(der[:, D_1LB:D_1LB + C], der[:, D_LB:D_LB + C], -1.0, 1.0, ALU.mult,
                                ALU.add).then_inc(der_ready, 1)

            def forget_sums():
                dve.wait_ge(f_ln, 1)
                z, az = att_s[0:H_FOX, 0, 0:S], att_s[0:H_FOX, 1, 0:S]
                chain.wait(v.tensor_scalar(z, z, 0.0, None, ALU.min))
                chain.wait(v.tensor_tensor(az, az, z, ALU.subtract))
                chain.wait(v.memset(z, 1.0))
                v.tensor_tensor_scan(ncum[:, :], z, az, 0.0, ALU.mult, ALU.add).then_inc(cum_ready, 1)

            for n in range(C):
                step("v", n)
                if n == 0:
                    dve.wait_ge(f_mm, 1)
                    v.tensor_tensor(att_s[0:H_FOX, 0, 0:S], bank[7][0:H_FOX, 0:S], RSTD[0:H_FOX, :],
                                    ALU.mult).then_inc(f_normed, 1)
            for n in range(8):
                step("gates", n)
                if n == 0:
                    forget_sums()
                if n == 4:
                    parameters()

            def lru_gain(t):
                dve.wait_ge(square_done, t + 1)
                v.scalar_tensor_tensor(out=XC[:, t, :], in0=ASQ[:, t % 2, :], scalar=1.0, in1=XC[:, t, :],
                                       op0=ALU.add, op1=ALU.mult).then_inc(gain_done, 1)

            def lru_scan(t):
                dve.wait_ge(b_done, t + 1)
                v.tensor_tensor_scan(XC[:, t, :], RG[:, t, :], IG[:, t, :], 0.0, ALU.mult,
                                     ALU.add).then_inc(scan_done, 1)

            def lru_lo(t):
                dve.wait_ge(yah, t + 1)
                v.tensor_tensor(u_lo[:, R + t, :], GA[:, t, :], u_hi[:, R + t, :].bitcast(F32),
                                ALU.subtract).then_inc(yal, 1)

            def maxima(n):
                b = n % 2
                dve.wait_ge(s_evac, 2 * n + 2)
                for j, (a, e) in enumerate([(0, P), (P, EXT)]):
                    v.tensor_reduce(stat_s[:, b, j:j + 1], att_s[:, b, a:e], AX.X, ALU.max).then_inc(mx_done, 1)
                dve.wait_ge(mx_done, 2 * n + 2)
                v.tensor_scalar(stat_s[:, b, 2:4], stat_s[:, b, 0:2], -1.0, None, ALU.mult).then_inc(negmax, 1)

            def probabilities(n):
                b = n % 2
                dve.wait_ge(exp_done, 2 * n + 2)
                v.reciprocal(stat_s[:, b, 6:8], stat_s[:, b, 4:6]).then_inc(rsum_done, 1)
                dve.wait_ge(rsum_done, n + 1)
                for j, (a, e) in enumerate([(0, P), (P, EXT)]):
                    v.tensor_scalar(att_s[:, b, a:e], att_s[:, b, a:e], stat_s[:, b, 6 + j:7 + j], None,
                                    ALU.mult).then_inc(p_ready, 1)

            def head_low(t, count):
                dve.wait_ge(y_hi, count)
                v.tensor_tensor(u_lo[:, t, :], bank[7][:, 0:S], u_hi[:, t, :].bitcast(F32),
                                ALU.subtract).then_inc(y_lo, 1)

            def fox_shift(n):
                b = n % 2
                dve.wait_ge(s_mm, n + 1)
                if n >= 2:
                    dve.wait_ge(pt_mm, n - 1)
                for j, (a, e) in enumerate([(0, P), (P, EXT)]):
                    v.scalar_tensor_tensor(out=att_s[:, b, a:e], in0=bank[4 + b][:, a:e], scalar=cum_t[:, j, n:n + 1],
                                           in1=mask[:, a:e], op0=ALU.add, op1=ALU.add).then_inc(s_evac, 1)

            dve.wait_ge(cst_in, 32)
            for t in range(R):
                step("ga", t)
                if t >= 1:
                    lru_gain(t - 1)
                if t == 4:
                    dve.wait_ge(cumt_mm, 1)
                    v.tensor_scalar(cum_t[:, :, :], bank[7][:, 0:2 * H_FOX].rearrange("p (b h) -> p b h", b=2), -1.0,
                                    None, ALU.mult).then_inc(cumt_ready, 1)
            dve.wait_ge(cumt_ready, 1)
            dve.wait_ge(evacuated, TILE["qk"])
            for s in range(4 * C):
                step("qk", s)
                if 0 <= s - 3 < H_FOX:
                    probabilities(s - 3)
                if 0 <= s - 6 < H_FOX and s % 2:
                    head_low((s - 6) // 2, (s - 6) // 2 + 1)
                for t in SCANS.get(s, []):
                    lru_scan(t)
                for t in SCANS.get(s - 3, []):
                    lru_lo(t)
                multiplied(PART["qk"] + s)
                t = s // 2 % C
                if s >= 2 * C:
                    normed((SGA if s < 3 * C else SGB)[:, s % C, :], TILE["qk"] + s)
                elif s % 2:
                    normed(K[:, t, :], TILE["qk"] + s)
                else:
                    v.scalar_tensor_tensor(out=Q[:, t, :], in0=out_of(TILE["qk"] + s), scalar=DH_FOX ** -0.5, in1=RSTD,
                                           op0=ALU.mult, op1=ALU.mult).then_inc(evacuated, 1)
                if s == 0:
                    lru_gain(R - 1)
                if 0 <= s - 2 < H_FOX:
                    fox_shift(s - 2)
                    maxima(s - 2)

            dve.wait_ge(sg_ready, 2 * C)
            for t in range(C):
                last = (R * t + R - 1) // BLK
                for n in range((R * t - 1) // BLK + 1 if t else 0, last + 1):
                    step("pa", n)
                multiplied(PART["pa"] + last)
                v.tensor_tensor(PRA[:, t, :], out_of(TILE["pa"] + t), SGA[:, t, :], ALU.mult).then_inc(evacuated, 1)

            def merged_low(t):
                dve.wait_ge(mh, t + 1)
                v.tensor_tensor(h_lo[:, t, :], PRA[:, t, :], h_hi[:, t, :].bitcast(F32), ALU.subtract).then_inc(ml, 1)

            for t in range(C):
                step("pb", t)
                if t >= 1:
                    merged_low(t - 1)
                multiplied(PART["pb"] + t)
                v.tensor_tensor(PRB[:, t, :], out_of(TILE["pb"] + t), SGB[:, t, :], ALU.mult).then_inc(evacuated, 1)
                dve.wait_ge(evacuated, TILE["pb"] + t + 1)
                v.tensor_tensor(PRA[:, t, :], PRA[:, t, :], PRB[:, t, :], ALU.add).then_inc(merged, 1)
            merged_low(C - 1)
            for t in range(C):
                step("wo", t)
            dve.wait_ge(x_back, 16)
            add_normed("post", "mix_post", 0, "ffn")

            def up_pair(i, p, first=False):
                pair = (2 * p, 2 * p + 1)
                for j in pair:
                    multiplied(PART["up"] + j, i, 4)
                    normed(UB[:, j, :], TILE["up"] + j)
                for j in pair:
                    if not (first and j == 0):
                        lo(i, 4, PART["up"] + j + LO_AHEAD)
                for j in pair:
                    dve.wait_ge(u_conv, lin(i, 4, j + 1))
                    v.scalar_tensor_tensor(out=YB[:, j, 1:S], in0=UB[:, j, 0:S - 1],
                                           scalar=dcol("fconv_w", lin(i, 4, 2 * F1 + j)), in1=YB[:, j, 1:S],
                                           op0=ALU.mult, op1=ALU.add).then_inc(tap_done, 1)
                for j in pair:
                    dve.wait_ge(tap_done, lin(i, 4, j + 1))
                    v.scalar_tensor_tensor(out=YB[:, j, 2:S], in0=UB[:, j, 0:S - 2],
                                           scalar=dcol("fconv_w", lin(i, 4, j)), in1=YB[:, j, 2:S],
                                           op0=ALU.mult, op1=ALU.add).then_inc(taps_done, 1)

            step("up", 0)
            rstd("ffn")
            up_pair(0, 0, first=True)
            up_pair(0, 1)
            with dve.Fori(1, 2 * F1 // 4) as i:
                up_pair(i, 0)
                up_pair(i, 1)
            for j in range(F1):
                step("down", j)
            add_normed("post2", "ffn_post", C, "n0")

            def gate_key(t):
                dve.wait_ge(f_raw, t + 1)
                v.tensor_scalar(FG[:, t, :], FG[:, t, :], der[:, D_1LB + t:D_1LB + t + 1],
                                der[:, D_LB + t:D_LB + t + 1], ALU.mult, ALU.add).then_inc(f_ready, 1)
                dve.wait_ge(f_ready, t + 1)
                v.tensor_scalar(KK[:, t, :], FG[:, t, :], -1.0, 1.0, ALU.mult, ALU.add).then_inc(k_ready, 1)

            step("hf", 0)
            rstd("n0")
            for t in range(C):
                multiplied(PART["hf"] + t)
                normed(FG[:, t, :], TILE["hf"] + t)
                if t >= 1:
                    step("hf", t)
                    gate_key(t - 1)
            for t in range(C):
                multiplied(PART["hq"] + t)
                normed(QS[:, t, :], TILE["hq"] + t)
                step("hq", t)
                if t == 0:
                    gate_key(C - 1)
                if t == 2:
                    dve.wait_ge(one_row, 1)
                    dve.wait_ge(logf_ready, 1)
                for c in {2: [0, 1], 3: [2], 4: [3], 5: [4, 5], 6: [6], 7: [7]}.get(t, []):
                    v.tensor_tensor_scan(CUM[:, c, :], ONES_ROW, CUM[:, c, :], 0.0, ALU.mult,
                                         ALU.add).then_inc(hcum_ready, 1)

            def halves(ap, l):
                w = flat(ap).rearrange("p (n b) -> p n b", b=2 ** l)
                return w[:, :, 0:2 ** (l - 1)], w[:, :, 2 ** (l - 1):]

            def level_args(l):
                low, _ = halves(CUM, l)
                elow, _ = halves(EB[l % 2], l)
                n, h = low.shape[1], low.shape[2]
                mid = low[:, :, h - 1:h].to_broadcast([P, n, h])
                if l >= 3:
                    dve.wait_ge(lev_mm, 4 + 2 * (l - 2))
                v.tensor_tensor(elow, mid, low, ALU.subtract).then_inc(arg_ready, 1)

            def level_keys(l):
                klow, _ = halves(KK, l)
                elow, _ = halves(EB[l % 2], l)
                dve.wait_ge(dec_ready, l)
                v.tensor_tensor(elow, elow, klow, ALU.mult).then_inc(x_low, 1)

            def take(l):
                if l == 0:
                    for g in range(4):
                        dve.wait_ge(lev_mm, g + 1)
                        v.copy_predicated(PD[:, 4 * g:4 * g + 4, :], LM[:, 0:1, :].to_broadcast([P, 4, P]),
                                          bank[4 + g][:, :].rearrange("p (n t) -> p n t", n=4)).then_inc(lev_sel, 1)
                    return
                b = 2 ** l
                for g in range(2):
                    dve.wait_ge(lev_sel, 4 if l == 1 else 4 + 2 * (l - 2) + g + 1)
                    dve.wait_ge(lev_mm, 4 + 2 * (l - 1) + g + 1)
                    dst = PD[:, 8 * g:8 * g + 8, :].rearrange("p z (n b) -> p z n b", b=b)[:, :, :, b // 2:]
                    pick = LM[:, l:l + 1, :].rearrange("p l (n b) -> p l n b", b=b)[:, :, :, b // 2:]
                    src = bank[4 + 2 * (l % 2) + g][:, :].rearrange("p (z n b) -> p z n b", z=8, b=b // 2)
                    v.copy_predicated(dst, pick.to_broadcast([P, 8, P // b, b // 2]), src).then_inc(lev_sel, 1)

            dve.wait_ge(hcum_ready, C)
            dve.wait_ge(lm_in, 16)
            dve.wait_ge(pd_zero, 1)
            level_args(1)
            columns(2)
            for l in range(1, LEVELS + 1):
                n = 2 * (l - 1)
                step("hi", n)
                if l < LEVELS:
                    level_args(l + 1)
                level_keys(l)
                take(l - 1)
                step("hi", n + 1)
                if n == C:
                    dve.wait_ge(evacuated, TILE["hg"])
                for t in (n - C, n - C + 1):
                    if t >= 0:
                        multiplied(PART["hg"] + t)
                        normed(OG[:, t, :], TILE["hg"] + t)
            for c in range(C + 1):
                if c < C:
                    dve.wait_ge(og_ready, 1 if c < C - 2 else 2)
                    dve.wait_ge(o_evac, c + 1)
                    v.scalar_tensor_tensor(out=OH[:, c, :], in0=OC[:, c, :], scalar=col("out_norm", c), in1=OG[:, c, :],
                                           op0=ALU.mult, op1=ALU.mult).then_inc(o_gated, 1)
                if c >= 1:
                    dve.wait_ge(oh_hi, c)
                    v.tensor_tensor(u_lo[:, c - 1, :], OH[:, c - 1, :], u_hi[:, c - 1, :].bitcast(F32),
                                    ALU.subtract).then_inc(oh_lo, 1)
            for t in range(3):
                step("ho", t)
            rstd("o")
            for t in range(C):
                if t == C - 1:
                    step("ho", t)
                multiplied(PART["ho"] + t)
                normed(M[:, t, :], TILE["ho"] + t)
                if 3 <= t < C - 1:
                    step("ho", t)
                dve.wait_ge(evacuated, TILE["ho"] + t + 1)
                v.tensor_tensor(X[:, t, :], X[:, t, :], M[:, t, :], ALU.add).then_inc(x_ready, 1)
                if t >= 1:
                    h_low("f0", t - 1)
            h_low("f0", C - 1)

            def add_branch(name, per, norm):
                for j in range(per * C):
                    step(name, j)
                    t = j // per
                    if j % per == 0 and t >= 1 and norm != "final":
                        h_low(norm, t - 1)
                    if j % per == per - 1:
                        multiplied(PART[name] + j)
                        v.tensor_tensor(X[:, t, :], X[:, t, :], out_of(TILE[name] + t), ALU.add).then_inc(evacuated, 1)
                if norm != "final":
                    h_low(norm, C - 1)

            def swiglu(name, norm, pairs0):
                step(name, 0)
                rstd(norm)

                def pair_tile(i, j, first=False):
                    multiplied(PART[name] + j, i, 4)
                    if j % 2 == 0:
                        dve.wait_ge(pair_free, lin(i, 2, pairs0 + j // 2 + 1))
                    normed(YB[:, j, :] if j % 2 else GR[:, j // 2, :], TILE[name] + j)
                    if not first:
                        lo(i, 4, PART[name] + j + LO_AHEAD)

                for j in range(4):
                    pair_tile(0, j, j == 0)
                with dve.Fori(1, 2 * F2 // 4) as i:
                    for j in range(4):
                        pair_tile(i, j)

            swiglu("up1", "f0", F1)
            add_branch("down1", 3, "n1")
            step("mv", 0)
            rstd("n1", with_columns=True)
            dve.wait_ge(bias_in, 32)
            v.tensor_tensor(BIAS, BIAS, mask[:, :].rearrange("p (o e) -> p o e", o=1).to_broadcast([P, H_MOBA, EXT]),
                            ALU.add).then_inc(bias_masked, 1)
            for n in range(1, C):
                step("mv", n)

            def moba_shift(h):
                n, b = H_FOX + h, h % 2
                dve.wait_ge(s_mm, n + 1)
                dve.wait_ge(pt_mm, n - 1)
                for j, (a, e) in enumerate([(0, P), (P, EXT)]):
                    v.scalar_tensor_tensor(out=att_s[:, b, a:e], in0=bank[4 + b][:, a:e], scalar=DH_MOBA ** -0.5,
                                           in1=BIAS[:, h, a:e], op0=ALU.mult, op1=ALU.add).then_inc(s_evac, 1)

            dve.wait_ge(bias_masked, 1)
            dve.wait_ge(evacuated, TILE["mqk"])
            for s in range(2 * C):
                step("mqk", s)
                h = (s - 2) // 2
                if s % 2 and s >= 3:
                    probabilities(H_FOX + (s - 3) // 2)
                if s % 2 == 0 and s >= 6:
                    head_low(h - 2, C + h - 1)
                multiplied(PART["mqk"] + s)
                normed((MK if s % 2 else MQ)[:, s // 2, :], TILE["mqk"] + s)
                if s % 2 == 0 and s >= 2:
                    moba_shift(h)
                    maxima(H_FOX + h)
            head_low(5, C + 6)
            moba_shift(7)
            maxima(H_FOX + 7)
            probabilities(H_FOX + 7)
            head_low(6, C + 7)
            head_low(7, C + 8)
            add_branch("mo", 1, "f1")
            swiglu("up2", "f1", F1 + F2)
            add_branch("down2", 3, "final")
            rstd("final")
            for c in range(C):
                if c % 4 != 3:
                    dve.wait_ge(fin_scaled, c + 1)
                    v.tensor_tensor(HT[:, c, :], HT[:, c, :], RSTD, ALU.mult).then_inc(ht_ready, 1)

        @block.gpsimd
        def _(pool):
            g = nc.gpsimd
            chain = Chain(pool, pool_step)

            def pair_sums(norm):
                for c in range(1, C, 2):
                    pool.wait_ge(sq_ready, C * PAIR_SUMS.index(norm) + c + 1)
                    g.tensor_tensor(SQ[:, c, :], SQ[:, c, :], SQ[:, c - 1, :], ALU.add).then_inc(pair_sum, 1)
                    if c == 3:
                        pool.wait_ge(pair_sum, 5 * PAIR_SUMS.index(norm) + 2)
                        g.tensor_tensor(SQ[:, 3, :], SQ[:, 3, :], SQ[:, 1, :], ALU.add).then_inc(pair_sum, 1)

            pool.dma_start(onehot, onehot_d).then_inc(tab_in, 16)
            pool.dma_start(table, table_d).then_inc(tab_in, 16)
            pool.dma_start(wf[:, :], wf_d).then_inc(wf_in, 16)
            pool.dma_start(ident[:, :], ident_d).then_inc(cst_in, 16)
            pool.dma_start(mask[:, :], mask_d).then_inc(cst_in, 16)
            g.memset(ONES_ROW, 1.0).then_inc(one_row, 1)
            pair_sums("mix")
            for t in range(R):
                pool.wait_ge(xch_ready, t + 1)
                g.tensor_tensor(u_lo[:, t, :], XC[:, t, :], u_hi[:, t, :].bitcast(F32),
                                ALU.subtract).then_inc(xcl_ready, 1)
            pool.wait_ge(ext_ready, 1)
            pool.dma_start(bass.AP(tensor=scr, offset=0, ap=[[P * EXT, H_MOBA], [EXT, P], [1, EXT]]),
                           ext.rearrange("h (o e) -> h o e", o=1).to_broadcast([H_MOBA, P, EXT])).then_inc(ext_out, 16)
            pool.wait_ge(cst_in, 32)
            g.tensor_copy(EYE_R, ident[0:H_FOX, 0:H_FOX]).then_inc(cum_split, 1)
            pool.wait_ge(cum_ready, 1)
            g.tensor_copy(CUM_HI, ncum[:, :]).then_inc(cum_split, 1)
            pool.wait_ge(cum_split, 2)
            g.tensor_tensor(CUM_LO, ncum[:, :], CUM_HI.bitcast(F32), ALU.subtract).then_inc(cum_split, 1)
            for t in range(R):
                pool.wait_ge(gates_evac, t + 1)
                pool.wait_ge(xcl_ready, R)
                g.tensor_tensor(IG[:, t, :], IG[:, t, :], XC[:, t, :], ALU.mult).then_inc(ix_done, 1)
            for t in range(R):
                pool.wait_ge(decay_done, t + 1)
                if t >= 2:
                    pool.wait_ge(gain_done, t - 1)
                g.tensor_tensor(ASQ[:, t % 2, :], RG[:, t, :], RG[:, t, :], ALU.mult).then_inc(square_done, 1)
                pool.wait_ge(evacuated, TILE["ga"] + t + 1)
                g.tensor_tensor(GA[:, t, :], GA[:, t, :], RSTD, ALU.mult).then_inc(ga_normed, 1)
            pool.wait_ge(root_done, 1)
            for t in range(R + 2):
                if t < R:
                    g.tensor_tensor(IG[:, t, :], IG[:, t, :], XC[:, t, :], ALU.mult).then_inc(b_done, 1)
                if t >= 2:
                    pool.wait_ge(scan_done, t - 1)
                    pool.wait_ge(gelu_done, 1)
                    g.tensor_tensor(GA[:, t - 2, :], GA[:, t - 2, :], XC[:, t - 2, :], ALU.mult).then_inc(ya_done, 1)
            pool.wait_ge(merged, C)
            pool.dma_start(X, x_d).then_inc(x_back, 16)
            pool.dma_start(LM, lmask_d).then_inc(lm_in, 16)
            pool.wait_ge(ml, C)
            g.memset(PD, 0.0).then_inc(pd_zero, 1)
            for pair in range(2):
                g.memset(PB[:, pair, 0:1], 0.0).then_inc(pair_free, 1)

            def squares(norm, src, count, n0):
                N = C - 1 if norm in LAST_BY_ACT else C
                for c in range(N):
                    pool.wait_ge(count, n0 + c + 1)
                    if c == 0:
                        chain.wait(g.tensor_tensor(ACC, src[:, c, :], src[:, c, :], ALU.mult))
                    else:
                        chain.wait(g.tensor_tensor(SQT, src[:, c, :], src[:, c, :], ALU.mult))
                        ins = g.tensor_tensor(ACC, ACC, SQT, ALU.add)
                        if c < N - 1:
                            chain.wait(ins)
                        else:
                            ins.then_inc(acc_ready, 1)

            def half_scaled(norm):
                pool.wait_ge(rstd_ready, NORMS[norm] + 1)
                for c in range(1, C, 2):
                    g.tensor_tensor(M[:, c, :], M[:, c, :], RSTD, ALU.mult).then_inc(post_pool, 1)

            def products(i, pair, pairs0, tiles_ready, t0):
                pool.wait_ge(gate_ready, lin(i, 2, pairs0 + pair + 1))
                pool.wait_ge(tiles_ready, lin(i, 4, t0 + 2 * pair + 2))
                g.tensor_tensor(PB[:, pair, :], GB[:, pair, :], YB[:, 2 * pair + 1, :], ALU.mult).then_inc(pair_free, 1)
                pool.wait_ge(pair_free, lin(i, 2, 2 + pairs0 + pair + 1))
                dst_h, dst_l = u_hi[:, bass.ds(i * 2 + pair, 1), :], u_lo[:, bass.ds(i * 2 + pair, 1), :]
                g.tensor_copy(dst_h, PB[:, pair:pair + 1, :]).then_inc(uh_ready, 1)
                pool.wait_ge(uh_ready, lin(i, 2, pairs0 + pair + 1))
                g.tensor_tensor(dst_l, PB[:, pair:pair + 1, :], dst_h.bitcast(F32), ALU.subtract).then_inc(ul_ready, 1)

            def swiglu(name, pairs0):
                with pool.Fori(0, F2 // 2) as i:
                    for pair in range(2):
                        products(i, pair, pairs0, evacuated, TILE[name])

            squares("post", M, evacuated, TILE["wo"])
            half_scaled("post")
            pair_sums("ffn")
            with pool.Fori(0, F1 // 2) as i:
                for pair in range(2):
                    products(i, pair, 0, taps_done, R)
            squares("post2", M, evacuated, TILE["down"])
            half_scaled("post2")
            pair_sums("n0")

            def halves(ap, l):
                w = flat(ap).rearrange("p (n b) -> p n b", b=2 ** l)
                return w[:, :, 0:2 ** (l - 1)], w[:, :, 2 ** (l - 1):]

            def level_args(l):
                low, up = halves(CUM, l)
                n, h = low.shape[1], low.shape[2]
                if l >= 3:
                    pool.wait_ge(lev_mm, 4 + 2 * (l - 2))
                g.tensor_tensor(halves(EB[l % 2], l)[1], up, low[:, :, h - 1:h].to_broadcast([P, n, h]),
                                ALU.subtract).then_inc(arg_up, 1)

            pool.wait_ge(hcum_ready, C)
            level_args(1)
            for l in range(1, LEVELS + 1):
                if l < LEVELS:
                    level_args(l + 1)
                w, q = halves(EB[l % 2], l)[1], halves(QS, l)[1]
                pool.wait_ge(dec_ready, l)
                g.tensor_tensor(w, w, q, ALU.mult).then_inc(x_up, 1)
            squares("o", OC, o_evac, 0)
            squares("f0", X, *X_SRC["f0"])
            swiglu("up1", F1)
            pool.wait_ge(ext_out, 16)
            for j, (a, e) in enumerate([(0, P), (P, EXT)]):
                pool.dma_start(BIAS[:, :, a:e], bass.AP(tensor=scr, offset=255 - P * j,
                               ap=[[EXT - 1, P], [P * EXT, H_MOBA], [1, e - a]])).then_inc(bias_in, 16)
            squares("n1", X, *X_SRC["n1"])
            squares("f1", X, *X_SRC["f1"])
            swiglu("up2", F1 + F2)
            squares("final", X, *X_SRC["final"])
            pool.wait_ge(rstd_ready, NORMS["final"] + 1)
            pool.wait_ge(fin_scaled, C)
            for c in range(3, C, 4):
                g.tensor_tensor(HT[:, c, :], HT[:, c, :], RSTD, ALU.mult).then_inc(ht_pool, 1)

        @block.tensor
        def _(pe):
            mm = nc.tensor.matmul

            def three(out, slot, b, r_hi, r_lo, start, stop):
                s = slice(b * P, (b + 1) * P)
                mm(out, w_hi[:, slot, s], r_hi, start=start, stop=False)
                mm(out, w_hi[:, slot, s], r_lo, start=False, stop=False)
                return mm(out, w_lo[:, slot, s], r_hi, start=False, stop=stop)

            def free_bank(i, m, t):
                if t >= BANKS or not isinstance(i, int):
                    pe.wait_ge(evacuated, lin(i, m, t - BANKS + 1))

            def tile(i, c, t, x_hi=h_hi, x_lo=h_lo, low=None, n0=0, blocks=range(BLK)):
                if blocks[0] == 0:
                    pe.wait_ge(lo_ready, lin(i, 4, c + 1))
                    free_bank(i, 4, t)
                for b in blocks:
                    if low is not None:
                        pe.wait_ge(low, n0 + b + 1)
                    last = three(bank[t % BANKS][:, 0:S], c % RING, b, x_hi[:, b, :], x_lo[:, b, :], b == 0,
                                 b == BLK - 1)
                if blocks[-1] == BLK - 1:
                    last.then_inc(part_done, 1)

            def tiles(c, t, n, x_hi=h_hi, x_lo=h_lo):
                with pe.Fori(0, n // 4) as i:
                    for j in range(4):
                        tile(i, c + j, t + j, x_hi, x_lo)

            def stat(norm, columns=False):
                pe.wait_ge(acc_ready, POOL_SUMS.index(norm) + 1)
                last = mm(bank[4][:, 0:S], ones[:, :], ACC, start=True, stop=norm not in LAST_BY_ACT)
                if norm in LAST_BY_ACT:
                    pe.wait_ge(last_sq, LAST_BY_ACT.index(norm) + 1)
                    last = mm(bank[4][:, 0:S], ones[:, :], SQL, start=False, stop=True)
                if columns:
                    for tok in range(2):
                        last = mm(bank[4][:, S + tok:S + tok + 1], ACC[:, tok * P:(tok + 1) * P], ones[:, 0:1],
                                  start=True, stop=True)
                last.then_inc(stat_done, 1)

            def keep_clock(n):
                for _ in range(n):
                    mm(bank[5][:, S:S + P], ones[:, :], ones[:, :], start=True, stop=True)

            def pair_stat(norm):
                for n, b in ((3, 3), (4, 5), (5, 7)):
                    pe.wait_ge(pair_sum, 5 * PAIR_SUMS.index(norm) + n)
                    last = mm(bank[4][:, 0:S], ones[:, :], SQ[:, b, :], start=(b == 3), stop=(b == C - 1))
                last.then_inc(stat_done, 1)

            def columns(norm):
                pe.wait_ge(rstd_ready, NORMS[norm] + 1)
                for tok in range(2):
                    last = mm(bank[4][:, S + tok:S + tok + 1], RSTD[0:1, tok * P:(tok + 1) * P], ones[0:1, 0:1],
                              start=True, stop=True)
                last.then_inc(col_mm, 1)

            def after_norm(norm, name, n):
                c, t = PART[name], TILE[name]
                pe.wait_ge(lo_ready, c + 2)
                free_bank(0, 0, t + 1)
                for b in range(BLK):
                    pe.wait_ge(hl_ready, H_COUNT[norm] + b + 1)
                    for j in range(2):
                        last = three(bank[(t + j) % BANKS][:, 0:S], (c + j) % RING, b, h_hi[:, b, :], h_lo[:, b, :],
                                     b == 0, b == BLK - 1)
                        if b == BLK - 1:
                            last.then_inc(part_done, 1)
                if norm in ("ffn", "n0"):
                    pair_stat(norm)
                else:
                    stat(norm)
                for j in (2, 3):
                    tile(0, c + j, t + j)
                tiles(c + 4, t + 4, n - 4)

            def token_tile(c, t, n, tok, low=None, n0=0):
                s0 = (c + n) % RING
                if tok == 0:
                    pe.wait_ge(lo_ready, c + n + 2)
                free_bank(0, 0, t + n + tok)
                out = bank[(t + n + tok) % BANKS][:, 0:S].rearrange("p (z f) -> p z f", z=2)
                ts = slice(tok * P, (tok + 1) * P)
                for b in range(BLK):
                    if low is not None:
                        pe.wait_ge(low, n0 + b + 1)
                    f = slice(b * P, (b + 1) * P)
                    mm(out, h_hi[:, b, ts], w_hi[:, s0:s0 + 2, f], start=(b == 0), stop=False)
                    mm(out, h_lo[:, b, ts], w_hi[:, s0:s0 + 2, f], start=False, stop=False)
                    last = mm(out, h_hi[:, b, ts], w_lo[:, s0:s0 + 2, f], start=False, stop=(b == BLK - 1))
                if tok == 1:
                    last.then_inc(part_done, 2)

            def down(name, KT, n0):
                for j in range(24):
                    c, t = PART[name] + j, TILE[name] + j // 3
                    pe.wait_ge(lo_ready, c + 1)
                    if j % 3 == 0:
                        free_bank(0, 0, t)
                    for b in range(min(BLK, KT - BLK * (j % 3))):
                        k = BLK * (j % 3) + b
                        if j < 3:
                            pe.wait_ge(ul_ready, n0 + k + 1)
                        last = three(bank[t % BANKS][:, 0:S], c % RING, b, u_hi[:, k, :], u_lo[:, k, :],
                                     k == 0, k == KT - 1)
                    last.then_inc(part_done, 1)

            pe.wait_ge(ones_ready, 1)
            keep_clock(24)
            tile(0, 0, 0, low=hl_ready)
            tile(0, 1, 1)
            pair_stat("mix")
            pe.wait_ge(tab_in, 32)
            mm(bank[5][0:H_MOBA, 0:EXT], table, onehot, start=True, stop=True).then_inc(ext_mm, 1)
            for t in range(2, R):
                if t == 6:
                    columns("mix")
                tile(0, PART["xa"] + t, TILE["xa"] + t)
            pe.wait_ge(wf_split, 2)
            for c in range(C):
                ws, out = slice(c * H_FOX, (c + 1) * H_FOX), bank[7][0:H_FOX, 0:S]
                mm(out, WF_HI[:, ws], h_hi[:, c, :], start=(c == 0), stop=False)
                mm(out, WF_HI[:, ws], h_lo[:, c, :], start=False, stop=False)
                last = mm(out, WF_LO[:, ws], h_hi[:, c, :], start=False, stop=(c == C - 1))
            last.then_inc(f_mm, 1)
            for n in range(0, C, 2):
                for tok in range(2):
                    token_tile(PART["v"], TILE["v"], n, tok)
            pe.wait_ge(xcl_ready, R)
            pe.wait_ge(ext_ready, 1)
            for n in range(8):
                c, g = PART["gates"] + n, n // 2 % 2
                pe.wait_ge(lo_ready, c + 1)
                if n >= 2:
                    pe.wait_ge(gates_evac, 5 * (n // 2) - (2 if n % 2 == 0 else 0))
                b = 0
                for j, o in enumerate(GATE_PARTS[n % 2]):
                    out = bank[4 + 2 * (n % 2) + j // 2][:, j % 2 * S:j % 2 * S + S]
                    for k, f in enumerate(GATE_IN[o]):
                        last = three(out, c % RING, b, u_hi[:, 5 * g + f, :], u_lo[:, 5 * g + f, :], k == 0,
                                     k == len(GATE_IN[o]) - 1)
                        b += 1
                last.then_inc(part_done, 1)
            pe.wait_ge(cst_in, 32)
            pe.wait_ge(cum_ready, 1)
            for b in range(2):
                last = nc.tensor.transpose(bank[7][:, b * H_FOX:(b + 1) * H_FOX], ncum[:, b * P:(b + 1) * P],
                                           ident[0:H_FOX, 0:H_FOX])
            last.then_inc(cumt_mm, 1)
            tiles(PART["ga"], TILE["ga"], 8)
            for t in range(8, R):
                tile(0, PART["ga"] + t, TILE["ga"] + t)

            def transposes(n):
                b = n % 2
                pe.wait_ge(p_ready, 2 * n + 2)
                if n >= 1:
                    pe.wait_ge(pt_copied, n)
                for j in range(3):
                    ks = slice(j * P, (j + 1) * P)
                    last = nc.tensor.transpose(bank[6][:, ks], att_s[:, b, ks], ident[:, :])
                last.then_inc(pt_mm, 1)

            def fox_scores(h):
                t, o, out = h // 2, h % 2 * DH_FOX, bank[4 + h % 2]
                pe.wait_ge(evacuated, TILE["qk"] + 2 * t + 2)
                if h >= 2:
                    pe.wait_ge(s_evac, 2 * h - 2)
                sel = EYE_R[:, h:h + 1].to_broadcast([H_FOX, P])
                for a, e, qb in ((0, P, 0), (P, EXT, 1)):
                    mm(out[:, a:e], Q[o:o + DH_FOX, t, qb * P:(qb + 1) * P], K[o:o + DH_FOX, t, 0:e - a],
                       start=True, stop=False)
                    mm(out[:, a:e], sel, CUM_HI[:, 0:e - a], start=False, stop=False)
                    last = mm(out[:, a:e], sel, CUM_LO[:, 0:e - a], start=False, stop=True)
                last.then_inc(s_mm, 1)

            def values(n, out, vt):
                pe.wait_ge(pt_copied, n + 1)
                pt = att_pt[:, n % 2, :]
                mm(out[:, 0:P], vt(0), pt[:, 0:P], start=True, stop=True)
                mm(out[:, P:S], vt(0), pt[:, P:2 * P], start=True, stop=False)
                mm(out[:, P:S], vt(1), pt[:, 2 * P:EXT], start=False, stop=True).then_inc(pv_mm, 1)

            def fox_values(h):
                if h >= 2 and h % 2 == 0:
                    pe.wait_ge(y_lo, h // 2)
                o = h % 2 * DH_FOX
                values(h, bank[7][o:o + DH_FOX, 0:S],
                       lambda kb: flat(V[:, 4 * kb:4 * kb + 4, :])[:, h * DH_FOX:(h + 1) * DH_FOX])

            pe.wait_ge(gates_evac, 2 * R)
            pe.wait_ge(cumt_ready, 1)
            pe.wait_ge(cum_split, 3)
            for s in range(3 * C):
                tile(0, PART["qk"] + s, TILE["qk"] + s)
                if 0 <= s - 4 < H_FOX:
                    transposes(s - 4)
                if 0 <= s - 2 < H_FOX:
                    fox_scores(s - 2)
                if 0 <= s - 5 < H_FOX:
                    fox_values(s - 5)
            tiles(PART["sb"], TILE["sb"], C)
            for t in range(C):
                for k in range(R):
                    n, b = divmod(R * t + k, BLK)
                    if b == 0:
                        pe.wait_ge(lo_ready, PART["pa"] + n + 1)
                    if t == 0:
                        pe.wait_ge(yal, k + 1)
                    if k == 0:
                        free_bank(0, 0, TILE["pa"] + t)
                    last = three(bank[(TILE["pa"] + t) % BANKS][:, 0:S], (PART["pa"] + n) % RING, b, u_hi[:, R + k, :],
                                 u_lo[:, R + k, :], k == 0, k == R - 1)
                    if b == BLK - 1:
                        last.then_inc(part_done, 1)
            pe.wait_ge(y_lo, C)
            tiles(PART["pb"], TILE["pb"], C, u_hi, u_lo)
            tile(0, PART["wo"], TILE["wo"], low=ml)
            for t in range(1, C):
                tile(0, PART["wo"] + t, TILE["wo"] + t)
            stat("post")
            keep_clock(20)
            after_norm("ffn", "up", 2 * F1)
            down("down", F1, 0)
            stat("post2")
            keep_clock(20)
            after_norm("n0", "hf", 2 * C)
            columns("n0")

            def level_mm(l):
                for g in range(2):
                    if l <= 2:
                        pe.wait_ge(lev_sel, 3 + g if l == 1 else 4)
                    else:
                        pe.wait_ge(lev_sel, 4 + 2 * (l - 3) + g + 1)
                    for j in range(8):
                        c, tok = (8 * g + j) // 2, slice(j % 2 * P, (j % 2 + 1) * P)
                        out = bank[4 + 2 * (l % 2) + g][:, j * P // 2:(j + 1) * P // 2]
                        later = EB[l % 2][:, c, tok].rearrange("p (n b) -> p n b", b=2 ** l)[:, :, 2 ** (l - 1):]
                        last = mm(out.rearrange("p (n b) -> p n b", b=2 ** (l - 1)), EB[l % 2][:, c, tok], later,
                                  start=True, stop=True)
                    last.then_inc(lev_mm, 1)

            def diagonal_mm():
                for g in range(4):
                    for j in range(4):
                        c, tok = (4 * g + j) // 2, slice(j % 2 * P, (j % 2 + 1) * P)
                        last = mm(bank[4 + g][:, j * P:(j + 1) * P], KK[:, c, tok], QS[:, c, tok], start=True,
                                  stop=True)
                    last.then_inc(lev_mm, 1)

            def across_mm():
                for g in range(2):
                    pe.wait_ge(lev_sel, 4 + 2 * (LEVELS - 3) + g + 1)
                    for j in range(4):
                        c = 4 * g + j
                        last = mm(bank[4 + g][:, j * P:(j + 1) * P], EB[0][:, c, 0:P], EB[0][:, c, P:S], start=True,
                                  stop=True)
                    last.then_inc(lev_mm, 1)

            for l in range(1, LEVELS + 1):
                n = 2 * (l - 1)
                if n < C:
                    token_tile(PART["hi"], TILE["hi"], n, 0)
                    if l == 1:
                        pe.wait_ge(k_ready, C)
                        pe.wait_ge(q_ready, C)
                        pe.wait_ge(col_ready, 2)
                        diagonal_mm()
                    token_tile(PART["hi"], TILE["hi"], n, 1)
                else:
                    for t in (n - C, n - C + 1)[:2 if l < LEVELS else 1]:
                        tile(0, PART["hg"] + t, TILE["hg"] + t)
                pe.wait_ge(x_low, l)
                pe.wait_ge(x_up, l)
                if l < LEVELS:
                    level_mm(l)
                else:
                    across_mm()
            tile(0, PART["hg"] + C - 1, TILE["hg"] + C - 1)
            pe.wait_ge(lev_sel, 4 + 2 * (LEVELS - 1))
            pe.wait_ge(px_copied, 2)
            for c in range(C):
                out = bank[5 + c % 3]
                if c >= 3:
                    pe.wait_ge(o_evac, c - 2)

                def it(tok):
                    return flat(INP[:, 4 * tok:4 * tok + 4, :])[:, c * P:(c + 1) * P]
                mm(out[:, 0:P], it(0), PD[:, 2 * c, :], start=True, stop=True)
                mm(out[:, P:S], it(0), PX[:, c, :], start=True, stop=False)
                mm(out[:, P:S], it(1), PD[:, 2 * c + 1, :], start=False, stop=True).then_inc(o_mm, 1)
            tile(0, PART["ho"], TILE["ho"], u_hi, u_lo, low=oh_lo)
            for t in (1, 2):
                tile(0, PART["ho"] + t, TILE["ho"] + t, u_hi, u_lo)
            stat("o")
            for t in range(3, C):
                tile(0, PART["ho"] + t, TILE["ho"] + t, u_hi, u_lo)
            after_norm("f0", "up1", 2 * F2)
            down("down1", F2, F1)
            for n in range(0, C, 2):
                for tok in range(2):
                    token_tile(PART["mv"], TILE["mv"], n, tok, hl_ready if n + tok == 0 else None, H_COUNT["n1"])
                    if n + tok == 0:
                        stat("n1", columns=True)

            def moba_scores(h):
                out = bank[4 + h % 2]
                pe.wait_ge(evacuated, TILE["mqk"] + 2 * h + 2)
                pe.wait_ge(s_evac, 2 * (H_FOX + h) - 2)
                mm(out[:, 0:P], MQ[:, h, 0:P], MK[:, h, 0:P], start=True, stop=True)
                mm(out[:, P:EXT], MQ[:, h, P:S], MK[:, h, :], start=True, stop=True).then_inc(s_mm, 1)

            def moba_values(h):
                pe.wait_ge(y_lo, C + h)
                values(H_FOX + h, bank[7][:, 0:S], lambda kb: flat(MV[:, 4 * kb:4 * kb + 4, :])[:, h * P:(h + 1) * P])

            for s in range(2 * C):
                tile(0, PART["mqk"] + s, TILE["mqk"] + s)
                if s % 2 == 0 and s >= 4:
                    transposes(H_FOX + (s - 4) // 2)
                if s % 2 == 0 and s >= 2:
                    moba_scores((s - 2) // 2)
                if s % 2 and s >= 5:
                    moba_values((s - 5) // 2)
            transposes(H_FOX + 6)
            moba_scores(7)
            moba_values(6)
            def first(t, blocks):
                tile(0, PART["mo"] + t, TILE["mo"] + t, u_hi, u_lo, y_lo, C, blocks)

            first(0, range(0, 6))
            first(1, range(0, 3))
            transposes(H_FOX + 7)
            first(1, range(3, 6))
            moba_values(7)
            first(0, range(6, 7))
            first(1, range(6, 7))
            first(2, range(0, 4))
            for t in range(3):
                first(t, range(7 if t < 2 else 4, BLK))
            for t in range(3, C):
                tile(0, PART["mo"] + t, TILE["mo"] + t, u_hi, u_lo)
            after_norm("f1", "up2", 2 * F2)
            down("down2", F2, F1 + F2)
            stat("final")


def bucket_of(dist):
    import math
    import numpy as np
    exact = BUCKETS // 2
    n = np.maximum(dist, 0)
    nf = np.maximum(n, exact).astype(np.float32)
    large = exact + (np.log(nf / np.float32(exact)) / np.float32(math.log(1024 / exact))
                     * np.float32(BUCKETS - exact)).astype(np.int32)
    return np.where(n < exact, n, np.minimum(large, BUCKETS - 1))


def kernel(**inputs):
    import numpy as np
    import concourse.bacc as bacc
    from concourse.bass_utils import run_bass_kernel_spmd

    a = {k: np.asarray(x) for k, x in inputs.items()}

    def parts_of(w):
        k, n = w.shape
        per = -(-k // (BLK * P))
        out = np.zeros((n // P, per, P, BLK, P), np.float32)
        for j in range(per):
            rows = w[j * BLK * P:(j + 1) * BLK * P]
            kb = rows.shape[0] // P
            out[:, j, :, :kb, :] = rows.reshape(kb, P, n // P, P).transpose(2, 1, 0, 3)
        return out.reshape(-1, P, BLK * P)

    def packed(w):
        k, n = w.shape
        b = w.reshape(k // P, P, n // P, P).transpose(2, 0, 1, 3).reshape(-1, BLK, P, P)
        return b.transpose(0, 2, 1, 3).reshape(-1, P, BLK * P)

    def gate_parts(w):
        out = np.zeros((2, 2, P, BLK, P), np.float32)
        for g in range(2):
            dense = np.zeros((5 * P, 5 * P), np.float32)
            for h in range(8):
                s = slice(h * RNN_BLOCK, (h + 1) * RNN_BLOCK)
                dense[s, s] = w[8 * g + h]
            for n, tiles in enumerate(GATE_PARTS):
                blocks = [(f, o) for o in tiles for f in GATE_IN[o]]
                for b, (f, o) in enumerate(blocks):
                    out[g, n, :, b, :] = dense[f * P:(f + 1) * P, o * P:(o + 1) * P]
        return out.reshape(4, P, BLK * P)

    def paired(w):
        k, n = w.shape
        return w.reshape(k, 2, n // (2 * P), P).transpose(0, 2, 1, 3).reshape(k, n)

    w_in = a["w_in"][0]
    o = np.cumsum([0, D_RNN, D_RNN, D, D, D, H_FOX, D, D])
    xa, ga, q, k, v, f, sa, sb_ = (w_in[:, o[i]:o[i + 1]] for i in range(8))
    hq, hf, hi_, hg = (a["hgrn_w_in_2"][0][:, i * D:(i + 1) * D] for i in range(4))
    mq, mk, mv = (a["moba_w_in_2"][0][:, i * D:(i + 1) * D] for i in range(3))
    stream = np.concatenate([
        parts_of(xa), parts_of(v), gate_parts(a["w_rg_x"][0]), gate_parts(a["w_rg_a"][0]), parts_of(ga),
        parts_of(paired(np.concatenate([q, k], axis=1))), parts_of(sa), parts_of(sb_),
        packed(a["w_proj_a"][0]), parts_of(a["w_proj_b"][0]),
        parts_of(a["w_out"][0]), parts_of(paired(a["w_up"][0])), parts_of(a["w_down"][0]),
        parts_of(hf), parts_of(hq), parts_of(hi_), parts_of(hg), parts_of(a["hgrn_w_out_2"][0]),
        parts_of(paired(a["ffn_w13_2"][0])), parts_of(a["ffn_w2_2"][0]),
        parts_of(mv), parts_of(paired(np.concatenate([mq, mk], axis=1))), parts_of(a["moba_w_out_2"][0]),
        parts_of(paired(a["ffn_w13_2"][1])), parts_of(a["ffn_w2_2"][1])])
    assert stream.shape[0] == PARTS

    def cols(x):
        return x.reshape(-1, P).T

    pad = np.zeros(P, np.float32)
    pad[:H_FOX] = a["b_forget"][0]
    par = np.concatenate([
        cols(a["mix_norm_pre"][0]), cols(a["mix_norm_post"][0]), cols(a["conv_a_w"][0]), cols(a["conv_a_b"][0]),
        cols(a["b_rg_a"][0]), cols(a["b_rg_x"][0]), cols(a["lru_lambda"][0]), cols(a["b_merge"][0]),
        cols(a["ffn_norm_pre"][0]), cols(a["ffn_norm_post"][0]), cols(paired(a["conv_f_w"][0])),
        cols(paired(a["conv_f_b"])), cols(a["norm_mix_2"]), cols(a["norm_ffn_2"]), cols(a["hgrn_lb_logits_2"]),
        cols(a["hgrn_out_norm_2"][0]), cols(a["final_norm_2"]), pad[:, None]], axis=1)
    par = np.ascontiguousarray(par)
    assert par.shape == (P, NCOL)

    x_t = np.ascontiguousarray(a["x"][0].T.reshape(C, P, S).transpose(1, 0, 2))
    wf = np.ascontiguousarray(f.reshape(C, P, H_FOX).transpose(1, 0, 2).reshape(P, C * H_FOX))

    onehot = (np.arange(BUCKETS)[:, None] == bucket_of(255 - np.arange(EXT))[None, :]).astype(np.float32)
    ident = np.eye(P, dtype=np.float32)
    causal = np.where(np.arange(P)[None, :] <= np.arange(P)[:, None], 0.0, NEG).astype(np.float32)
    mask = np.concatenate([causal, np.zeros((P, P), np.float32), causal], axis=1)
    s, t = np.arange(P)[:, None], np.arange(P)[None, :]
    lmask = np.stack([s == t] + [(s >> l == t >> l) & (s >> (l - 1) != t >> (l - 1)) & (s < t)
                                 for l in range(1, LEVELS)], axis=1).astype(np.int32)

    arrays = {"stream": stream, "par": par, "x_t": x_t, "wf": wf,
              "table": np.ascontiguousarray(a["rel_bias_table_2"]), "onehot": onehot, "ident": ident,
              "mask": mask, "lmask": np.ascontiguousarray(lmask)}
    nc = bacc.Bacc("TRN2", target_bir_lowering=False, num_devices=1)
    aps = [nc.dram_tensor("in_" + n, x.shape, mybir.dt.from_np(x.dtype), kind="ExternalInput").ap()
           for n, x in arrays.items()]
    out = nc.dram_tensor("out", (P, C, S), F32, kind="ExternalOutput").ap()
    build(nc, *aps, out)
    r = run_bass_kernel_spmd(nc, [{"in_" + n: x for n, x in arrays.items()}], core_ids=[0])
    y = r.results[0]["out"]
    return np.ascontiguousarray(y.transpose(2, 1, 0).reshape(1, S, D))
```
